# Optimizing a Trainium2 kernel written in Bass

```python
import math
import jax, jax.numpy as jnp
from jax import lax
import numpy as np

D_MODEL = 1024
BATCH = 1
SEQ = 1024
DEPTH = 1

MEM_LEN = 256
BRANCH_WIDTH = 512
N_BRANCHES = 5
GDN_HEADS = 4
GDN_HEAD_DIM = 128
GDN_CONV = 4
GDN_CHUNK = 64
CONF_WIDTH = 31
SWA_Q_HEADS = 8
SWA_KV_HEADS = 2
SWA_HEAD_DIM = 64
WINDOW = 128
REL_BUCKETS = 32
REL_MAX_DIST = 128
LRU_BLOCKS = 8
LRU_BLOCK_W = BRANCH_WIDTH // LRU_BLOCKS
LRU_CONV = 4
LRU_C = 8.0
XATTN_HEADS = 4
XATTN_HEAD_DIM = BRANCH_WIDTH // XATTN_HEADS
NORM_EPS = 1e-6

SPLIT_SIZES = (3 * BRANCH_WIDTH, BRANCH_WIDTH, GDN_HEADS, GDN_HEADS,
               2 * BRANCH_WIDTH, BRANCH_WIDTH,
               SWA_Q_HEADS * SWA_HEAD_DIM, 2 * SWA_KV_HEADS * SWA_HEAD_DIM, BRANCH_WIDTH,
               BRANCH_WIDTH, BRANCH_WIDTH,
               XATTN_HEADS * XATTN_HEAD_DIM, BRANCH_WIDTH,
               N_BRANCHES * D_MODEL)
IN_COLS = sum(SPLIT_SIZES)


def _rms_norm(x, g):
    xf = x.astype(jnp.float32)
    y = xf * lax.rsqrt(jnp.mean(xf * xf, axis=-1, keepdims=True) + NORM_EPS)
    return (y * g.astype(jnp.float32)).astype(x.dtype)

def _layer_norm(x, g, b):
    xf = x.astype(jnp.float32)
    mu = jnp.mean(xf, axis=-1, keepdims=True)
    var = jnp.mean(jnp.square(xf - mu), axis=-1, keepdims=True)
    y = (xf - mu) * lax.rsqrt(var + NORM_EPS)
    return (y * g.astype(jnp.float32) + b.astype(jnp.float32)).astype(x.dtype)

def _l2_norm(x):
    return x * lax.rsqrt(jnp.sum(x * x, axis=-1, keepdims=True) + NORM_EPS)

def _causal_dwconv(x, w, b=None):
    K, C = w.shape
    y = lax.conv_general_dilated(x, w[:, None, :].astype(x.dtype), window_strides=(1,),
                                 padding=((K - 1, 0),), dimension_numbers=('NWC', 'WIO', 'NWC'),
                                 feature_group_count=C)
    if b is not None:
        y = y + b.astype(x.dtype)
    return y

def _gated_delta_rule(q, k, v, g, beta):
    B, S, H, DK = q.shape
    DV = v.shape[-1]
    C = GDN_CHUNK
    N = S // C

    def chunks(t):
        return jnp.swapaxes(t.reshape((B, N, C, H) + t.shape[3:]), 2, 3)

    qc, kc, vc, gc, bc = (chunks(t) for t in (q, k, v, g, beta))
    G = jnp.cumsum(gc, axis=-1)
    idx = jnp.arange(C)
    tril = idx[:, None] >= idx[None, :]
    strict = idx[:, None] > idx[None, :]
    L = jnp.exp(jnp.where(tril, G[..., :, None] - G[..., None, :], -jnp.inf))
    kb = kc * bc[..., None]
    A = jnp.where(strict, jnp.einsum('bnhid,bnhjd->bnhij', kb, kc) * L, 0.0)
    rhs = jnp.concatenate([vc * bc[..., None], kb * jnp.exp(G)[..., None]], axis=-1)
    sol = lax.linalg.triangular_solve(A + jnp.eye(C, dtype=A.dtype), rhs, left_side=True, lower=True)
    u, w = sol[..., :DV], sol[..., DV:]
    attn = jnp.einsum('bnhid,bnhjd->bnhij', qc, kc) * L
    q_dec = qc * jnp.exp(G)[..., None]
    k_dec = kc * jnp.exp(G[..., -1:] - G)[..., None]
    chunk_decay = jnp.exp(G[..., -1])

    def step(state, inp):
        u_n, w_n, attn_n, qd_n, kd_n, cd_n = inp
        v_new = u_n - jnp.einsum('bhck,bhkv->bhcv', w_n, state)
        o = jnp.einsum('bhck,bhkv->bhcv', qd_n, state) + jnp.einsum('bhij,bhjv->bhiv', attn_n, v_new)
        state = state * cd_n[..., None, None] + jnp.einsum('bhck,bhcv->bhkv', kd_n, v_new)
        return state, o

    xs = tuple(jnp.moveaxis(t, 1, 0) for t in (u, w, attn, q_dec, k_dec, chunk_decay))
    s0 = jnp.zeros((B, H, DK, DV), q.dtype)
    _, o = lax.scan(step, s0, xs)
    o = jnp.moveaxis(o, 0, 1)
    return jnp.swapaxes(o, 2, 3).reshape(B, S, H, DV)

def _t5_bucket(dist):
    n = np.maximum(dist, 0)
    max_exact = REL_BUCKETS // 2
    large = max_exact + (np.log(np.maximum(n, 1) / max_exact) / np.log(REL_MAX_DIST / max_exact)
                         * (REL_BUCKETS - max_exact)).astype(np.int32)
    large = np.minimum(large, REL_BUCKETS - 1)
    return np.where(n < max_exact, n, large).astype(np.int32)

def _swa_sinks(q, k, v, sinks, band_bias):
    B, S, HQ, hd = q.shape
    HKV = k.shape[2]
    G = HQ // HKV
    W = WINDOW
    N = S // W
    qb = q.reshape(B, N, W, HKV, G, hd)

    def band(t):
        tb = t.reshape(B, N, W, HKV, hd)
        prev = jnp.pad(tb, ((0, 0), (1, 0), (0, 0), (0, 0), (0, 0)))[:, :-1]
        return jnp.concatenate([prev, tb], axis=2)

    kb, vb = band(k), band(v)
    s = jnp.einsum('bniKgd,bnjKd->bnKgij', qb, kb).astype(jnp.float32) * (hd ** -0.5)
    s = s + band_bias.astype(jnp.float32).reshape(1, 1, HKV, G, W, 2 * W)
    i = jnp.arange(W)[:, None]
    j = jnp.arange(2 * W)[None, :]
    dist = i + W - j
    valid = (dist >= 0) & (dist < W)
    valid = valid[None] & ((jnp.arange(N)[:, None, None] > 0) | (j >= W)[None])
    s = jnp.where(valid[None, :, None, None], s, -jnp.inf)
    sink = sinks.astype(jnp.float32).reshape(1, 1, HKV, G, 1, 1)
    m = jnp.maximum(jnp.max(s, axis=-1, keepdims=True), sink)
    p = jnp.exp(s - m)
    p = p / (jnp.sum(p, axis=-1, keepdims=True) + jnp.exp(sink - m))
    o = jnp.einsum('bnKgij,bnjKd->bniKgd', p.astype(v.dtype), vb)
    return o.reshape(B, S, HQ, hd)

def _rglru(x, w_a, b_a, w_x, b_x, lam):
    B, S, W = x.shape
    xf = x.astype(jnp.float32)
    xb = xf.reshape(B, S, LRU_BLOCKS, LRU_BLOCK_W)
    r = jax.nn.sigmoid(jnp.einsum('bsnc,ncd->bsnd', xb, w_a.astype(jnp.float32)).reshape(B, S, W) + b_a)
    ig = jax.nn.sigmoid(jnp.einsum('bsnc,ncd->bsnd', xb, w_x.astype(jnp.float32)).reshape(B, S, W) + b_x)
    log_a = -LRU_C * r * jax.nn.softplus(-lam.astype(jnp.float32))
    a = jnp.exp(log_a)
    bterm = jnp.sqrt(-jnp.expm1(2.0 * log_a)) * (ig * xf)

    def combine(left, right):
        a1, b1 = left
        a2, b2 = right
        return a1 * a2, a2 * b1 + b2

    _, h = lax.associative_scan(combine, (a, bterm), axis=1)
    return h.astype(x.dtype)

def _hybrid_mixer(h, mem, w_in, b_in, a_conv_w, a_log, a_dt_bias, a_norm_g,
                  b_dw_w, b_dw_b, b_ln_g, b_ln_b, c_sinks, band_bias,
                  d_conv_w, d_conv_b, d_w_a, d_b_a, d_w_x, d_b_x, d_lambda,
                  g_mem, w_mem_kv, w_br, w_out):
    B, S, _ = h.shape
    dt = h.dtype
    proj = h @ w_in + b_in
    offsets = [int(o) for o in np.cumsum(SPLIT_SIZES)[:-1]]
    (a_qkv, a_z, a_beta, a_alpha, b_glu, b_z, c_q, c_kv, c_z,
     d_x, d_z, e_q, e_z, gates) = jnp.split(proj, offsets, axis=-1)

    qkv = jax.nn.silu(_causal_dwconv(a_qkv, a_conv_w)).astype(jnp.float32)
    aq, ak, av = jnp.split(qkv, 3, axis=-1)
    aq = _l2_norm(aq.reshape(B, S, GDN_HEADS, GDN_HEAD_DIM)) * (GDN_HEAD_DIM ** -0.5)
    ak = _l2_norm(ak.reshape(B, S, GDN_HEADS, GDN_HEAD_DIM))
    av = av.reshape(B, S, GDN_HEADS, GDN_HEAD_DIM)
    beta = jax.nn.sigmoid(a_beta.astype(jnp.float32))
    g = -jnp.exp(a_log.astype(jnp.float32)) * jax.nn.softplus(a_alpha.astype(jnp.float32) + a_dt_bias)
    ao = _gated_delta_rule(aq, ak, av, g, beta)
    ao = _rms_norm(ao, a_norm_g).reshape(B, S, BRANCH_WIDTH).astype(dt)
    y_a = ao * jax.nn.silu(a_z)

    glu_a, glu_b = jnp.split(b_glu, 2, axis=-1)
    bu = glu_a * jax.nn.sigmoid(glu_b)
    bu = _causal_dwconv(bu, b_dw_w, b_dw_b)
    bu = jax.nn.silu(_layer_norm(bu, b_ln_g, b_ln_b))
    y_b = bu * jax.nn.silu(b_z)

    cq = c_q.reshape(B, S, SWA_Q_HEADS, SWA_HEAD_DIM)
    ck, cv = jnp.split(c_kv, 2, axis=-1)
    ck = ck.reshape(B, S, SWA_KV_HEADS, SWA_HEAD_DIM)
    cv = cv.reshape(B, S, SWA_KV_HEADS, SWA_HEAD_DIM)
    co = _swa_sinks(cq, ck, cv, c_sinks, band_bias).reshape(B, S, BRANCH_WIDTH)
    y_c = co * jax.nn.silu(c_z)

    dxc = _causal_dwconv(d_x, d_conv_w, d_conv_b)
    do = _rglru(dxc, d_w_a, d_b_a, d_w_x, d_b_x, d_lambda)
    y_d = do * jax.nn.silu(d_z)

    mem_kv = _rms_norm(mem, g_mem) @ w_mem_kv
    mk, mv = jnp.split(mem_kv, 2, axis=-1)
    mk = mk.reshape(B, MEM_LEN, XATTN_HEADS, XATTN_HEAD_DIM)
    mv = mv.reshape(B, MEM_LEN, XATTN_HEADS, XATTN_HEAD_DIM)
    eq = e_q.reshape(B, S, XATTN_HEADS, XATTN_HEAD_DIM)
    es = jnp.einsum('bshd,bmhd->bhsm', eq, mk).astype(jnp.float32) * (XATTN_HEAD_DIM ** -0.5)
    ep = jax.nn.softmax(es, axis=-1).astype(dt)
    eo = jnp.einsum('bhsm,bmhd->bshd', ep, mv).reshape(B, S, BRANCH_WIDTH)
    y_e = eo * jax.nn.silu(e_z)

    ys = jnp.stack([y_a, y_b.astype(dt), y_c.astype(dt), y_d.astype(dt), y_e.astype(dt)], axis=2)
    branch_out = jnp.einsum('bsnw,nwd->bsnd', ys, w_br)
    gate = jax.nn.sigmoid(gates.reshape(B, S, N_BRANCHES, D_MODEL))
    merged = jnp.sum(gate * branch_out, axis=2)
    return merged @ w_out

def first_inputs(seed: int = 0) -> dict:
    key = jax.random.key(seed)
    ks = jax.random.split(key, 32)
    f32 = jnp.float32
    L = DEPTH
    W = BRANCH_WIDTH

    def nrm(k, shape, scale):
        return scale * jax.random.normal(k, shape, f32)

    def gain(k, shape):
        return 1.0 + 0.05 * jax.random.normal(k, shape, f32)

    x = nrm(ks[0], (BATCH, SEQ, D_MODEL), 1.0)
    mem = nrm(ks[1], (BATCH, MEM_LEN, D_MODEL), 1.0)
    g_pre = gain(ks[2], (L, D_MODEL))
    g_post = gain(ks[3], (L, D_MODEL))
    w_in = nrm(ks[4], (L, D_MODEL, IN_COLS), D_MODEL ** -0.5)
    b_in = nrm(ks[5], (L, IN_COLS), 0.02)
    a_conv_w = nrm(ks[6], (L, GDN_CONV, 3 * W), GDN_CONV ** -0.5)
    a_log = jnp.log(jax.random.uniform(ks[7], (L, GDN_HEADS), f32, 1.0, 16.0))
    dt0 = jnp.exp(jax.random.uniform(ks[8], (L, GDN_HEADS), f32, math.log(1e-3), math.log(0.1)))
    a_dt_bias = dt0 + jnp.log(-jnp.expm1(-dt0))
    a_norm_g = gain(ks[9], (L, GDN_HEAD_DIM))
    b_dw_w = nrm(ks[10], (L, CONF_WIDTH, W), CONF_WIDTH ** -0.5)
    b_dw_b = nrm(ks[11], (L, W), 0.02)
    b_ln_g = gain(ks[12], (L, W))
    b_ln_b = nrm(ks[13], (L, W), 0.02)
    c_sinks = nrm(ks[14], (L, SWA_Q_HEADS), 0.5)
    rel_bias = nrm(ks[15], (REL_BUCKETS, SWA_Q_HEADS), 0.5)
    d_conv_w = nrm(ks[16], (L, LRU_CONV, W), LRU_CONV ** -0.5)
    d_conv_b = nrm(ks[17], (L, W), 0.02)
    d_w_a = nrm(ks[18], (L, LRU_BLOCKS, LRU_BLOCK_W, LRU_BLOCK_W), LRU_BLOCK_W ** -0.5)
    d_b_a = nrm(ks[19], (L, W), 0.02)
    d_w_x = nrm(ks[20], (L, LRU_BLOCKS, LRU_BLOCK_W, LRU_BLOCK_W), LRU_BLOCK_W ** -0.5)
    d_b_x = nrm(ks[21], (L, W), 0.02)
    u = jax.random.uniform(ks[22], (L, W), f32, 0.9, 0.999)
    a0 = u ** (1.0 / LRU_C)
    d_lambda = jnp.log(a0) - jnp.log1p(-a0)
    g_mem = gain(ks[23], (L, D_MODEL))
    w_mem_kv = nrm(ks[24], (L, D_MODEL, 2 * W), D_MODEL ** -0.5)
    w_br = nrm(ks[25], (L, N_BRANCHES, W, D_MODEL), W ** -0.5)
    w_out = nrm(ks[26], (L, D_MODEL, D_MODEL), D_MODEL ** -0.5)
    return {"x": x, "mem": mem, "g_pre": g_pre, "g_post": g_post, "w_in": w_in, "b_in": b_in,
            "a_conv_w": a_conv_w, "a_log": a_log, "a_dt_bias": a_dt_bias, "a_norm_g": a_norm_g,
            "b_dw_w": b_dw_w, "b_dw_b": b_dw_b, "b_ln_g": b_ln_g, "b_ln_b": b_ln_b,
            "c_sinks": c_sinks, "rel_bias": rel_bias,
            "d_conv_w": d_conv_w, "d_conv_b": d_conv_b, "d_w_a": d_w_a, "d_b_a": d_b_a,
            "d_w_x": d_w_x, "d_b_x": d_b_x, "d_lambda": d_lambda,
            "g_mem": g_mem, "w_mem_kv": w_mem_kv, "w_br": w_br, "w_out": w_out}

def first_block(x, mem, g_pre, g_post, w_in, b_in, a_conv_w, a_log, a_dt_bias, a_norm_g,
              b_dw_w, b_dw_b, b_ln_g, b_ln_b, c_sinks, rel_bias,
              d_conv_w, d_conv_b, d_w_a, d_b_a, d_w_x, d_b_x, d_lambda,
              g_mem, w_mem_kv, w_br, w_out):
    i = np.arange(WINDOW)[:, None]
    j = np.arange(2 * WINDOW)[None, :]
    bucket = _t5_bucket(i + WINDOW - j)
    band_bias = jnp.transpose(rel_bias[bucket], (2, 0, 1))
    for l in range(DEPTH):
        h = _rms_norm(x, g_pre[l])
        y = _hybrid_mixer(h, mem, w_in[l], b_in[l], a_conv_w[l], a_log[l], a_dt_bias[l], a_norm_g[l],
                          b_dw_w[l], b_dw_b[l], b_ln_g[l], b_ln_b[l], c_sinks[l], band_bias,
                          d_conv_w[l], d_conv_b[l], d_w_a[l], d_b_a[l], d_w_x[l], d_b_x[l], d_lambda[l],
                          g_mem[l], w_mem_kv[l], w_br[l], w_out[l])
        x = x + _rms_norm(y, g_post[l])
    return x


_first_inputs = first_inputs


def first_inputs(seed=0):
    import zlib

    import numpy as np

    out = dict(_first_inputs(seed))
    spreads = {}
    factors = {'b_dw_b': 4.361,
     'b_ln_g': 15.089,
     'b_ln_b': 38.39,
     'c_sinks': 64.0,
     'd_b_a': 64.0,
     'd_b_x': 64.0,
     'g_mem': 8.0,
     'a_norm_g': 8.0,
     'rel_bias': 8.0,
     'd_conv_b': 5.537,
     'd_w_a': 2.975}
    for name, (base, spread) in spreads.items():
        noise = np.random.default_rng([zlib.crc32(name.encode()), seed]).standard_normal(out[name].shape)
        drawn = base * np.exp(spread * noise) if base else spread * noise
        out[name] = __import__('jax').numpy.asarray(drawn.astype(out[name].dtype))
    for name, factor in factors.items():
        out[name] = (out[name] * factor).astype(out[name].dtype)
    return out


DEPTH_2 = 2

HEAD_DIM = 128
EPS = 1e-6
ROPE_THETA = 500000.0
ROT_DIM = HEAD_DIM // 4
N_MEM = 256
MEM_HEADS = 4
DIL_GROUPS = ((128, 1), (512, 4), (2048, 16))
A_HEADS = 4
POOL_SIZES = (2, 4, 8, 16)
POOL_CH = 128
CHUNK = 128
C_GROUPS = 8
C_CH = 128

A_WIDTH = A_HEADS * HEAD_DIM
B_WIDTH = len(POOL_SIZES) * POOL_CH
C_WIDTH = C_GROUPS * C_CH
M_WIDTH = MEM_HEADS * HEAD_DIM
EVEN_MIX = A_WIDTH + B_WIDTH + M_WIDTH
ODD_MIX = C_WIDTH + M_WIDTH
A_QK_WIDTH = 2 * len(DIL_GROUPS) * A_WIDTH
EVEN_IN = A_QK_WIDTH + A_WIDTH + B_WIDTH + M_WIDTH + EVEN_MIX
ODD_IN = 2 * C_WIDTH + M_WIDTH + ODD_MIX
N_EVEN = (DEPTH_2 + 1) // 2
N_ODD = DEPTH_2 // 2


def rmsnorm(x, g):
    xf = x.astype(jnp.float32)
    y = xf * lax.rsqrt(jnp.mean(xf * xf, axis=-1, keepdims=True) + EPS)
    return (y * g.astype(jnp.float32)).astype(x.dtype)

def layernorm(x, g, b):
    xf = x.astype(jnp.float32)
    mu = jnp.mean(xf, axis=-1, keepdims=True)
    xc = xf - mu
    y = xc * lax.rsqrt(jnp.mean(xc * xc, axis=-1, keepdims=True) + EPS)
    return (y * g.astype(jnp.float32) + b.astype(jnp.float32)).astype(x.dtype)

def rope_tables(positions):
    pos = positions.astype(jnp.float32)
    inv = ROPE_THETA ** (-jnp.arange(0, ROT_DIM, 2, dtype=jnp.float32) / ROT_DIM)
    ang = pos[..., None] * inv
    return jnp.cos(ang), jnp.sin(ang)

def apply_partial_rope(x, cos, sin):
    half = ROT_DIM // 2
    xr = x[..., :ROT_DIM].astype(jnp.float32)
    x1, x2 = xr[..., :half], xr[..., half:]
    c, s = cos[:, :, None, :], sin[:, :, None, :]
    rot = jnp.concatenate([x1 * c - x2 * s, x2 * c + x1 * s], axis=-1).astype(x.dtype)
    return jnp.concatenate([rot, x[..., ROT_DIM:]], axis=-1)

def _to_strided(x, dil, blk):
    b, s, h, d = x.shape
    unit = dil * blk
    lp = -(-s // unit) * unit
    x = jnp.pad(x, ((0, 0), (0, lp - s), (0, 0), (0, 0)))
    x = x.reshape(b, lp // dil, dil, h, d).transpose(0, 2, 1, 3, 4)
    return x.reshape(b, dil, lp // unit, blk, h, d)

def _from_strided(x, seq):
    b, dil, nb, blk = x.shape[:4]
    rest = x.shape[4:]
    x = jnp.moveaxis(x.reshape((b, dil, nb * blk) + rest), 1, 2)
    return x.reshape((b, nb * blk * dil) + rest)[:, :seq]

def dilated_window_group(q, k, v, window, dil):
    span = window // dil
    blk = span
    seq = q.shape[1]
    qb, kb, vb = (_to_strided(t, dil, blk) for t in (q, k, v))
    nb = qb.shape[2]

    def with_prev(t):
        prev = jnp.concatenate([jnp.zeros_like(t[:, :, :1]), t[:, :, :-1]], axis=2)
        return jnp.concatenate([prev, t], axis=3)

    kk, vv = with_prev(kb), with_prev(vb)
    scores = jnp.einsum('brnqhd,brnkhd->brnhqk', qb, kk,
                        preferred_element_type=jnp.float32) * (HEAD_DIM ** -0.5)
    qi = jnp.arange(blk)[:, None]
    kj = jnp.arange(2 * blk)[None, :]
    off = blk + qi - kj
    band = (off >= 0) & (off <= span)
    not_before_start = (jnp.arange(nb)[:, None, None] > 0) | (kj[None] >= blk)
    valid = band[None] & not_before_start
    scores = jnp.where(valid[None, None, :, None], scores, -jnp.inf)
    m = jnp.max(scores, axis=-1)
    p = jnp.exp(scores - m[..., None])
    den = jnp.sum(p, axis=-1)
    num = jnp.einsum('brnhqk,brnkhd->brnqhd', p, vv.astype(jnp.float32))
    m = jnp.swapaxes(m, 3, 4)
    den = jnp.swapaxes(den, 3, 4)
    return _from_strided(num, seq), _from_strided(m, seq), _from_strided(den, seq)

def dilated_attention_mixer(qk, v_a, cos, sin):
    nums, ms, dens = [], [], []
    for gi, (window, dil) in enumerate(DIL_GROUPS):
        q = apply_partial_rope(qk[:, :, gi, 0], cos, sin)
        k = apply_partial_rope(qk[:, :, gi, 1], cos, sin)
        num, m, den = dilated_window_group(q, k, v_a, window, dil)
        nums.append(num); ms.append(m); dens.append(den)
    ms = jnp.stack(ms)
    wts = jnp.exp(ms - jnp.max(ms, axis=0, keepdims=True))
    num = sum(wts[g][..., None] * nums[g] for g in range(len(DIL_GROUPS)))
    den = jnp.sum(wts * jnp.stack(dens), axis=0)
    out = num / den[..., None]
    b, s = out.shape[:2]
    return out.reshape(b, s, A_WIDTH).astype(v_a.dtype)

def multiscale_pool(xp, w_pool, scale):
    b, s, _ = xp.shape
    xg = xp.reshape(b, s, len(POOL_SIZES), POOL_CH).astype(jnp.float32)
    c = jnp.cumsum(xg, axis=1)
    t = jnp.arange(s)
    outs = []
    for gi, w in enumerate(POOL_SIZES):
        cg = c[:, :, gi]
        lag = jnp.pad(cg, ((0, 0), (w, 0), (0, 0)))[:, :s]
        cnt = jnp.minimum(t + 1, w).astype(jnp.float32)[None, :, None]
        outs.append((cg - lag) / cnt - xg[:, :, gi])
    pooled = jnp.stack(outs, axis=2)
    y = jnp.einsum('bsgc,gcd->bsgd', pooled, w_pool.astype(jnp.float32))
    return (y.reshape(b, s, B_WIDTH) * scale.astype(jnp.float32)).astype(xp.dtype)

def chunked_spatial_gating(u, v, ln_g, ln_b, w_s, b_s):
    b, s, _ = u.shape
    vn = layernorm(v, ln_g, ln_b)
    vc = vn.reshape(b, s // CHUNK, CHUNK, C_GROUPS, C_CH)
    tril = jnp.tril(jnp.ones((CHUNK, CHUNK), dtype=bool))
    ws = jnp.where(tril[None], w_s, jnp.zeros_like(w_s))
    mixed = jnp.einsum('gts,bnsgc->bntgc', ws, vc) + b_s.T[None, None, :, :, None]
    return u * mixed.reshape(b, s, C_WIDTH)

def memory_attention(q_m, mem_n, w_mem_kv):
    b, s = q_m.shape[:2]
    q = q_m.reshape(b, s, MEM_HEADS, HEAD_DIM)
    mk, mv = jnp.split(mem_n @ w_mem_kv, 2, axis=-1)
    mk = mk.reshape(b, -1, MEM_HEADS, HEAD_DIM)
    mv = mv.reshape(b, -1, MEM_HEADS, HEAD_DIM)
    sc = jnp.einsum('bshd,bmhd->bhsm', q, mk,
                    preferred_element_type=jnp.float32) * (HEAD_DIM ** -0.5)
    p = jax.nn.softmax(sc, axis=-1)
    out = jnp.einsum('bhsm,bmhd->bshd', p, mv.astype(jnp.float32))
    return out.reshape(b, s, M_WIDTH).astype(q_m.dtype)

def even_layer(x, cos, sin, mem_n, g_norm, w_in, w_pool, pool_scale, w_mem_kv, w_out):
    b, s, _ = x.shape
    h = rmsnorm(x, g_norm)
    proj = h @ w_in
    cuts = np.cumsum([A_QK_WIDTH, A_WIDTH, B_WIDTH, M_WIDTH]).tolist()
    qk, v_a, x_b, q_m, z = jnp.split(proj, cuts, axis=-1)
    qk = qk.reshape(b, s, len(DIL_GROUPS), 2, A_HEADS, HEAD_DIM)
    v_a = v_a.reshape(b, s, A_HEADS, HEAD_DIM)
    a_out = dilated_attention_mixer(qk, v_a, cos, sin)
    b_out = multiscale_pool(x_b, w_pool, pool_scale)
    m_out = memory_attention(q_m, mem_n, w_mem_kv)
    y = jnp.concatenate([a_out, b_out, m_out], axis=-1) * jax.nn.silu(z)
    return x + y @ w_out

def odd_layer(x, mem_n, g_norm, w_in, ln_g, ln_b, w_s, b_s, w_mem_kv, w_out):
    h = rmsnorm(x, g_norm)
    proj = h @ w_in
    cuts = np.cumsum([C_WIDTH, C_WIDTH, M_WIDTH]).tolist()
    u, v, q_m, z = jnp.split(proj, cuts, axis=-1)
    c_out = chunked_spatial_gating(u, v, ln_g, ln_b, w_s, b_s)
    m_out = memory_attention(q_m, mem_n, w_mem_kv)
    y = jnp.concatenate([c_out, m_out], axis=-1) * jax.nn.silu(z)
    return x + y @ w_out

def second_inputs(seed: int = 0) -> dict:
    key = jax.random.key(seed)
    ks = jax.random.split(key, 24)
    nrm = jax.random.normal
    f32 = jnp.float32
    offs = jax.random.randint(ks[2], (BATCH, 1), 0, 1024)
    positions = (jnp.arange(SEQ, dtype=jnp.int32)[None, :] + offs).astype(jnp.int32)
    return {
        "x": nrm(ks[0], (BATCH, SEQ, D_MODEL), f32),
        "mem": nrm(ks[1], (BATCH, N_MEM, D_MODEL), f32),
        "positions": positions,
        "g_mem": 1.0 + 0.02 * nrm(ks[3], (D_MODEL,), f32),
        "even_norm_g": 1.0 + 0.02 * nrm(ks[4], (N_EVEN, D_MODEL), f32),
        "even_w_in": nrm(ks[5], (N_EVEN, D_MODEL, EVEN_IN), f32) * D_MODEL ** -0.5,
        "even_w_pool": nrm(ks[6], (N_EVEN, len(POOL_SIZES), POOL_CH, POOL_CH), f32) * POOL_CH ** -0.5,
        "even_pool_scale": 1.0 + 0.02 * nrm(ks[7], (N_EVEN, B_WIDTH), f32),
        "even_w_mem_kv": nrm(ks[8], (N_EVEN, D_MODEL, 2 * M_WIDTH), f32) * D_MODEL ** -0.5,
        "even_w_out": nrm(ks[9], (N_EVEN, EVEN_MIX, D_MODEL), f32) * EVEN_MIX ** -0.5,
        "odd_norm_g": 1.0 + 0.02 * nrm(ks[10], (N_ODD, D_MODEL), f32),
        "odd_w_in": nrm(ks[11], (N_ODD, D_MODEL, ODD_IN), f32) * D_MODEL ** -0.5,
        "odd_ln_g": 1.0 + 0.02 * nrm(ks[12], (N_ODD, C_WIDTH), f32),
        "odd_ln_b": 0.02 * nrm(ks[13], (N_ODD, C_WIDTH), f32),
        "odd_w_s": nrm(ks[14], (N_ODD, C_GROUPS, CHUNK, CHUNK), f32) * CHUNK ** -0.5,
        "odd_b_s": 1.0 + 0.02 * nrm(ks[15], (N_ODD, C_GROUPS, CHUNK), f32),
        "odd_w_mem_kv": nrm(ks[16], (N_ODD, D_MODEL, 2 * M_WIDTH), f32) * D_MODEL ** -0.5,
        "odd_w_out": nrm(ks[17], (N_ODD, ODD_MIX, D_MODEL), f32) * ODD_MIX ** -0.5,
        "final_norm_g": 1.0 + 0.02 * nrm(ks[18], (D_MODEL,), f32),
    }

def second_block(x, mem, positions, g_mem, even_norm_g, even_w_in, even_w_pool, even_pool_scale,
              even_w_mem_kv, even_w_out, odd_norm_g, odd_w_in, odd_ln_g, odd_ln_b, odd_w_s,
              odd_b_s, odd_w_mem_kv, odd_w_out, final_norm_g):
    cos, sin = rope_tables(positions)
    mem_n = rmsnorm(mem, g_mem)
    for layer in range(DEPTH_2):
        i = layer // 2
        if layer % 2 == 0:
            x = even_layer(x, cos, sin, mem_n, even_norm_g[i], even_w_in[i], even_w_pool[i],
                           even_pool_scale[i], even_w_mem_kv[i], even_w_out[i])
        else:
            x = odd_layer(x, mem_n, odd_norm_g[i], odd_w_in[i], odd_ln_g[i], odd_ln_b[i],
                          odd_w_s[i], odd_b_s[i], odd_w_mem_kv[i], odd_w_out[i])
    return rmsnorm(x, final_norm_g)


_first_inputs_2 = second_inputs


def second_inputs(seed=0):
    import zlib

    import numpy as np

    out = dict(_first_inputs_2(seed))
    spreads = {}
    factors = {'g_mem': 8.0,
     'even_norm_g': 5.82,
     'even_pool_scale': 8.0,
     'odd_norm_g': 3.829,
     'odd_ln_g': 8.0,
     'odd_ln_b': 8.0,
     'odd_b_s': 7.15,
     'final_norm_g': 2.903}
    for name, (base, spread) in spreads.items():
        noise = np.random.default_rng([zlib.crc32(name.encode()), seed]).standard_normal(out[name].shape)
        drawn = base * np.exp(spread * noise) if base else spread * noise
        out[name] = __import__('jax').numpy.asarray(drawn.astype(out[name].dtype))
    for name, factor in factors.items():
        out[name] = (out[name] * factor).astype(out[name].dtype)
    return out


_narrow_inputs = second_inputs


def second_inputs(seed=0):

    out = dict(_narrow_inputs(seed))
    wider = {'odd_norm_g': 3.03,
     'odd_ln_g': 8.79,
     'odd_ln_b': 8.57,
     'odd_b_s': 6.82,
     'final_norm_g': 3.27}
    for name, times in wider.items():
        mean = out[name].mean()
        out[name] = (mean + times * (out[name] - mean)).astype(out[name].dtype)
    return out


def setup_inputs(seed=0):
    out = dict(first_inputs(seed))
    for name, value in second_inputs(seed + 1).items():
        if name != "x":
            out[name + "_2"] = value
    return out


def reference(
    x, mem, g_pre, g_post, w_in, b_in, a_conv_w, a_log, a_dt_bias, a_norm_g, b_dw_w, b_dw_b,
    b_ln_g, b_ln_b, c_sinks, rel_bias, d_conv_w, d_conv_b, d_w_a, d_b_a, d_w_x, d_b_x, d_lambda,
    g_mem, w_mem_kv, w_br, w_out, mem_2, positions_2, g_mem_2, even_norm_g_2, even_w_in_2,
    even_w_pool_2, even_pool_scale_2, even_w_mem_kv_2, even_w_out_2, odd_norm_g_2, odd_w_in_2,
    odd_ln_g_2, odd_ln_b_2, odd_w_s_2, odd_b_s_2, odd_w_mem_kv_2, odd_w_out_2, final_norm_g_2,
):
    x = first_block(
        x, mem, g_pre, g_post, w_in, b_in, a_conv_w, a_log, a_dt_bias, a_norm_g, b_dw_w, b_dw_b,
        b_ln_g, b_ln_b, c_sinks, rel_bias, d_conv_w, d_conv_b, d_w_a, d_b_a, d_w_x, d_b_x,
        d_lambda, g_mem, w_mem_kv, w_br, w_out,
    )
    return second_block(
        x, mem_2, positions_2, g_mem_2, even_norm_g_2, even_w_in_2, even_w_pool_2,
        even_pool_scale_2, even_w_mem_kv_2, even_w_out_2, odd_norm_g_2, odd_w_in_2, odd_ln_g_2,
        odd_ln_b_2, odd_w_s_2, odd_b_s_2, odd_w_mem_kv_2, odd_w_out_2, final_norm_g_2,
    )


_drawn_inputs = setup_inputs


def setup_inputs(seed=0):
    import zlib

    import numpy as np

    out = dict(_drawn_inputs(seed))
    spreads = {}
    factors = {}
    for name, (base, spread) in spreads.items():
        noise = np.random.default_rng([zlib.crc32(name.encode()), seed]).standard_normal(out[name].shape)
        drawn = base * np.exp(spread * noise) if base else spread * noise
        out[name] = __import__('jax').numpy.asarray(drawn.astype(out[name].dtype))
    for name, factor in factors.items():
        out[name] = (out[name] * factor).astype(out[name].dtype)
    return out
```

```python
from contextlib import ExitStack

import numpy as np
import concourse.bass as bass
from concourse import mybir

F32 = mybir.dt.float32
F32R = mybir.dt.float32r
I32 = mybir.dt.int32
ACT = mybir.ActivationFunctionType
ALU = mybir.AluOpType
AX = mybir.AxisListType.X

P = 128
T = 1024
D = 1024
KD = D // P
HALF = 512
W = 512
MEM = 256
NEG = -1.0e30
EPS = 1e-6

C_AQKV, C_AZ, C_BA = 0, 1536, 2048
C_GLU, C_BZ = 2056, 3080
C_CQ, C_CKV, C_CZ = 3592, 4104, 4360
C_DX, C_DZ, C_EQ, C_EZ, C_GATE = 4872, 5384, 5896, 6408, 6920
C2_V, C2_X, C2_Q, C2_Z = 3072, 3584, 4096, 4608
C3_U, C3_V, C3_Q, C3_Z = 0, 1024, 2048, 2560

REL_BUCKETS, REL_MAX_DIST, WINDOW = 32, 128, 128
NLEVEL = 7


def bucket_of(dist):
    n = np.maximum(dist, 0)
    exact = REL_BUCKETS // 2
    large = exact + (np.log(np.maximum(n, 1) / exact) / np.log(REL_MAX_DIST / exact)
                     * (REL_BUCKETS - exact)).astype(np.int32)
    return np.where(n < exact, n, np.minimum(large, REL_BUCKETS - 1))


def constant_parts():
    i = np.arange(P)[:, None]
    j = np.arange(P)[None, :]
    c = {}
    c["ident"] = (i == j)
    c["ones"] = np.ones((P, P))
    c["upto"] = (i <= j)
    c["negafter"] = np.where(i > j, NEG, 0.0)
    for lv in range(NLEVEL):
        s = 1 << lv
        c[f"lev{lv}"] = ((i // (2 * s)) == (j // (2 * s))) & ((i // s) % 2 == 0) & ((j // s) % 2 == 1)
    k2 = np.arange(2 * P)[None, :]
    ok = (k2 >= i) & (k2 <= i + P)
    c["band"] = np.where(ok, 0.0, NEG)
    c["bandfirst"] = np.where(ok & (k2 >= P), 0.0, NEG)
    c["pair"] = np.where(((i // 64) == (j // 64)) & (j <= i), 0.0, NEG)
    perm = np.zeros((P, 32))
    for m in range(32):
        perm[(m + 16) % 32, m] = 1.0
    c["perm"] = perm
    inv = np.zeros((P, 2))
    inv[:32, 0] = np.tile(500000.0 ** (-np.arange(0, 32, 2, dtype=np.float32) / np.float32(32)), 2)
    inv[:32, 1] = np.where(np.arange(32) < 16, -1.0, 1.0)
    c["rope"] = inv
    c["icount"] = np.broadcast_to(np.concatenate(
        [1.0 / np.minimum(np.arange(16) + 1, w) for w in (2, 4, 8, 16)])[None], (P, 64))
    return {k: np.ascontiguousarray(np.asarray(v, np.float32)) for k, v in c.items()}


def bias_parts():
    pos = np.arange(384)
    dist = 255 - pos
    ok = (dist >= 0) & (dist < WINDOW)
    hot = np.zeros((P, 384), np.float32)
    hot[bucket_of(dist)[ok], pos[ok]] = 1.0
    mask = np.zeros((P, 384), np.float32)
    mask[:8] = np.where(ok, 0.0, NEG)
    flip = np.eye(P, dtype=np.float32)[::-1]
    return np.ascontiguousarray(np.concatenate([hot, mask, flip], axis=1))


def constants():
    parts = constant_parts()
    at, n = {}, 0
    for k, v in parts.items():
        at[k] = (n, v.shape[1])
        n += v.shape[1]
    return np.concatenate(list(parts.values()), axis=1), at, n


class Event:
    def __init__(self, sem, base):
        self.sem, self.base = sem, base

    def nth(self, i):
        return self.base + i + 1


class Signals:
    def __init__(self, nc, ctx):
        self.nc, self.ctx, self.sems, self.next = nc, ctx, {}, {}

    def sem(self, name):
        if name not in self.sems:
            self.sems[name] = self.ctx.enter_context(self.nc.semaphore(name))
            self.next[name] = 0
        return self.sems[name]

    def take(self, name, n):
        sem = self.sem(name)
        base = self.next[name]
        self.next[name] = base + n
        return Event(sem, base)


class Job:
    def __init__(self, t, nk):
        self.t, self.nk, self.slot = t, nk, t % 2


class Run:
    def __init__(self, t0, pairs, src, nk):
        self.t0, self.pairs, self.src, self.nk = t0, pairs, src, nk

    def t(self, i, p):
        return self.t0 + 2 * i + p


def rows128(v):
    return v.rearrange("(n p) -> n p", p=P)


def hybrid_program(nc, A, out):
    ctx = ExitStack()
    with ctx:
        _hybrid(nc, ctx, A, out)


def _hybrid(nc, ctx, A, out):
    def sb(name, shape, dt=F32):
        return ctx.enter_context(nc.sbuf_tensor(name, shape, dt))

    sig = Signals(nc, ctx)
    _, CAT, NCONST = constants()

    h_hi = sb("h_hi", [P, KD, T], F32R)
    h_lo = sb("h_lo", [P, KD, T], F32R)
    y_hi = sb("y_hi", [P, 4, T], F32R)
    y_lo = sb("y_lo", [P, 4, T], F32R)
    acc = sb("acc", [P, KD, T])
    w_raw = sb("w_raw", [P, 2, KD, P])
    w_hi = sb("w_hi", [P, 2, KD, P], F32R)
    w_lo = sb("w_lo", [P, 2, KD, P], F32R)
    wrk = sb("wrk", [P, 11, T])
    cst = sb("cst", [P, NCONST])
    cols = sb("cols", [P, 392])
    small = sb("small", [P, 344])
    pool_one = sb("pool_one", [P, 1])
    ps = ctx.enter_context(nc.psum_tensor("ps", [P, 8, HALF], F32))
    x_fm = nc.dram_tensor("x_fm", [KD, P, T], F32, kind="Internal").ap()
    bias_rows = nc.dram_tensor("bias_rows", [8, 384], F32, kind="Internal")

    def C(name):
        a, n = CAT[name]
        return cst[:, a:a + n]

    ident, ones = C("ident"), C("ones")

    def wt(j, half=None):
        return wrk[:, j, :] if half is None else wrk[:, j, half * HALF:(half + 1) * HALF]

    b_in = A["b_in"][0]
    segs = []

    def seg(name, ap):
        segs.append((name, ap))

    seg("b_aqkv", rows128(b_in[C_AQKV:C_AZ]))
    seg("b_az", rows128(b_in[C_AZ:C_BA]))
    seg("b_ba", rows128(b_in[C_BA:C_BA + P]))
    seg("b_glu", rows128(b_in[C_GLU:C_BZ]))
    seg("b_bz", rows128(b_in[C_BZ:C_CQ]))
    seg("b_cq", b_in[C_CQ:C_CKV].rearrange("(u t j) -> t u j", u=2, j=64))
    seg("b_ckv", rows128(b_in[C_CKV:C_CZ]))
    seg("b_cz", b_in[C_CZ:C_DX].rearrange("(u t j) -> t u j", u=2, j=64))
    seg("b_dx", rows128(b_in[C_DX:C_DZ]))
    seg("b_dz", rows128(b_in[C_DZ:C_EQ]))
    seg("b_eq", rows128(b_in[C_EQ:C_EZ]))
    seg("b_ez", rows128(b_in[C_EZ:C_GATE]))
    seg("b_gate", rows128(b_in[C_GATE:C_GATE + 5 * D]))
    for name in ("g_pre", "g_post", "g_mem", "b_dw_b", "b_ln_g", "b_ln_b", "d_conv_b", "d_b_a", "d_b_x",
                 "d_lambda", "a_norm_g", "even_norm_g_2", "odd_norm_g_2", "even_pool_scale_2",
                 "odd_ln_g_2", "odd_ln_b_2"):
        seg(name, rows128(A[name][0]))
    seg("g_mem_2", rows128(A["g_mem_2"]))
    seg("final_norm_g_2", rows128(A["final_norm_g_2"]))
    for name in ("a_conv_w", "d_conv_w", "b_dw_w"):
        seg(name, A[name][0].rearrange("k (n p) -> (k n) p", p=P))
    COL, nrows = {}, 0
    row_loads = []
    for name, ap in segs:
        COL[name] = nrows
        n, done = ap.shape[0], 0
        while done < n:
            k = min(n - done, P - nrows % P)
            row_loads.append((nrows // P, nrows % P, k, ap[done:done + k]))
            done += k
            nrows += k
    TABLE_ROWS = [min(P, nrows - P * j) for j in range(-(-nrows // P))]
    assert nrows <= 392, nrows

    def col(name, i=0):
        j = COL[name] + i
        return cols[:, j:j + 1]

    raw_loaded = [sig.sem(f"raw_loaded{s}") for s in range(2)]
    tiles_split = sig.sem("tiles_split")
    dense_out = sig.sem("dense_out")
    dense_free = [sig.sem(f"dense_free{b}") for b in range(2)]
    runs, ntiles = [], 0

    def run(pairs, src0, src1, nk0=KD, nk1=KD):
        nonlocal ntiles
        r = Run(ntiles, pairs, (src0, src1), (nk0, nk1))
        runs.append(r)
        ntiles += 2 * pairs
        return r

    def weights(name, layer=0):
        w = A[name]
        w = w[layer] if len(w.shape) == 3 else w
        return w.rearrange("(k p) n -> p k n", p=P)

    def tiles_of(w, first, step=P):
        return lambda i: w[:, :, bass.ds(i * step + first, P)] if not isinstance(i, int) \
            else w[:, :, first + i * step:first + i * step + P]

    def both(w, first):
        return tiles_of(w, first, 2 * P), tiles_of(w, first + P, 2 * P)

    def rhs_h(part, k, b):
        return (h_hi, h_lo)[part][:, k, b * HALF:(b + 1) * HALF]

    def rhs_y(part, k, b):
        return (y_hi, y_lo)[part][:, k, b * HALF:(b + 1) * HALF]

    def mem_view(t):
        return t[:, 0:2, :].rearrange("p a (b m) -> p (a b) m", m=MEM)

    def rhs_mem(part, k, b):
        return mem_view((y_hi, y_lo)[part])[:, k, b * P:(b + 1) * P]

    engines = ("pe", "act", "dve")
    at_end = {e: sig.sem(f"{e}_at_stage_end") for e in engines}
    stages = []

    def stage(name, **fns):
        stages.append((name, fns))

    class Chain:
        def __init__(self, eng, name):
            self.eng, self.sem, self.n = eng, sig.sem(name), 0

        def link(self, ins):
            self.eng.wait_ge(self.sem, self.mark(ins))

        def mark(self, ins):
            self.n += 1
            ins.then_inc(self.sem, 1)
            return self.n

        def after(self, n):
            self.eng.wait_ge(self.sem, n)

    chains = {}

    def dense_tile(pe, t, slot, nk, rhs, n=HALF):
        pe.wait_ge(tiles_split, t + 1)
        for b in range(2):
            pe.wait_ge(dense_free[b], t + 1)
            for k in range(nk):
                for q, (w, part) in enumerate(((w_hi, 0), (w_hi, 1), (w_lo, 0))):
                    mm = nc.tensor.matmul(ps[:, b, 0:n], w[:, slot, k, :], rhs(part, k, b),
                                          start=(k == 0 and q == 0), stop=(k == nk - 1 and q == 2))
            mm.then_inc(dense_out, 1)

    def dense_run(pe, r, rhs0, rhs1, n=HALF):
        def body(i):
            for p, rhs in ((0, rhs0), (1, rhs1)):
                dense_tile(pe, r.t(i, p), (r.t0 + p) % 2, r.nk[p], rhs, n)
        if r.pairs == 1:
            body(0)
        else:
            with pe.Fori(0, r.pairs, 1) as i:
                body(i)

    def out_ready(eng, t, b):
        eng.wait_ge(dense_out, 2 * t + b + 1)

    def out_taken(eng, t, b):
        eng.wait_ge(dense_free[b], t + 2)

    def project(name, r, dst, bias=None, rhs=None, n=HALF):
        def f_pe(pe):
            dense_run(pe, r, rhs or rhs_h, rhs or rhs_h, n)

        def f_act(act):
            for j in range(2 * r.pairs):
                t = r.t0 + j
                for b in range(2):
                    out_ready(act, t, b)
                    if bias is None:
                        nc.scalar.activation(dst(j, b), ps[:, b, 0:n], ACT.Copy).then_inc(dense_free[b], 1)
                    else:
                        nc.scalar.activation(dst(j, b), ps[:, b, 0:n], ACT.Identity,
                                             bias=bias(j)).then_inc(dense_free[b], 1)
        stage(name, pe=f_pe, act=f_act)

    def to_tiles(first):
        return lambda j, b: wt(first + j, b)

    def gate_z(name, r, o, bias, sz, yt, yfirst=0):
        done = sig.take("y_done", 4 * r.pairs)

        def f_pe(pe):
            dense_run(pe, r, rhs_h, rhs_h)

        def f_act(act):
            for j in range(2 * r.pairs):
                for b in range(2):
                    out_ready(act, r.t0 + j, b)
                    if j >= 1:
                        act.wait_ge(done.sem, done.nth(2 * (j - 1) + b))
                    nc.scalar.activation(wt(sz, b), ps[:, b, :], ACT.Silu,
                                         bias=bias(j) if bias else 0.0).then_inc(dense_free[b], 1)

        def f_dve(dve):
            ch = chains["dve"]
            for j in range(2 * r.pairs):
                for b in range(2):
                    out_taken(dve, r.t0 + j, b)
                    ch.link(nc.vector.tensor_tensor(wt(yt, b), o(j, b), wt(sz, b), ALU.mult))
                    hi = y_hi[:, yfirst + j, b * HALF:(b + 1) * HALF]
                    lo = y_lo[:, yfirst + j, b * HALF:(b + 1) * HALF]
                    ch.link(nc.vector.tensor_copy(hi, wt(yt, b)))
                    nc.vector.tensor_tensor(lo, wt(yt, b), hi.bitcast(F32), ALU.subtract).then_inc(done.sem, 1)
        stage(name, pe=f_pe, act=f_act, dve=f_dve)

    def merge(name, r, gate_bias, first):
        done = sig.take("merged", 2 * r.pairs)

        def f_pe(pe):
            dense_run(pe, r, rhs_y, rhs_h)

        def f_act(act):
            for i in range(r.pairs):
                for p in range(2):
                    for b in range(2):
                        out_ready(act, r.t(i, p), b)
                        if i >= 1:
                            act.wait_ge(done.sem, done.nth(2 * (i - 1) + b))
                        if p == 0:
                            nc.scalar.activation(wt(4, b), ps[:, b, :], ACT.Copy).then_inc(dense_free[b], 1)
                        else:
                            nc.scalar.activation(wt(5, b), ps[:, b, :], ACT.Sigmoid,
                                                 bias=gate_bias(i)).then_inc(dense_free[b], 1)

        def f_dve(dve):
            ch = chains["dve"]
            for i in range(r.pairs):
                for b in range(2):
                    out_taken(dve, r.t(i, 1), b)
                    a = acc[:, i, b * HALF:(b + 1) * HALF]
                    if first:
                        nc.vector.tensor_tensor(a, wt(4, b), wt(5, b), ALU.mult).then_inc(done.sem, 1)
                    else:
                        ch.link(nc.vector.tensor_tensor(wt(6, b), wt(4, b), wt(5, b), ALU.mult))
                        nc.vector.tensor_tensor(a, a, wt(6, b), ALU.add).then_inc(done.sem, 1)
        stage(name, pe=f_pe, act=f_act, dve=f_dve)

    def add_out(name, r):
        def f_pe(pe):
            dense_run(pe, r, rhs_y, rhs_y)

        def f_dve(dve):
            for j in range(2 * r.pairs):
                for b in range(2):
                    out_ready(dve, r.t0 + j, b)
                    a = acc[:, j, b * HALF:(b + 1) * HALF]
                    nc.vector.tensor_tensor(a, a, ps[:, b, :], ALU.add).then_inc(dense_free[b], 1)
        stage(name, pe=f_pe, dve=f_dve)

    def norm(name, src, n, g, emit, nemit=1, width=D, nk=KD, sq=0, rs=2):
        squared = sig.take("squared", 2 * nk)
        summed = sig.take("squares_summed", 2 * nk)
        root = sig.take("root", 2)

        def f_act(act):
            for b in range(2):
                for k in range(nk):
                    i = b * nk + k
                    if i >= 2:
                        act.wait_ge(summed.sem, summed.nth(i - 2))
                    nc.scalar.activation(wt(sq, i % 2)[:, 0:n], src(k, b), ACT.Square).then_inc(squared.sem, 1)
                act.wait_ge(summed.sem, summed.nth(b * nk + nk - 1))
                nc.scalar.activation(wt(rs, b)[:, 0:n], ps[:, 2 + b, 0:n], ACT.Sqrt, bias=EPS,
                                     scale=1.0 / width).then_inc(root.sem, 1)

        def f_pe(pe):
            for b in range(2):
                for k in range(nk):
                    i = b * nk + k
                    pe.wait_ge(squared.sem, squared.nth(i))
                    nc.tensor.matmul(ps[:, 2 + b, 0:n], ones, wt(sq, i % 2)[:, 0:n], start=(k == 0),
                                     stop=(k == nk - 1)).then_inc(summed.sem, 1)

        def f_dve(dve):
            ch = chains["dve"]
            for b in range(2):
                dve.wait_ge(root.sem, root.nth(b))
                ch.link(nc.vector.reciprocal(wt(rs, b)[:, 0:n], wt(rs, b)[:, 0:n]))
                for k in range(nk):
                    emit(ch, k, b, wt(rs, b)[:, 0:n])
        stage(name, pe=f_pe, act=f_act, dve=f_dve)

    def split_emit(src, g, hi, lo, n, tmp=3):
        def emit(ch, k, b, root):
            t = wt(tmp, k % 2)[:, 0:n]
            ch.link(nc.vector.scalar_tensor_tensor(t, src(k, b), g(k), root, ALU.mult, ALU.mult))
            ch.link(nc.vector.tensor_copy(hi(k, b), t))
            ch.link(nc.vector.tensor_tensor(lo(k, b), t, hi(k, b).bitcast(F32), ALU.subtract))
        return emit

    def acc_at(k, b):
        return acc[:, k, b * HALF:(b + 1) * HALF]

    def norm_acc(name, g):
        norm(name, acc_at, HALF, None, split_emit(
            acc_at, lambda k: col(g, k), lambda k, b: h_hi[:, k, b * HALF:(b + 1) * HALF],
            lambda k, b: h_lo[:, k, b * HALF:(b + 1) * HALF], HALF))

    def head_norm(name, tile, n, scale, factor, sq=4, rs=6):
        squared = sig.take("hn_squared", 2 * n)
        summed = sig.take("hn_summed", 2 * n)
        root = sig.take("hn_root", 2 * n)
        normed = sig.take("hn_normed", 2 * n)

        def f_act(act):
            for i in range(2 * n + 2):
                if i < 2 * n:
                    if i >= 2:
                        act.wait_ge(summed.sem, summed.nth(i - 2))
                    nc.scalar.activation(wt(sq, i % 2), tile(i // 2, i % 2), ACT.Square).then_inc(squared.sem, 1)
                if i >= 2:
                    j = i - 2
                    act.wait_ge(summed.sem, summed.nth(j))
                    if j >= 2:
                        act.wait_ge(normed.sem, normed.nth(j - 2))
                    nc.scalar.activation(wt(rs, j % 2), ps[:, 2 + j % 4, :], ACT.Sqrt, bias=EPS,
                                         scale=scale).then_inc(root.sem, 1)

        def f_pe(pe):
            for i in range(2 * n):
                pe.wait_ge(squared.sem, squared.nth(i))
                if i >= 4:
                    pe.wait_ge(root.sem, root.nth(i - 4))
                nc.tensor.matmul(ps[:, 2 + i % 4, :], ones, wt(sq, i % 2), start=True,
                                 stop=True).then_inc(summed.sem, 1)

        def f_dve(dve):
            ch = chains["dve"]
            for i in range(2 * n):
                dve.wait_ge(root.sem, root.nth(i))
                ch.link(nc.vector.reciprocal(wt(rs, i % 2), wt(rs, i % 2)))
                x = tile(i // 2, i % 2)
                nc.vector.scalar_tensor_tensor(x, x, factor(i // 2), wt(rs, i % 2), ALU.mult,
                                               ALU.mult).then_inc(normed.sem, 1)
        stage(name, pe=f_pe, act=f_act, dve=f_dve)

    def conv(ch, tiles, dsts, taps, wcol, bcol=None):
        n = len(tiles)
        last = [0] * n
        for s in range(taps):
            for i in range(n):
                w = wcol(taps - 1 - s, i)
                if s == 0:
                    if bcol is None:
                        ins = nc.vector.tensor_scalar(dsts[i], tiles[i], w, None, ALU.mult)
                    else:
                        ins = nc.vector.tensor_scalar(dsts[i], tiles[i], w, bcol(i), ALU.mult, ALU.add)
                else:
                    ch.after(last[i])
                    ins = nc.vector.scalar_tensor_tensor(dsts[i][:, s:T], tiles[i][:, 0:T - s], w,
                                                         dsts[i][:, s:T], ALU.mult, ALU.add)
                last[i] = ch.mark(ins)
        ch.after(max(last))

    def layer_norm(name, tile, nk, width, g, tmp, finish=None):
        sq, rs = tmp
        total = sig.take("ln_total", 2)
        centered = sig.take("ln_centered", 2 * nk)
        squared = sig.take("ln_squared", 2 * nk)
        summed = sig.take("ln_summed", 2 * nk)
        root = sig.take("ln_root", 2)
        scaled = sig.take("ln_scaled", 2 * nk)

        def f_pe(pe):
            for b in range(2):
                for k in range(nk):
                    mm = nc.tensor.matmul(ps[:, 4 + b, :], ones, tile(k, b), start=(k == 0), stop=(k == nk - 1))
                mm.then_inc(total.sem, 1)
            for b in range(2):
                for k in range(nk):
                    i = b * nk + k
                    pe.wait_ge(squared.sem, squared.nth(i))
                    nc.tensor.matmul(ps[:, 2 + b, :], ones, wt(sq, i % 2), start=(k == 0),
                                     stop=(k == nk - 1)).then_inc(summed.sem, 1)

        def f_act(act):
            for b in range(2):
                for k in range(nk):
                    i = b * nk + k
                    act.wait_ge(centered.sem, centered.nth(i))
                    if i >= 2:
                        act.wait_ge(summed.sem, summed.nth(i - 2))
                    nc.scalar.activation(wt(sq, i % 2), tile(k, b), ACT.Square).then_inc(squared.sem, 1)
                act.wait_ge(summed.sem, summed.nth(b * nk + nk - 1))
                nc.scalar.activation(wt(rs, b), ps[:, 2 + b, :], ACT.Sqrt, bias=EPS,
                                     scale=1.0 / width).then_inc(root.sem, 1)
            if finish:
                for b in range(2):
                    for k in range(nk):
                        act.wait_ge(scaled.sem, scaled.nth(b * nk + k))
                        finish(k, b)

        def f_dve(dve):
            ch = chains["dve"]
            for b in range(2):
                dve.wait_ge(total.sem, total.nth(b))
                for k in range(nk):
                    nc.vector.scalar_tensor_tensor(tile(k, b), ps[:, 4 + b, :], -1.0 / width, tile(k, b),
                                                   ALU.mult, ALU.add).then_inc(centered.sem, 1)
            for b in range(2):
                dve.wait_ge(root.sem, root.nth(b))
                ch.link(nc.vector.reciprocal(wt(rs, b), wt(rs, b)))
                for k in range(nk):
                    nc.vector.scalar_tensor_tensor(tile(k, b), tile(k, b), g(k), wt(rs, b), ALU.mult,
                                                   ALU.mult).then_inc(scaled.sem, 1)
        stage(name, pe=f_pe, act=f_act, dve=f_dve)

    def softplus(name, a, e, z, z2, q):
        s_e = sig.take("softplus_exp", 1)

        def f_act(act):
            ch = chains["act"]
            ch.link(nc.scalar.activation(e, a, ACT.Abs))
            nc.scalar.activation(e, e, ACT.Exp, scale=-1.0).then_inc(s_e.sem, 1)

        def f_dve(dve):
            ch = chains["dve"]
            dve.wait_ge(s_e.sem, s_e.nth(0))
            ch.link(nc.vector.tensor_scalar(z, e, 2.0, None, ALU.add))
            ch.link(nc.vector.reciprocal(z, z))
            ch.link(nc.vector.tensor_tensor(z, e, z, ALU.mult))
            ch.link(nc.vector.tensor_tensor(z2, z, z, ALU.mult))
            ch.link(nc.vector.tensor_scalar(q, z2, 1.0 / 17, None, ALU.mult))
            for c in (15, 13, 11, 9, 7, 5, 3):
                ch.link(nc.vector.scalar_tensor_tensor(q, q, 1.0 / c, z2, ALU.add, ALU.mult))
            ch.link(nc.vector.scalar_tensor_tensor(q, q, 1.0, z, ALU.add, ALU.mult))
            ch.link(nc.vector.tensor_scalar(a, a, 0.0, None, ALU.max))
            ch.link(nc.vector.scalar_tensor_tensor(a, q, 2.0, a, ALU.mult, ALU.add))
        stage(name, act=f_act, dve=f_dve)

    class Unit:
        def __init__(self, scores, bias, pv):
            self.scores, self.bias, self.pv = scores, bias, pv

    def attention(name, steps, width, scale, has_bias, normalize, spt, ptt, pv, take, sinks=None, stats=None):
        N = len(steps)
        nkb = width // P
        scored = sig.take("scored", N)
        maxed = sig.take("score_max", N)
        expd = sig.take("probs_exp", N)
        normd = sig.take("probs_ready", N)
        turned = sig.take("probs_turned", N)
        pt_ready = sig.take("turned_copied", N)
        mixed = sig.take("values_mixed", N)
        taken = sig.take("values_taken", N)
        S = ps[:, 2:4, :].rearrange("p a (u w) -> p (a u) w", w=256)
        PT = ps[:, 4:6, :].rearrange("p a w -> p (a w)").rearrange("p (k u w) -> p k u w", k=2, u=4)
        SB = wt(spt).rearrange("p (u w) -> p u w", u=4)
        PB = wt(ptt).rearrange("p (k u w) -> p k u w", k=2, u=4)
        lo = 256 - width
        mx, nmx, den, rden, esk = (small[:, 256 + 4 * q:260 + 4 * q] for q in range(5))

        def f_pe(pe):
            def scores(n):
                if n >= 1:
                    pe.wait_ge(expd.sem, expd.nth(n - 1))
                for u, unit in enumerate(steps[n]):
                    for c, l, r in unit.scores:
                        mm = nc.tensor.matmul(S[:, u, c], l, r, start=True, stop=True)
                mm.then_inc(scored.sem, 1)
            scores(0)
            for n in range(N):
                if n + 1 < N:
                    scores(n + 1)
                pe.wait_ge(normd.sem, normd.nth(n))
                if n >= 1:
                    pe.wait_ge(pt_ready.sem, pt_ready.nth(n - 1))
                for u in range(4):
                    for kb in range(nkb):
                        mm = nc.tensor.transpose(PT[:, kb, u, :], SB[:, u, lo + kb * P:lo + (kb + 1) * P], ident)
                mm.then_inc(turned.sem, 1)
                pe.wait_ge(pt_ready.sem, pt_ready.nth(n))
                if n >= 2:
                    pe.wait_ge(taken.sem, taken.nth(n - 2))
                mm = pv(pe, n, ps[:, 6 + n % 2, :], PB)
                mm.then_inc(mixed.sem, 1)

        def f_act(act):
            for n in range(N):
                act.wait_ge(maxed.sem, maxed.nth(n))
                for u in range(4):
                    src = SB[:, u, lo:256] if has_bias else S[:, u, lo:256]
                    ins = nc.scalar.activation(SB[:, u, lo:256], src, ACT.Exp, bias=nmx[:, u:u + 1],
                                               scale=1.0 if has_bias else scale, accum_out=den[:, u:u + 1])
                if sinks is not None:
                    nc.scalar.activation(esk, esk, ACT.Exp).then_inc(expd.sem, 1)
                else:
                    ins.then_inc(expd.sem, 1)
                act.wait_ge(turned.sem, turned.nth(n))
                if n >= 1:
                    act.wait_ge(mixed.sem, mixed.nth(n - 1))
                nc.scalar.activation(PB[:, 0:nkb], PT[:, 0:nkb], ACT.Copy).then_inc(pt_ready.sem, 1)

        def f_dve(dve):
            ch = chains["dve"]

            def take_away(n):
                dve.wait_ge(mixed.sem, mixed.nth(n))
                take(n, ps[:, 6 + n % 2, :]).then_inc(taken.sem, 1)
            for n in range(N):
                dve.wait_ge(scored.sem, scored.nth(n))
                if n >= 1:
                    dve.wait_ge(turned.sem, turned.nth(n - 1))
                if has_bias:
                    for u in range(4):
                        ins = nc.vector.scalar_tensor_tensor(SB[:, u, lo:256], S[:, u, lo:256], scale,
                                                             steps[n][u].bias, ALU.mult, ALU.add)
                    ch.link(ins)
                    ch.link(nc.vector.tensor_reduce(mx, SB[:, :, lo:256], AX, ALU.max))
                else:
                    ch.link(nc.vector.tensor_reduce(mx, S[:, :, lo:256], AX, ALU.max))
                if sinks is not None:
                    ch.link(nc.vector.tensor_tensor(mx, mx, sinks(n), ALU.max))
                    ch.link(nc.vector.tensor_tensor(esk, sinks(n), mx, ALU.subtract))
                if stats:
                    ch.link(nc.vector.tensor_copy(stats(n)[0], mx))
                nc.vector.tensor_scalar(nmx, mx, -1.0 if has_bias else -scale, None,
                                        ALU.mult).then_inc(maxed.sem, 1)
                if n >= 1:
                    take_away(n - 1)
                dve.wait_ge(expd.sem, expd.nth(n))
                if not normalize:
                    nc.vector.tensor_copy(stats(n)[1], den).then_inc(normd.sem, 1)
                    continue
                if sinks is not None:
                    ch.link(nc.vector.tensor_tensor(den, den, esk, ALU.add))
                ch.link(nc.vector.reciprocal(rden, den))
                for u in range(4):
                    ins = nc.vector.tensor_scalar(SB[:, u, lo:256], SB[:, u, lo:256], rden[:, u:u + 1],
                                                  None, ALU.mult)
                ins.then_inc(normd.sem, 1)
            take_away(N - 1)
        stage(name, pe=f_pe, act=f_act, dve=f_dve)

    loaded = sig.sem("loaded")
    nloads = [0]

    def load(act, dst, src):
        nloads[0] += 1
        act.dma_start(dst, src).then_inc(loaded, 16)

    def loads_done(act):
        act.wait_ge(loaded, 16 * nloads[0])

    x_tiles = A["x"][0].rearrange("(n p) d -> n p d", p=P)

    def load_inputs(act):
        load(act, cst[:], A["consts"])
        for table, row, k, ap in row_loads:
            dst = wt(0)[row:row + k, table * P:(table + 1) * P]
            if len(ap.shape) == 3:
                dst = dst.rearrange("p (u j) -> p u j", u=2)
            load(act, dst, ap)
        for n in range(T // P):
            load(act, wt(1 + n), x_tiles[n])
        loads_done(act)
    stage("load", act=load_inputs)

    x_turned = sig.take("x_turned", T // P + 1)
    x_copied = sig.take("x_copied", T // P + 1)

    def turn_inputs(pe):
        for j, n in enumerate(TABLE_ROWS):
            mm = nc.tensor.transpose(ps[:, 2, j * P:j * P + n], wt(0)[0:n, j * P:(j + 1) * P], ident[0:n, 0:n])
        mm.then_inc(x_turned.sem, 1)
        for n in range(T // P):
            if n >= 2:
                pe.wait_ge(x_copied.sem, x_copied.nth(n - 2 + 1))
            for d in range(KD):
                mm = nc.tensor.transpose(ps[:, 4 + 2 * (n % 2) + d // 4, (d % 4) * P:(d % 4 + 1) * P],
                                         wt(1 + n)[:, d * P:(d + 1) * P], ident)
            mm.then_inc(x_turned.sem, 1)

    def copy_inputs(dve):
        dve.wait_ge(x_turned.sem, x_turned.nth(0))
        nc.vector.tensor_copy(cols[:, 0:nrows], ps[:, 2, 0:nrows]).then_inc(x_copied.sem, 1)
        for n in range(T // P):
            dve.wait_ge(x_turned.sem, x_turned.nth(n + 1))
            src = ps[:, 4 + 2 * (n % 2):6 + 2 * (n % 2), :].rearrange("p a (d t) -> p (a d) t", t=P)
            nc.vector.tensor_copy(acc[:, :, n * P:(n + 1) * P], src).then_inc(x_copied.sem, 1)
    stage("turn x", pe=turn_inputs, dve=copy_inputs)

    x_stored = sig.sem("x_stored")

    def store_x(act):
        act.dma_start(x_fm.rearrange("k p t -> p k t"), acc[:]).then_inc(x_stored, 16)
    stage("store x", act=store_x)
    norm_acc("norm x", "g_pre")

    w_in = weights("w_in")
    w_br = [A["w_br"][0, n].rearrange("(k p) n -> p k n", p=P) for n in range(5)]

    def merge_run(n, w=None):
        return run(KD, tiles_of(w if w is not None else w_br[n], 0), tiles_of(w_in, C_GATE + n * D), 4, KD)

    def a_tile(j, b=None):
        if j < 8:
            return acc[:, j, :] if b is None else acc_at(j, b)
        return wt(j - 8, b)

    def wait_x(act):
        act.wait_ge(x_stored, 16)
    stage("x stored", act=wait_x)
    project("A project", run(6, *both(w_in, C_AQKV)), a_tile, lambda j: col("b_aqkv", j))
    r_ba = run(1, tiles_of(w_in, C_BA), tiles_of(w_in, C_BA))
    project("A beta alpha", r_ba, lambda j, b: wt(9 + j, b), lambda j: col("b_ba", 0))

    conved = sig.take("a_conved", 12)
    silued = sig.take("a_silued", 12)

    def a_conv(dve):
        ch = chains["dve"]
        for j in range(0, 12, 2):
            if j >= 2:
                dve.wait_ge(silued.sem, silued.nth(j - 1))
            conv(ch, [a_tile(j), a_tile(j + 1)], [wt(4), wt(5)], 4,
                 lambda tap, i, j=j: col("a_conv_w", tap * 12 + j + i))
            nc.vector.engine_nop().then_inc(conved.sem, 1)
            nc.vector.engine_nop().then_inc(conved.sem, 1)

    def a_silu(act):
        for j in range(12):
            act.wait_ge(conved.sem, conved.nth(j | 1))
            nc.scalar.activation(a_tile(j), wt(4 + j % 2), ACT.Silu).then_inc(silued.sem, 1)
    stage("A conv", dve=a_conv, act=a_silu)
    head_norm("A norm q k", a_tile, 8, 1.0, lambda j: P ** -0.5 if j < 4 else 1.0)

    ba = wt(9)[0:8, :]
    r8 = small[0:8, 300:302]

    def ba_rows(act):
        load(act, small[4:8, 300:301], A["a_dt_bias"].rearrange("a h -> h a"))
        load(act, small[4:8, 301:302], A["a_log"].rearrange("a h -> h a"))
        loads_done(act)

    def ba_zero(dve):
        nc.vector.memset(small[0:8, 300:302], 0.0)
    stage("A rows zero", dve=ba_zero)
    stage("A rows", act=ba_rows)

    def ba_sig(act):
        ch = chains["act"]
        nc.scalar.activation(wt(8)[0:8, :], ba, ACT.Sigmoid)
        nc.scalar.activation(r8[:, 1:2], r8[:, 1:2], ACT.Exp)

    def ba_shift(dve):
        nc.vector.tensor_scalar(wt(7)[0:8, :], ba, r8[:, 0:1], None, ALU.add)
    stage("A sigmoid", act=ba_sig, dve=ba_shift)
    softplus("A softplus", wt(7)[0:8, :], wt(4)[0:8, :], wt(5)[0:8, :], wt(6)[0:8, :], wt(10)[0:8, :])

    def ba_decay(dve):
        nc.vector.tensor_scalar(wt(7)[0:8, :], wt(7)[0:8, :], r8[:, 1:2], -1.0, ALU.mult, ALU.mult)
    stage("A decay", dve=ba_decay)

    beta_t = small[:, 0:64].rearrange("p (n h) -> p n h", h=8)
    g_t = small[:, 64:128].rearrange("p (n h) -> p n h", h=8)
    gc_t = small[:, 128:192].rearrange("p (n h) -> p n h", h=8)

    def ba_turn(pe):
        for n in range(8):
            nc.tensor.transpose(ps[:, 2, n * 8:n * 8 + 8], wt(8)[0:8, n * P:(n + 1) * P], ident[0:8, 0:8])
            nc.tensor.transpose(ps[:, 3, n * 8:n * 8 + 8], wt(7)[0:8, n * P:(n + 1) * P], ident[0:8, 0:8])

    def ba_copy(dve):
        nc.vector.tensor_copy(small[:, 0:64], ps[:, 2, 0:64])
        nc.vector.tensor_copy(small[:, 64:128], ps[:, 3, 0:64])

    def ba_sum(pe):
        nc.tensor.matmul(ps[:, 4, 0:64], C("upto"), small[:, 64:128], start=True, stop=True)

    def ba_sum_copy(dve):
        nc.vector.tensor_copy(small[:, 128:192], ps[:, 4, 0:64])
    stage("A turn", pe=ba_turn)
    stage("A turned", dve=ba_copy)
    stage("A running sum", pe=ba_sum)
    stage("A running sum copied", dve=ba_sum_copy)

    def slot(j):
        return wrk[:, 4 + j // 2, (j % 2) * HALF:(j % 2 + 1) * HALF].rearrange("p (h c) -> p h c", h=4)

    LT, AT, BT, ZZ, TT, UU, VB, KBE, KDEC, ATT, ST, EG = (slot(j) for j in range(12))
    dk, eg, nbeg, ekd = (small[:, 200 + 4 * q:204 + 4 * q] for q in range(4))

    def four(b):
        return ps[:, b, :].rearrange("p (h c) -> p h c", h=4)

    def all4(m):
        return m.unsqueeze(1).to_broadcast([P, 4, P])

    gdn_pe = sig.take("gdn_pe", 8 * (2 + 2 * NLEVEL))
    gdn_act = sig.take("gdn_act", 8 * (3 + NLEVEL))
    gdn_dve = sig.take("gdn_dve", 8 * (4 + 2 * NLEVEL))

    def delta_chunk(n):
        c = slice(n * P, (n + 1) * P)
        step_pe = lambda i: (gdn_pe.sem, gdn_pe.nth(n * (2 + 2 * NLEVEL) + i))
        step_act = lambda i: (gdn_act.sem, gdn_act.nth(n * (3 + NLEVEL) + i))
        step_dve = lambda i: (gdn_dve.sem, gdn_dve.nth(n * (4 + 2 * NLEVEL) + i))

        def f_pe(pe):
            def turned(dst, lhsT, rhs):
                for h in range(4):
                    mm = nc.tensor.matmul(four(dst)[:, h, :], lhsT(h), rhs(h), start=True, stop=True)
                return mm
            for h in range(4):
                nc.tensor.transpose(four(2)[:, h, :], acc[:, 4 + h, c], ident)
                nc.tensor.transpose(four(3)[:, h, :], wt(h)[:, c], ident)
            turned(4, lambda h: gc_t[:, n, 4 + h:5 + h].to_broadcast([P, P]), lambda h: ident)
            turned(5, lambda h: beta_t[:, n, h:h + 1].to_broadcast([P, P]), lambda h: ident)
            turned(6, lambda h: acc[:, 4 + h, c], lambda h: acc[:, 4 + h, c])
            turned(7, lambda h: acc[:, 4 + h, c], lambda h: acc[:, h, c]).then_inc(gdn_pe.sem, 1)
            pe.wait_ge(*step_dve(3))
            pe.wait_ge(*step_act(2))
            for h in range(4):
                mm = nc.tensor.transpose(four(2)[:, h, :], BT[:, h, :], ident)
            mm.then_inc(gdn_pe.sem, 1)
            for lv in range(1, NLEVEL):
                pe.wait_ge(*step_dve(2 + 2 * lv))
                pe.wait_ge(*step_dve(3 + 2 * lv))
                turned(2, lambda h: BT[:, h, :], lambda h: TT[:, h, :]).then_inc(gdn_pe.sem, 1)
                pe.wait_ge(*step_act(2 + lv))
                if lv < NLEVEL - 1:
                    turned(3, lambda h: UU[:, h, :], lambda h: ZZ[:, h, :])
                turned(4, lambda h: ZZ[:, h, :], lambda h: UU[:, h, :]).then_inc(gdn_pe.sem, 1)
            L = NLEVEL
            pe.wait_ge(*step_dve(2 + 2 * L))
            turned(6, lambda h: KBE[:, h, :], lambda h: UU[:, h, :]).then_inc(gdn_pe.sem, 1)
            pe.wait_ge(*step_act(2 + L))
            for h in range(4):
                mm = nc.tensor.matmul(four(5)[:, h, :], UU[:, h, :], VB[:, h, :], start=True, stop=(n == 0))
                if n > 0:
                    mm = nc.tensor.matmul(four(5)[:, h, :], ZZ[:, h, :], ST[:, h, :], start=False, stop=True)
            mm.then_inc(gdn_pe.sem, 1)
            pe.wait_ge(*step_dve(3 + 2 * L))
            for h in range(4):
                if n > 0:
                    nc.tensor.matmul(four(7)[:, h, :], ST[:, h, :], acc[:, h, c], start=True, stop=False)
                mm = nc.tensor.matmul(four(7)[:, h, :], TT[:, h, :], ATT[:, h, :], start=(n == 0), stop=True)
            turned(2, lambda h: KDEC[:, h, :], lambda h: TT[:, h, :])

        def f_act(act):
            act.wait_ge(*step_pe(0))
            nc.scalar.activation(EG, four(4), ACT.Exp)
            nc.scalar.activation(eg, gc_t[:, n, 4:8], ACT.Exp).then_inc(gdn_act.sem, 1)
            act.wait_ge(*step_dve(0))
            nc.scalar.activation(ekd, dk, ACT.Exp)
            nc.scalar.activation(LT, LT, ACT.Exp).then_inc(gdn_act.sem, 1)
            act.wait_ge(*step_act(1))
            act.wait_ge(*step_dve(1))
            for h in range(4):
                nc.scalar.activation(VB[:, h, :], four(3)[:, h, :], ACT.Copy, scale=beta_t[:, n, h:h + 1])
                nc.scalar.activation(KBE[:, h, :], four(2)[:, h, :], ACT.Copy, scale=nbeg[:, h:h + 1])
                ins = nc.scalar.activation(KDEC[:, h, :], four(2)[:, h, :], ACT.Copy, scale=ekd[:, h:h + 1])
            ins.then_inc(gdn_act.sem, 1)
            for lv in range(1, NLEVEL):
                act.wait_ge(*step_pe(2 * lv))
                nc.scalar.activation(ZZ, four(2), ACT.Copy).then_inc(gdn_act.sem, 1)
            act.wait_ge(*step_pe(2 * NLEVEL))
            nc.scalar.activation(ZZ, four(6), ACT.Copy).then_inc(gdn_act.sem, 1)

        def f_dve(dve):
            ch = chains["dve"]
            dve.wait_ge(*step_pe(0))
            dve.wait_ge(*step_act(0))
            for h in range(4):
                nc.vector.scalar_tensor_tensor(LT[:, h, :], four(4)[:, h, :], gc_t[:, n, 4 + h:5 + h],
                                               C("negafter"), ALU.subtract, ALU.add)
            nc.vector.tensor_tensor(dk, four(4)[:, :, P - 1], gc_t[:, n, 4:8], ALU.subtract).then_inc(gdn_dve.sem, 1)
            dve.wait_ge(*step_act(0))
            nc.vector.scalar_tensor_tensor(nbeg, eg, -1.0, beta_t[:, n, 0:4], ALU.mult,
                                           ALU.mult).then_inc(gdn_dve.sem, 1)
            ch.link(nc.vector.tensor_tensor(acc[:, 0:4, c], acc[:, 0:4, c], EG, ALU.mult))
            dve.wait_ge(*step_act(1))
            ch.link(nc.vector.tensor_tensor(AT, four(6), LT, ALU.mult))
            ch.link(nc.vector.tensor_tensor(AT, AT, four(5), ALU.mult))
            nc.vector.tensor_tensor(ATT, four(7), LT, ALU.mult).then_inc(gdn_dve.sem, 1)
            nc.vector.tensor_tensor(BT, AT, all4(C("lev0")), ALU.mult).then_inc(gdn_dve.sem, 1)
            dve.wait_ge(*step_dve(3))
            ch.link(nc.vector.tensor_tensor(UU, all4(ident), BT, ALU.subtract))
            dve.wait_ge(*step_pe(1))
            nc.vector.tensor_tensor(TT, all4(ident), four(2), ALU.subtract).then_inc(gdn_dve.sem, 1)
            for lv in range(1, NLEVEL):
                if lv > 1:
                    dve.wait_ge(*step_pe(2 * (lv - 1) + 1))
                nc.vector.tensor_tensor(BT, AT, all4(C(f"lev{lv}")), ALU.mult).then_inc(gdn_dve.sem, 1)
                dve.wait_ge(*step_pe(2 * lv + 1))
                if lv < NLEVEL - 1:
                    nc.vector.tensor_tensor(TT, TT, four(3), ALU.subtract)
                nc.vector.tensor_tensor(UU, UU, four(4), ALU.subtract).then_inc(gdn_dve.sem, 1)
            dve.wait_ge(*step_pe(2 * NLEVEL + 1))
            nc.vector.tensor_copy(TT, four(5)).then_inc(gdn_dve.sem, 1)
        stage(f"A chunk {n}", pe=f_pe, act=f_act, dve=f_dve)

        def s_act(act):
            nc.scalar.activation(acc[:, 0:4, c], four(7), ACT.Copy)

        def s_dve(dve):
            for h in range(4):
                if n == 0:
                    nc.vector.tensor_copy(ST[:, h, :], four(2)[:, h, :])
                else:
                    nc.vector.scalar_tensor_tensor(ST[:, h, :], ST[:, h, :], EG[:, h, P - 1:P],
                                                   four(2)[:, h, :], ALU.mult, ALU.add)
        stage(f"A chunk {n} state", act=s_act, dve=s_dve)

    for n in range(8):
        delta_chunk(n)
    head_norm("A norm out", a_tile, 4, 1.0 / P, lambda j: col("a_norm_g"))
    gate_z("A z", run(2, *both(w_in, C_AZ)), acc_at, lambda j: col("b_az", j), 4, 5)
    merge("A merge", merge_run(0), lambda i: col("b_gate", i), True)

    r_glu = run(4, tiles_of(w_in, C_GLU), tiles_of(w_in, C_GLU + W))
    gdone = sig.take("glu_done", 8)

    def b_pe(pe):
        dense_run(pe, r_glu, rhs_h, rhs_h)

    def b_act(act):
        for i in range(4):
            for p in range(2):
                for b in range(2):
                    out_ready(act, r_glu.t(i, p), b)
                    if p == 1 and i >= 1:
                        act.wait_ge(gdone.sem, gdone.nth(2 * (i - 1) + b))
                    nc.scalar.activation(wt((i, 4)[p], b), ps[:, b, :], (ACT.Identity, ACT.Sigmoid)[p],
                                         bias=col("b_glu", 4 * p + i)).then_inc(dense_free[b], 1)

    def b_dve(dve):
        for i in range(4):
            for b in range(2):
                out_taken(dve, r_glu.t(i, 1), b)
                nc.vector.tensor_tensor(wt(i, b), wt(i, b), wt(4, b), ALU.mult).then_inc(gdone.sem, 1)
    stage("B glu", pe=b_pe, act=b_act, dve=b_dve)

    def b_conv(dve):
        conv(chains["dve"], [wt(i) for i in range(4)], [wt(4 + i) for i in range(4)], 31,
             lambda tap, i: col("b_dw_w", tap * 4 + i), lambda i: col("b_dw_b", i))
    stage("B conv", dve=b_conv)
    layer_norm("B norm", lambda k, b: wt(4 + k, b), 4, W, lambda k: col("b_ln_g", k), (8, 9),
               lambda k, b: nc.scalar.activation(wt(k, b), wt(4 + k, b), ACT.Silu, bias=col("b_ln_b", k)))
    gate_z("B z", run(2, *both(w_in, C_BZ)), wt, lambda j: col("b_bz", j), 4, 5)
    merge("B merge", merge_run(1), lambda i: col("b_gate", 8 + i), False)

    def swapped(w, first):
        v = w[:, :, first:first + W].rearrange("p k (u t j) -> p k u t j", u=2, j=64)
        return lambda i, p: ("columns", [v[:, :, u, 2 * i + p, :] for u in range(2)])
    cq = swapped(w_in, C_CQ)
    cz = swapped(w_in, C_CZ)
    for i in range(2):
        r = run(1, lambda _, i=i: cq(i, 0), lambda _, i=i: cq(i, 1))
        project("C q", r, lambda j, b, i=i: wt(2 * i + j, b), lambda j, i=i: col("b_cq", 2 * i + j))
    project("C k v", run(1, *both(w_in, C_CKV)), lambda j, b: wt((4, 6)[j], b), lambda j: col("b_ckv", j))

    def c_load(act):
        load(act, wt(7)[:, 0:896], A["bias_consts"])
        load(act, wt(8)[0:32, 0:8], A["rel_bias"])
        load(act, small[:, 304:312], A["c_sinks"].to_broadcast([P, 8]) if False else A["c_sinks"][0].partition_broadcast(P))
        loads_done(act)
    stage("C load", act=c_load)

    def c_rows_pe(pe):
        nc.tensor.matmul(ps[0:8, 2, 0:384], wt(8)[0:32, 0:8], wt(7)[0:32, 0:384], start=True, stop=True)
        for n in range(8):
            nc.tensor.transpose(ps[:, 4 + n // 4, (n % 4) * P:(n % 4 + 1) * P], wt(6)[:, n * P:(n + 1) * P], ident)

    def c_rows_dve(dve):
        nc.vector.tensor_tensor(wt(8)[0:8, 128:512], ps[0:8, 2, 0:384], wt(7)[0:8, 384:768], ALU.add)
        nc.vector.tensor_copy(wt(5), ps[:, 4:6, :].rearrange("p a w -> p (a w)"))
    stage("C bias rows", pe=c_rows_pe)
    stage("C bias rows", dve=c_rows_dve)

    def c_skew(act):
        load(act, bias_rows.ap(), wt(8)[0:8, 128:512])
        loads_done(act)
        skew = bass.AP(tensor=bias_rows.ap().tensor, offset=0, ap=[[1, P], [384, 8], [1, 256]])
        load(act, wrk[:, 9:11, :].rearrange("p a (h j) -> p (a h) j", h=4), skew)
        loads_done(act)
    stage("C skew", act=c_skew)

    def c_flip_pe(pe):
        for g in range(4):
            nc.tensor.matmul(ps[:, 4 + g, :], wt(7)[:, 768:896], wt(9 + g // 2, g % 2), start=True, stop=True)

    def c_flip_dve(dve):
        for g in range(4):
            nc.vector.tensor_copy(wt(9 + g // 2, g % 2), ps[:, 4 + g, :])
    stage("C flip", pe=c_flip_pe)
    stage("C flipped", dve=c_flip_dve)

    def c_attention():
        bias = wrk[:, 9:11, :].rearrange("p a (h j) -> p (a h) j", h=4)
        steps, where = [], []
        for n in range(8):
            for K in range(2):
                units = []
                for t in range(4):
                    rows = slice(64 * K, 64 * K + 64)
                    q = wt(t)[rows, n * P:(n + 1) * P]
                    if n == 0:
                        sc = [(slice(0, P), q, wt(4)[rows, 0:P]), (slice(P, 256), q, wt(4)[rows, 0:P])]
                    else:
                        sc = [(slice(0, 256), q, wt(4)[rows, (n - 1) * P:(n + 1) * P])]
                    units.append(Unit(sc, bias[:, 4 * K + t, :], None))
                steps.append(units)
                where.append((n, K))
        return steps, where

    c_steps, c_where = c_attention()
    first_steps, rest_steps = c_steps[:2], c_steps[2:]

    def c_run(name, steps, where, width):
        if width == P:
            for units in steps:
                for u in units:
                    u.scores = [u.scores[1]]
                    u.bias = u.bias[:, P:256]

        def pv(pe, s, dst, PB):
            n, K = where[s]
            rows = slice(64 * K, 64 * K + 64)
            blocks = [n] if width == P else [n - 1, n]
            for kb, blk in enumerate(blocks):
                mm = nc.tensor.matmul(dst[rows, :], wt(5)[:, blk * P + 64 * K:blk * P + 64 * K + 64],
                                      PB[:, kb, :, :], start=(kb == 0), stop=(kb == len(blocks) - 1))
            return mm

        def take(s, src):
            n, K = where[s]
            rows = slice(64 * K, 64 * K + 64)
            return nc.vector.tensor_copy(wrk[rows, 0:4, n * P:(n + 1) * P],
                                         src[rows, :].rearrange("p (h c) -> p h c", h=4))
        attention(name, steps, width, 64 ** -0.5, True, True, 7, 8, pv, take,
                  sinks=lambda s: small[:, 304 + 4 * where[s][1]:308 + 4 * where[s][1]])
    c_run("C attention, first block", first_steps, c_where[:2], P)
    c_run("C attention", rest_steps, c_where[2:], 256)
    for i in range(2):
        r = run(1, lambda _, i=i: cz(i, 0), lambda _, i=i: cz(i, 1))
        gate_z("C z", r, lambda j, b, i=i: wt(2 * i + j, b), lambda j, i=i: col("b_cz", 2 * i + j), 4, 5, 2 * i)
    w_c = A["w_br"][0, 2].rearrange("(u k j) n -> u j k n", u=2, j=64)
    merge_c = run(KD, lambda i: ("rows", [tiles_of(w_c[u], 0)(i) for u in range(2)]),
                  tiles_of(w_in, C_GATE + 2 * D), 4, KD)
    merge("C merge", merge_c, lambda i: col("b_gate", 16 + i), False)

    project("D x", run(2, *both(w_in, C_DX)), to_tiles(0), lambda j: col("b_dx", j))

    def d_zero(dve):
        nc.vector.memset(wrk[:, 9:11, 0:HALF], 0.0)
        nc.vector.tensor_scalar(small[:, 320:324], cols[:, COL["d_lambda"]:COL["d_lambda"] + 4], -1.0, None, ALU.mult)

    def d_load(act):
        for tile, name in ((9, "d_w_a"), (10, "d_w_x")):
            for u in range(2):
                load(act, wt(tile)[64 * u:64 * u + 64, 0:HALF].rearrange("c (t d) -> c t d", t=4)
                     [:, :, 64 * u:64 * u + 64],
                     A[name][0].rearrange("(t u) c d -> u c t d", u=2)[u])
        loads_done(act)
    stage("D zero", dve=d_zero)
    stage("D load", act=d_load)
    softplus("D softplus", small[:, 320:324], small[:, 324:328], small[:, 328:332], small[:, 332:336],
             small[:, 336:340])

    def d_rate(dve):
        nc.vector.tensor_scalar(small[:, 324:328], small[:, 320:324], -8.0, None, ALU.mult)
        nc.vector.tensor_scalar(small[:, 328:332], small[:, 320:324], 8.0, None, ALU.mult)
    stage("D rate", dve=d_rate)

    for i in range(4):
        def dc(dve, i=i):
            conv(chains["dve"], [wt(i)], [wt(4)], 4, lambda tap, _: col("d_conv_w", tap * 4 + i),
                 lambda _: col("d_conv_b", i))
        stage("D conv", dve=dc)

        def dg_pe(pe, i=i):
            for g in range(2):
                for b in range(2):
                    nc.tensor.matmul(ps[:, 2 + 2 * g + b, :], wt(9 + g)[:, i * P:(i + 1) * P], wt(4, b),
                                     start=True, stop=True)
        stage("D gates", pe=dg_pe)

        def dg_act(act, i=i):
            ch = chains["act"]
            flat = lambda b: ps[:, b:b + 2, :].rearrange("p a w -> p (a w)")
            ch.link(nc.scalar.activation(wt(5), flat(2), ACT.Sigmoid, bias=col("d_b_a", i)))
            nc.scalar.activation(wt(6), flat(4), ACT.Sigmoid, bias=col("d_b_x", i))
            nc.scalar.activation(wt(7), wt(5), ACT.Exp, scale=small[:, 324 + i:325 + i])
            nc.scalar.activation(wt(8), wt(5), ACT.Tanh, scale=small[:, 328 + i:329 + i])
        stage("D gate values", act=dg_act)

        def dt_dve(dve, i=i):
            ch = chains["dve"]
            ch.link(nc.vector.tensor_scalar(wt(5), wt(8), 1.0, None, ALU.add))
            ch.link(nc.vector.reciprocal(wt(5), wt(5)))
            nc.vector.scalar_tensor_tensor(wt(8), wt(8), 2.0, wt(5), ALU.mult, ALU.mult)
            nc.vector.tensor_tensor(wt(6), wt(6), wt(4), ALU.mult)
        stage("D input factor", dve=dt_dve)

        def dr_act(act):
            nc.scalar.activation(wt(8), wt(8), ACT.Sqrt)
        stage("D root", act=dr_act)

        def ds_dve(dve, i=i):
            ch = chains["dve"]
            ch.link(nc.vector.tensor_tensor(wt(6), wt(6), wt(8), ALU.mult))
            nc.vector.tensor_tensor_scan(wt(i), wt(7), wt(6), 0.0, ALU.mult, ALU.add)
        stage("D scan", dve=ds_dve)
    gate_z("D z", run(2, *both(w_in, C_DZ)), wt, lambda j: col("b_dz", j), 4, 5)
    merge("D merge", merge_run(3), lambda i: col("b_gate", 24 + i), False)

    def memory_attention(tag, mem, g, w_kv, w_q, first, bias):
        def m_load(act):
            for j in range(2):
                load(act, wt(4 + j), mem[0].rearrange("(n p) d -> n p d", p=P)[j])
            loads_done(act)
        stage(tag + " memory", act=m_load)
        mem_t = wrk[:, 6:8, :].rearrange("p a (k m) -> p (a k) m", m=MEM)

        def m_turn(pe):
            for j in range(2):
                for k in range(KD):
                    nc.tensor.transpose(ps[:, 2 + k // 2, (k % 2) * MEM + j * P:(k % 2) * MEM + (j + 1) * P],
                                        wt(4 + j)[:, k * P:(k + 1) * P], ident)

        def m_copy(dve):
            nc.vector.tensor_copy(wrk[:, 6:8, :].rearrange("p a (b m) -> p (a b) m", m=HALF), ps[:, 2:6, :])
        stage(tag + " memory turned", pe=m_turn)
        stage(tag + " memory copied", dve=m_copy)
        src = lambda k, b: mem_t[:, k, b * P:(b + 1) * P]
        norm(tag + " memory norm", src, P, None, split_emit(
            src, lambda k: col(g, k), lambda k, b: mem_view(y_hi)[:, k, b * P:(b + 1) * P],
            lambda k, b: mem_view(y_lo)[:, k, b * P:(b + 1) * P], P))
        kv = wrk[:, 8:10, :].rearrange("p a (h m) -> p (a h) m", m=MEM)
        project(tag + " k v", run(4, *both(w_kv, 0)), lambda j, b: kv[:, j, b * P:(b + 1) * P],
                rhs=rhs_mem, n=P)
        v_t = wt(10).rearrange("p (m c) -> p m c", m=2)

        def v_turn(pe):
            for h in range(4):
                for m in range(2):
                    nc.tensor.transpose(ps[:, 2 + m, h * P:(h + 1) * P], kv[:, 4 + h, m * P:(m + 1) * P], ident)

        def v_copy(dve):
            nc.vector.tensor_copy(v_t, ps[:, 2:4, :])
        stage(tag + " v turned", pe=v_turn)
        stage(tag + " v copied", dve=v_copy)
        project(tag + " q", run(2, *both(w_q, first)), to_tiles(0), bias)
        steps = [[Unit([(slice(0, 256), wt(h)[:, (4 * s4 + u) * P:(4 * s4 + u + 1) * P], kv[:, h, :])], None, None)
                  for u in range(4)] for h in range(4) for s4 in range(2)]

        def pv(pe, s, dst, PB):
            h = s // 2
            for kb in range(2):
                mm = nc.tensor.matmul(dst, v_t[:, kb, h * P:(h + 1) * P], PB[:, kb, :, :],
                                      start=(kb == 0), stop=(kb == 1))
            return mm

        def take(s, src):
            return nc.vector.tensor_copy(wt(s // 2, s % 2), src)
        attention(tag + " attention", steps, 256, P ** -0.5, False, True, 4, 5, pv, take)

    memory_attention("E", A["mem"], "g_mem", weights("w_mem_kv"), w_in, C_EQ, lambda j: col("b_eq", j))
    gate_z("E z", run(2, *both(w_in, C_EZ)), wt, lambda j: col("b_ez", j), 4, 5)
    merge("E merge", merge_run(4), lambda i: col("b_gate", 32 + i), False)

    def part_acc(dve):
        ch = chains["dve"]
        for k in range(KD):
            ch.link(nc.vector.tensor_copy(h_hi[:, k, :], acc[:, k, :]))
            nc.vector.tensor_tensor(h_lo[:, k, :], acc[:, k, :], h_hi[:, k, :].bitcast(F32), ALU.subtract)
    stage("merged, in parts", dve=part_acc)
    project("first block out", run(4, *both(weights("w_out"), 0)), acc_at)

    def x_back(act):
        load(act, wrk[:, 3:11, :], x_fm.rearrange("k p t -> p k t"))
        loads_done(act)
    stage("x back", act=x_back)

    def post(ch, k, b, root):
        y = acc_at(k, b)
        ch.link(nc.vector.scalar_tensor_tensor(y, y, col("g_post", k), root, ALU.mult, ALU.mult))
        ch.link(nc.vector.tensor_tensor(y, y, wt(3 + k, b), ALU.add))
    norm("post norm", acc_at, HALF, None, post)

    norm_acc("even norm", "even_norm_g_2")
    w2 = weights("even_w_in_2")
    w2o = A["even_w_out_2"][0].rearrange("(b k p) n -> b p k n", b=3, p=P)
    w2kv = weights("even_w_mem_kv_2")

    def r_load(act):
        load(act, wt(0).bitcast(I32)[0:32, :], A["positions_2"][0].partition_broadcast(32))
        loads_done(act)

    TWO_PI_1, TWO_PI_2, TWO_PI_3 = 6.28125, 1.9350051879882812e-03, 3.0199159819210e-07
    ri = wt(1).bitcast(I32)[0:32, :]

    def r_dve(dve):
        ch = chains["dve"]
        a, n, m = wt(2)[0:32, :], wt(3)[0:32, :], wt(4)[0:32, :]
        ch.link(nc.vector.tensor_copy(a, wt(0).bitcast(I32)[0:32, :]))
        ch.link(nc.vector.tensor_scalar(a, a, C("rope")[0:32, 0:1], None, ALU.mult))
        for dst, quarter in ((10, 0.0), (9, 0.25)):
            d = wt(dst)[0:32, :]
            ch.link(nc.vector.tensor_scalar(n, a, 0.15915494309189535, quarter, ALU.mult, ALU.add))
            ch.link(nc.vector.tensor_copy(ri, n))
            ch.link(nc.vector.tensor_copy(n, ri))
            ch.link(nc.vector.scalar_tensor_tensor(d, n, -TWO_PI_1, a, ALU.mult, ALU.add))
            ch.link(nc.vector.scalar_tensor_tensor(d, n, -TWO_PI_2, d, ALU.mult, ALU.add))
            ch.link(nc.vector.scalar_tensor_tensor(d, n, -TWO_PI_3, d, ALU.mult, ALU.add))
            ch.link(nc.vector.tensor_scalar(d, d, quarter * 6.283185307179586, None, ALU.add))
            for bound, op in ((3.14159265, ALU.is_gt), (-3.14159265, ALU.is_lt)):
                ch.link(nc.vector.tensor_scalar(m, d, bound, -6.283185307179586 if bound > 0 else
                                                6.283185307179586, op, ALU.mult))
                ch.link(nc.vector.tensor_tensor(d, d, m, ALU.add))
            ch.link(nc.vector.tensor_scalar(d, d, 3.1415925, -3.1415925, ALU.min, ALU.max))

    def r_sin(act):
        nc.scalar.activation(wt(10)[0:32, :], wt(10)[0:32, :], ACT.Sin)
        nc.scalar.activation(wt(9)[0:32, :], wt(9)[0:32, :], ACT.Sin)

    def r_sign(dve):
        nc.vector.tensor_scalar(wt(10)[0:32, :], wt(10)[0:32, :], C("rope")[0:32, 1:2], None, ALU.mult)
    stage("positions", act=r_load)
    stage("angles", dve=r_dve)
    stage("sines", act=r_sin)
    stage("signed sine", dve=r_sign)

    def rope(tiles):
        def f_pe(pe):
            for j, t in enumerate(tiles):
                for b in range(2):
                    nc.tensor.matmul(ps[0:32, 2 + 2 * j + b, :], C("perm")[0:32, :], wt(t, b)[0:32, :],
                                     start=True, stop=True)

        def f_dve(dve):
            ch = chains["dve"]
            for j, t in enumerate(tiles):
                sw = ps[0:32, 2 + 2 * j:4 + 2 * j, :].rearrange("p a w -> p (a w)")
                x, tmp = wt(t)[0:32, :], wt(7 + j)[0:32, :]
                ch.link(nc.vector.tensor_tensor(tmp, sw, wt(10)[0:32, :], ALU.mult))
                ch.link(nc.vector.tensor_tensor(x, x, wt(9)[0:32, :], ALU.mult))
                nc.vector.tensor_tensor(x, x, tmp, ALU.add)
        stage("rope swap", pe=f_pe)
        stage("rope", dve=f_dve)

    st_m = small[:, 0:24].rearrange("p (g u) -> p g u", g=3)
    st_d = small[:, 24:48].rearrange("p (g u) -> p g u", g=3)

    def dilated_head(h):
        cq2 = lambda g: g * 2 * W + h * P
        ck2 = lambda g: g * 2 * W + W + h * P
        one = lambda c: tiles_of(w2, c)
        r_a = run(1, one(C2_V + h * P), one(cq2(0)))
        r_b = run(1, one(ck2(0)), one(cq2(1)))
        r_c = run(1, one(ck2(1)), one(cq2(2)))
        r_d = run(1, one(ck2(2)), one(C2_Z + h * P))
        project("v q0", r_a, lambda j, b: wt((4, 0)[j], b))
        project("k0 q1", r_b, lambda j, b: wt((3, 1)[j], b))
        rope([0, 3])
        dilated_group(h, 0)
        project("k1 q2", r_c, lambda j, b: wt((3, 2)[j], b))
        rope([1, 3])
        dilated_group(h, 1)

        def f_pe(pe):
            dense_run(pe, r_d, rhs_h, rhs_h)

        def f_act(act):
            for b in range(2):
                out_ready(act, r_d.t0, b)
                nc.scalar.activation(wt(3, b), ps[:, b, :], ACT.Copy).then_inc(dense_free[b], 1)
            for b in range(2):
                out_ready(act, r_d.t0 + 1, b)
                nc.scalar.activation(wt(6, b), ps[:, b, :], ACT.Silu).then_inc(dense_free[b], 1)
        stage("k2 z", pe=f_pe, act=f_act)
        rope([2, 3])
        dilated_group(h, 2)
        dilated_join(h)

    def token_view(ap, g):
        if g == 0:
            return ap.rearrange("p (u i) -> p u i", i=P)
        if g == 1:
            return ap.rearrange("p (n i r) -> p r n i", n=2, r=4)
        return ap.rearrange("p (i r) -> p r i", r=16)

    def queries(t, g, u):
        v = token_view(wt(t), g)
        if g == 0:
            return v[:, u, :]
        if g == 1:
            return v[:, u // 2, u % 2, :]
        return v[:, 2 * u:2 * u + 2, :]

    def dilated_group(h, g):
        def vt_pe(pe):
            for u in range(8):
                src = queries(4, g, u)
                if g == 2:
                    src = wt(7)[:, u * P:(u + 1) * P]
                nc.tensor.transpose(ps[:, 2 + u // 4, (u % 4) * P:(u % 4 + 1) * P], src, ident)

        def vt_dve(dve):
            nc.vector.tensor_copy(wt(5), ps[:, 2:4, :].rearrange("p a w -> p (a w)"))
        if g == 2:
            def regroup(dve):
                ch = chains["dve"]
                for t in (4, 2, 3):
                    ch.link(nc.vector.tensor_copy(wt(7).rearrange("p (r i) -> p r i", r=16), token_view(wt(t), 2)))
                    if t != 4:
                        ch.link(nc.vector.tensor_copy(wt(t), wt(7)))
            def regroup2(dve):
                ch = chains["dve"]
                for t in (2, 3):
                    ch.link(nc.vector.tensor_copy(wt(7).rearrange("p (r i) -> p r i", r=16), token_view(wt(t), 2)))
                    ch.link(nc.vector.tensor_copy(wt(t), wt(7)))
                ch.link(nc.vector.tensor_copy(wt(7).rearrange("p (r i) -> p r i", r=16), token_view(wt(4), 2)))
            stage("by residue", dve=regroup2)
        stage("v turned", pe=vt_pe)
        stage("v copied", dve=vt_dve)
        steps = []
        for s in range(2):
            units = []
            for u in range(4 * s, 4 * s + 4):
                if g == 2:
                    q, k = (wt(t)[:, u * P:(u + 1) * P] for t in (2, 3))
                    units.append(Unit([(slice(P, 256), q, k)], C("pair"), None))
                    continue
                q = queries(g, g, u)
                first = u == 0 if g == 0 else u % 2 == 0
                if first:
                    k = queries(3, g, u)
                    sc = [(slice(0, P), q, k), (slice(P, 256), q, k)]
                else:
                    sc = [(slice(0, P), q, queries(3, g, u - 1)), (slice(P, 256), q, queries(3, g, u))]
                units.append(Unit(sc, C("bandfirst") if first else C("band"), None))
            steps.append(units)
        width = P if g == 2 else 256

        def pv(pe, s, dst, PB):
            for u4 in range(4):
                u = 4 * s + u4
                first = u == 0 if g == 0 else u % 2 == 0
                blocks = [u] if g == 2 else [u if first else u - 1, u]
                for kb, blk in enumerate(blocks):
                    mm = nc.tensor.matmul(dst[:, u4 * P:(u4 + 1) * P], wt(5)[:, blk * P:(blk + 1) * P],
                                          PB[:, kb, u4, :], start=(kb == 0), stop=(kb == len(blocks) - 1))
            return mm

        def take(s, src):
            if g == 0:
                return nc.vector.tensor_copy(wt(0, s), src)
            if g == 1:
                return nc.vector.tensor_copy(token_view(wt(1), 1)[:, 2 * s:2 * s + 2],
                                             src.rearrange("p (r n i) -> p r n i", r=2, n=2))
            return nc.vector.tensor_copy(wt(2, s), src)
        attention(f"dilated {g}", steps, width, P ** -0.5, True, False, 7, 8, pv, take,
                  stats=lambda s: (st_m[:, g, 4 * s:4 * s + 4], st_d[:, g, 4 * s:4 * s + 4]))

    def spread(which, g):
        for u in range(8):
            nc.tensor.matmul(ps[:, 2 + 2 * g + u // 4, (u % 4) * P:(u % 4 + 1) * P],
                             which[:, g, u:u + 1].to_broadcast([P, P]), ident, start=True, stop=True)

    def dilated_join(h):
        def m_pe(pe):
            for g in range(3):
                spread(st_m, g)

        def grouped(g):
            flat = ps[:, 2 + 2 * g:4 + 2 * g, :].rearrange("p a w -> p (a w)")
            if g == 0:
                return flat
            if g == 1:
                return flat.rearrange("p (r n i) -> p r n i", r=4, n=2)
            return flat.rearrange("p (r i) -> p r i", r=16)

        def tok(t, g):
            return wt(t) if g == 0 else token_view(wt(t), g)

        def parts(g):
            if g == 1:
                return [(lambda ap, n=n: ap[:, :, n, :]) for n in range(2)]
            return [lambda ap: ap]

        def m_dve(dve):
            ch = chains["dve"]
            for g in range(3):
                for cut in parts(g):
                    ch.link(nc.vector.tensor_copy(cut(tok((3, 4, 5)[g], g)), cut(grouped(g))))
            ch.link(nc.vector.tensor_tensor(wt(7), wt(3), wt(4), ALU.max))
            ch.link(nc.vector.tensor_tensor(wt(7), wt(7), wt(5), ALU.max))
            for t in (3, 4, 5):
                ch.link(nc.vector.tensor_tensor(wt(t), wt(t), wt(7), ALU.subtract))
            ch.link(nc.vector.tensor_copy(wt(8), wt(2)))
            ch.link(nc.vector.tensor_copy(token_view(wt(2), 2), wt(8).rearrange("p (r i) -> p r i", r=16)))

        def w_act(act):
            for t in (3, 4, 5):
                nc.scalar.activation(wt(t), wt(t), ACT.Exp)

        def d_pe(pe):
            for g in range(3):
                spread(st_d, g)

        def d_dve(dve):
            ch = chains["dve"]
            for g in range(3):
                t = (7, 8, 8)[g]
                for cut in parts(g):
                    ch.link(nc.vector.tensor_tensor(cut(tok(t, g)), cut(grouped(g)), cut(tok((3, 4, 5)[g], g)), ALU.mult))
                if g:
                    ch.link(nc.vector.tensor_tensor(wt(7), wt(7), wt(8), ALU.add))
            ch.link(nc.vector.reciprocal(wt(7), wt(7)))
            ch.link(nc.vector.tensor_tensor(wt(7), wt(7), wt(6), ALU.mult))
            for g in range(3):
                ch.link(nc.vector.tensor_tensor(wt(g), wt(g), wt(3 + g), ALU.mult))
            ch.link(nc.vector.tensor_tensor(wt(0), wt(0), wt(1), ALU.add))
            ch.link(nc.vector.tensor_tensor(wt(0), wt(0), wt(2), ALU.add))
            ch.link(nc.vector.tensor_tensor(wt(0), wt(0), wt(7), ALU.mult))
            ch.link(nc.vector.tensor_copy(y_hi[:, h, :], wt(0)))
            nc.vector.tensor_tensor(y_lo[:, h, :], wt(0), y_hi[:, h, :].bitcast(F32), ALU.subtract)
        stage("maxima spread", pe=m_pe)
        stage("joint maximum", dve=m_dve)
        stage("group weights", act=w_act, pe=d_pe)
        stage("join", dve=d_dve)

    for h in range(4):
        dilated_head(h)
    add_out("even out A", run(4, *both(w2o[0], 0), 4, 4))

    project("pool x", run(2, *both(w2, C2_X)), to_tiles(0))

    def p_load(act):
        load(act, wt(10)[:, 0:HALF].rearrange("p (g d) -> p g d", g=4),
             A["even_w_pool_2"][0].rearrange("g c d -> c g d"))
        loads_done(act)

    def p_dve(dve):
        ch = chains["dve"]
        for i in range(4):
            src, s = wt(i), 1
            for lv in range(i + 1):
                dst = wt(5 + (lv % 2))
                ch.link(nc.vector.tensor_copy(dst[:, 0:s], src[:, 0:s]))
                ch.link(nc.vector.tensor_tensor(dst[:, s:T], src[:, s:T], src[:, 0:T - s], ALU.add))
                src, s = dst, 2 * s
            ch.link(nc.vector.tensor_tensor(small[:, 64:80], src[:, 0:16], C("icount")[:, 16 * i:16 * i + 16], ALU.mult))
            ch.link(nc.vector.tensor_tensor(small[:, 64:80], small[:, 64:80], wt(i)[:, 0:16], ALU.subtract))
            ch.link(nc.vector.scalar_tensor_tensor(wt(i), src, 1.0 / s, wt(i), ALU.mult, ALU.subtract))
            ch.link(nc.vector.tensor_copy(wt(i)[:, 0:16], small[:, 64:80]))
    stage("pool sums", act=p_load, dve=p_dve)
    pooled = sig.take("pool_out", 8)
    ptaken = sig.take("pool_taken", 8)

    def p_pe(pe):
        for i in range(8):
            if i >= 4:
                pe.wait_ge(ptaken.sem, ptaken.nth(i - 4))
            nc.tensor.matmul(ps[:, 2 + i % 4, :], wt(10)[:, (i // 2) * P:(i // 2 + 1) * P], wt(i // 2, i % 2),
                             start=True, stop=True).then_inc(pooled.sem, 1)

    def p_act(act):
        for i in range(8):
            act.wait_ge(pooled.sem, pooled.nth(i))
            nc.scalar.activation(wt(i // 2, i % 2), ps[:, 2 + i % 4, :], ACT.Copy,
                                 scale=col("even_pool_scale_2", i // 2)).then_inc(ptaken.sem, 1)
    stage("pool mix", pe=p_pe, act=p_act)
    gate_z("pool z", run(2, *both(w2, C2_Z + W)), wt, None, 4, 5)
    add_out("even out B", run(4, *both(w2o[1], 0), 4, 4))

    memory_attention("even", A["mem_2"], "g_mem_2", w2kv, w2, C2_Q, None)
    gate_z("even memory z", run(2, *both(w2, C2_Z + 2 * W)), wt, None, 4, 5)
    add_out("even out M", run(4, *both(w2o[2], 0), 4, 4))

    norm_acc("odd norm", "odd_norm_g_2")
    w3 = weights("odd_w_in_2")
    w3o = A["odd_w_out_2"][0].rearrange("(b k p) n -> b p k n", b=3, p=P)
    project("odd v", run(4, *both(w3, C3_V)), to_tiles(0))
    layer_norm("odd ln", lambda k, b: wt(k, b), KD, D, lambda k: col("odd_ln_g_2", k), (8, 9),
               lambda k, b: nc.scalar.activation(wt(k, b), wt(k, b), ACT.Identity, bias=col("odd_ln_b_2", k)))

    def s_load(act):
        load(act, wt(8).rearrange("p (g s) -> p g s", g=8), A["odd_w_s_2"][0].rearrange("g t s -> t g s"))
        load(act, wt(10).rearrange("p (g s) -> p g s", g=8), A["odd_b_s_2"][0].partition_broadcast(P))
        loads_done(act)

    def s_pe(pe):
        for g in range(8):
            nc.tensor.transpose(ps[:, 2 + g // 4, (g % 4) * P:(g % 4 + 1) * P], wt(8)[:, g * P:(g + 1) * P], ident)

    def s_dve(dve):
        nc.vector.tensor_tensor(wt(9).rearrange("p (g t) -> p g t", g=8),
                                ps[:, 2:4, :].rearrange("p a (g t) -> p (a g) t", g=4),
                                C("upto").unsqueeze(1).to_broadcast([P, 8, P]), ALU.mult)
    stage("mix load", act=s_load)
    stage("mix turned", pe=s_pe)
    stage("mix masked", dve=s_dve)

    vturned = sig.take("sg_turned", 8)
    vcopied = sig.take("sg_copied", 8)
    smixed = sig.take("sg_mixed", 8)
    sadded = sig.take("sg_added", 8)

    def g_pe(pe):
        for g in range(8):
            if g >= 1:
                pe.wait_ge(vcopied.sem, vcopied.nth(g - 1))
            for n in range(8):
                mm = nc.tensor.transpose(ps[:, 2 + n // 4, (n % 4) * P:(n % 4 + 1) * P], wt(g)[:, n * P:(n + 1) * P], ident)
            mm.then_inc(vturned.sem, 1)
            pe.wait_ge(vcopied.sem, vcopied.nth(g))
            if g >= 1:
                pe.wait_ge(sadded.sem, sadded.nth(g - 1))
            for n in range(8):
                mm = nc.tensor.matmul(ps[:, 4 + n // 4, (n % 4) * P:(n % 4 + 1) * P], wt(8)[:, n * P:(n + 1) * P],
                                      wt(9)[:, g * P:(g + 1) * P], start=True, stop=True)
            mm.then_inc(smixed.sem, 1)

    def g_act(act):
        for g in range(8):
            act.wait_ge(vturned.sem, vturned.nth(g))
            if g >= 1:
                act.wait_ge(smixed.sem, smixed.nth(g - 1))
            nc.scalar.activation(wt(8), ps[:, 2:4, :].rearrange("p a w -> p (a w)"), ACT.Copy).then_inc(vcopied.sem, 1)

    def g_dve(dve):
        for g in range(8):
            dve.wait_ge(smixed.sem, smixed.nth(g))
            nc.vector.tensor_tensor(wt(g).rearrange("p (n t) -> p n t", n=8),
                                    ps[:, 4:6, :].rearrange("p a (n t) -> p (a n) t", n=4),
                                    wt(10)[:, g * P:(g + 1) * P].unsqueeze(1).to_broadcast([P, 8, P]),
                                    ALU.add).then_inc(sadded.sem, 1)
    stage("mix", pe=g_pe, act=g_act, dve=g_dve)

    r_u = run(4, *both(w3, C3_U))

    def u_pe(pe):
        dense_run(pe, r_u, rhs_h, rhs_h)

    def u_dve(dve):
        for j in range(8):
            for b in range(2):
                out_ready(dve, r_u.t0 + j, b)
                nc.vector.tensor_tensor(wt(j, b), wt(j, b), ps[:, b, :], ALU.mult).then_inc(dense_free[b], 1)
    stage("odd u", pe=u_pe, dve=u_dve)
    for part in range(2):
        gate_z("odd z", run(2, *both(w3, C3_Z + part * W)), lambda j, b, part=part: wt(4 * part + j, b), None, 8, 9)
        add_out("odd out", run(4, *both(w3o[part], 0), 4, 4))
    memory_attention("odd", A["mem_2"], "g_mem_2", weights("odd_w_mem_kv_2"), w3, C3_Q, None)
    gate_z("odd memory z", run(2, *both(w3, C3_Z + 2 * W)), wt, None, 4, 5)
    add_out("odd out M", run(4, *both(w3o[2], 0), 4, 4))

    def last(ch, k, b, root):
        y = acc_at(k, b)
        ch.link(nc.vector.scalar_tensor_tensor(y, y, col("final_norm_g_2", k), root, ALU.mult, ALU.mult))
    norm("final norm", acc_at, HALF, None, last, sq=8, rs=9)
    oturned = sig.take("out_turned", KD)
    ocopied = sig.take("out_copied", KD)

    def o_pe(pe):
        for k in range(KD):
            if k >= 2:
                pe.wait_ge(ocopied.sem, ocopied.nth(k - 2))
            for n in range(8):
                mm = nc.tensor.transpose(ps[:, 2 + 2 * (k % 2) + n // 4, (n % 4) * P:(n % 4 + 1) * P],
                                         acc[:, k, n * P:(n + 1) * P], ident)
            mm.then_inc(oturned.sem, 1)

    def o_dve(dve):
        for k in range(KD):
            dve.wait_ge(oturned.sem, oturned.nth(k))
            b = 2 + 2 * (k % 2)
            nc.vector.tensor_copy(wrk[:, 0:8, k * P:(k + 1) * P],
                                  ps[:, b:b + 2, :].rearrange("p a (n d) -> p (a n) d", n=4)).then_inc(ocopied.sem, 1)
    stage("out turned", pe=o_pe, dve=o_dve)

    def o_store(act):
        load(act, out[0].rearrange("(n p) d -> p n d", p=P), wrk[:, 0:8, :])
        loads_done(act)
    stage("out", act=o_store)

    assert ntiles % 2 == 0

    def play(name, eng):
        chains[name] = Chain(eng, f"{name}_chain")
        for n, (_, fns) in enumerate(stages):
            if name in fns:
                fns[name](eng)
            eng.drain().then_inc(at_end[name], 1)
            for other in engines:
                if other != name:
                    eng.wait_ge(at_end[other], n + 1)

    block = ctx.enter_context(nc.Block())

    @block.sync
    def _(sp):
        def load_tile(slot_, nk, src):
            if not isinstance(src, tuple):
                sp.dma_start(w_raw[:, slot_, 0:nk, :], src).then_inc(raw_loaded[slot_], 32)
                return
            kind, pieces = src
            for u, piece in enumerate(pieces):
                dst = w_raw[:, slot_, 0:nk, 64 * u:64 * u + 64] if kind == "columns" else \
                    w_raw[64 * u:64 * u + 64, slot_, 0:nk, :]
                sp.dma_start(dst, piece).then_inc(raw_loaded[slot_], 16)

        for r in runs:
            def body(i, r=r):
                for p in range(2):
                    t = r.t(i, p)
                    if not isinstance(t, int) or t >= 2:
                        sp.wait_ge(tiles_split, t - 1)
                    load_tile((r.t0 + p) % 2, r.nk[p], r.src[p](i))
            if r.pairs == 1:
                body(0)
            elif r.t0 == 0:
                body(0)
                with sp.Fori(1, r.pairs, 1) as i:
                    body(i)
            else:
                with sp.Fori(0, r.pairs, 1) as i:
                    body(i)

    @block.gpsimd
    def _(pool):
        def split(t, s, raw_count):
            pool.wait_ge(raw_loaded[s], raw_count)
            nc.gpsimd.tensor_tensor(w_hi[:, s], w_raw[:, s], one, ALU.mult).then_inc(hi_ready, 1)
            pool.wait_ge(hi_ready, t + 2)
            nc.gpsimd.tensor_tensor(w_lo[:, s], w_raw[:, s], w_hi[:, s].bitcast(F32),
                                    ALU.subtract).then_inc(tiles_split, 1)
        hi_ready = sig.sem("hi_ready")
        nc.gpsimd.memset(pool_one[:], 1.0).then_inc(hi_ready, 1)
        pool.wait_ge(hi_ready, 1)
        one = pool_one[:].unsqueeze(2).to_broadcast([P, KD, P])
        for s in range(2):
            split(s, s, 32)
        with pool.Fori(1, ntiles // 2, 1) as i:
            for s in range(2):
                pool.wait_ge(dense_out, 2 * (2 * i + s) - 2)
                split(2 * i + s, s, 32 * i + 32)

    @block.scalar
    def _(act):
        play("act", act)

    @block.vector
    def _(dve):
        for b in range(2):
            nc.vector.engine_nop().then_inc(dense_free[b], 1)
        play("dve", dve)

    @block.tensor
    def _(pe):
        play("pe", pe)


_OUT = (1, T, D)


def kernel(**inputs):
    import concourse.bacc as _bacc
    from concourse.bass_utils import run_bass_kernel_spmd as _run

    nc = _bacc.Bacc("TRN2", target_bir_lowering=False, num_devices=1)
    arrays = {k: np.ascontiguousarray(v) for k, v in inputs.items()}
    arrays["consts"] = np.ascontiguousarray(constants()[0])
    arrays["bias_consts"] = bias_parts()
    A = {k: nc.dram_tensor(f"in_{k}", v.shape, mybir.dt.from_np(v.dtype), kind="ExternalInput").ap()
         for k, v in arrays.items()}
    out = nc.dram_tensor("out", _OUT, F32, kind="ExternalOutput").ap()
    hybrid_program(nc, A, out)
    r = _run(nc, [{f"in_{k}": v for k, v in arrays.items()}], core_ids=[0])
    return r.results[0]["out"]
```

```python
from contextlib import ExitStack

import numpy as np
import concourse.bass as bass
from concourse import mybir

F32 = mybir.dt.float32
F32R = mybir.dt.float32r
I32 = mybir.dt.int32
ACT = mybir.ActivationFunctionType
ALU = mybir.AluOpType
AX = mybir.AxisListType.X

P = 128
T = 1024
D = 1024
KD = D // P
HALF = 512
W = 512
MEM = 256
NEG = -1.0e30
EPS = 1e-6

C_AQKV, C_AZ, C_BA = 0, 1536, 2048
C_GLU, C_BZ = 2056, 3080
C_CQ, C_CKV, C_CZ = 3592, 4104, 4360
C_DX, C_DZ, C_EQ, C_EZ, C_GATE = 4872, 5384, 5896, 6408, 6920
C2_V, C2_X, C2_Q, C2_Z = 3072, 3584, 4096, 4608
C3_U, C3_V, C3_Q, C3_Z = 0, 1024, 2048, 2560

REL_BUCKETS, REL_MAX_DIST, WINDOW = 32, 128, 128
NLEVEL = 7
CHUNK_TIME = 84.0


def bucket_of(dist):
    n = np.maximum(dist, 0)
    exact = REL_BUCKETS // 2
    large = exact + (np.log(np.maximum(n, 1) / exact) / np.log(REL_MAX_DIST / exact)
                     * (REL_BUCKETS - exact)).astype(np.int32)
    return np.where(n < exact, n, np.minimum(large, REL_BUCKETS - 1))


def constant_parts():
    i = np.arange(P)[:, None]
    j = np.arange(P)[None, :]
    c = {}
    c["ident"] = (i == j)
    c["ones"] = np.ones((P, P))
    c["upto"] = (i <= j)
    c["negafter"] = np.where(i > j, NEG, 0.0)
    for lv in range(NLEVEL):
        s = 1 << lv
        c[f"lev{lv}"] = ((i // (2 * s)) == (j // (2 * s))) & ((i // s) % 2 == 0) & ((j // s) % 2 == 1)
    k2 = np.arange(2 * P)[None, :]
    ok = (k2 >= i) & (k2 <= i + P)
    c["band"] = np.where(ok, 0.0, NEG)
    c["bandfirst"] = np.where(ok & (k2 >= P), 0.0, NEG)
    c["pair"] = np.where(((i // 64) == (j // 64)) & (j <= i), 0.0, NEG)
    perm = np.zeros((P, 32))
    for m in range(32):
        perm[(m + 16) % 32, m] = 1.0
    c["perm"] = perm
    inv = np.zeros((P, 2))
    inv[:32, 0] = np.tile(500000.0 ** (-np.arange(0, 32, 2, dtype=np.float32) / np.float32(32)), 2)
    inv[:32, 1] = np.where(np.arange(32) < 16, -1.0, 1.0)
    c["rope"] = inv
    c["icount"] = np.broadcast_to(np.concatenate(
        [1.0 / np.minimum(np.arange(16) + 1, w) for w in (2, 4, 8, 16)])[None], (P, 64))
    return {k: np.ascontiguousarray(np.asarray(v, np.float32)) for k, v in c.items()}


def bias_parts():
    pos = np.arange(384)
    dist = 255 - pos
    ok = (dist >= 0) & (dist < WINDOW)
    hot = np.zeros((P, 384), np.float32)
    hot[bucket_of(dist)[ok], pos[ok]] = 1.0
    mask = np.zeros((P, 384), np.float32)
    mask[:8] = np.where(ok, 0.0, NEG)
    flip = np.eye(P, dtype=np.float32)[::-1]
    return np.ascontiguousarray(np.concatenate([hot, mask, flip], axis=1))


def constants():
    parts = constant_parts()
    at, n = {}, 0
    for k, v in parts.items():
        at[k] = (n, v.shape[1])
        n += v.shape[1]
    return np.concatenate(list(parts.values()), axis=1), at, n


class Event:
    def __init__(self, sem, base):
        self.sem, self.base = sem, base

    def nth(self, i):
        return self.base + i + 1


class Signals:
    def __init__(self, nc, ctx):
        self.nc, self.ctx, self.sems, self.next = nc, ctx, {}, {}

    def sem(self, name):
        if name not in self.sems:
            self.sems[name] = self.ctx.enter_context(self.nc.semaphore(name))
            self.next[name] = 0
        return self.sems[name]

    def take(self, name, n):
        sem = self.sem(name)
        base = self.next[name]
        self.next[name] = base + n
        return Event(sem, base)


class Run:
    def __init__(self, t0, n, src, nk):
        self.t0, self.n, self.src, self.nk = t0, n, src, nk
        self.pairs = n // 2

    def t(self, i, p):
        return self.t0 + 2 * i + p


def rows128(v):
    return v.rearrange("(n p) -> n p", p=P)


def hybrid_program(nc, A, out):
    ctx = ExitStack()
    with ctx:
        _hybrid(nc, ctx, A, out)


def _hybrid(nc, ctx, A, out):
    def sb(name, shape, dt=F32):
        return ctx.enter_context(nc.sbuf_tensor(name, shape, dt))

    sig = Signals(nc, ctx)
    _, CAT, NCONST = constants()

    h_hi = sb("h_hi", [P, KD, T], F32R)
    h_lo = sb("h_lo", [P, KD, T], F32R)
    y_hi = sb("y_hi", [P, 4, T], F32R)
    y_lo = sb("y_lo", [P, 4, T], F32R)
    acc = sb("acc", [P, KD, T])
    w_raw = sb("w_raw", [P, 2, KD, P])
    w_hi = sb("w_hi", [P, 2, KD, P], F32R)
    w_lo = sb("w_lo", [P, 2, KD, P], F32R)
    wrk = sb("wrk", [P, 11, T])
    cst = sb("cst", [P, NCONST])
    cols = sb("cols", [P, 392])
    small = sb("small", [P, 344])
    pool_one = sb("pool_one", [P, 1])
    ps = ctx.enter_context(nc.psum_tensor("ps", [P, 8, HALF], F32))
    x_fm = nc.dram_tensor("x_fm", [KD, P, T], F32, kind="Internal").ap()
    bias_rows = nc.dram_tensor("bias_rows", [8, 384], F32, kind="Internal")

    def C(name):
        a, n = CAT[name]
        return cst[:, a:a + n]

    ident, ones = C("ident"), C("ones")

    def wt(j, half=None):
        return wrk[:, j, :] if half is None else wrk[:, j, half * HALF:(half + 1) * HALF]

    b_in = A["b_in"][0]
    segs = []

    def seg(name, ap):
        segs.append((name, ap))

    seg("b_aqkv", rows128(b_in[C_AQKV:C_AZ]))
    seg("b_az", rows128(b_in[C_AZ:C_BA]))
    seg("b_ba", rows128(b_in[C_BA:C_BA + P]))
    seg("b_glu", rows128(b_in[C_GLU:C_BZ]))
    seg("b_bz", rows128(b_in[C_BZ:C_CQ]))
    seg("b_cq", b_in[C_CQ:C_CKV].rearrange("(u t j) -> t u j", u=2, j=64))
    seg("b_ckv", rows128(b_in[C_CKV:C_CZ]))
    seg("b_cz", b_in[C_CZ:C_DX].rearrange("(u t j) -> t u j", u=2, j=64))
    seg("b_dx", rows128(b_in[C_DX:C_DZ]))
    seg("b_dz", rows128(b_in[C_DZ:C_EQ]))
    seg("b_eq", rows128(b_in[C_EQ:C_EZ]))
    seg("b_ez", rows128(b_in[C_EZ:C_GATE]))
    seg("b_gate", rows128(b_in[C_GATE:C_GATE + 5 * D]))
    for name in ("g_pre", "g_post", "g_mem", "b_dw_b", "b_ln_g", "b_ln_b", "d_conv_b", "d_b_a", "d_b_x",
                 "d_lambda", "a_norm_g", "even_norm_g_2", "odd_norm_g_2", "even_pool_scale_2",
                 "odd_ln_g_2", "odd_ln_b_2"):
        seg(name, rows128(A[name][0]))
    seg("g_mem_2", rows128(A["g_mem_2"]))
    seg("final_norm_g_2", rows128(A["final_norm_g_2"]))
    for name in ("a_conv_w", "d_conv_w", "b_dw_w"):
        seg(name, A[name][0].rearrange("k (n p) -> (k n) p", p=P))
    COL, nrows = {}, 0
    row_loads = []
    for name, ap in segs:
        COL[name] = nrows
        n, done = ap.shape[0], 0
        while done < n:
            k = min(n - done, P - nrows % P)
            row_loads.append((nrows // P, nrows % P, k, ap[done:done + k]))
            done += k
            nrows += k
    TABLE_ROWS = [min(P, nrows - P * j) for j in range(-(-nrows // P))]
    assert nrows <= 392, nrows

    def col(name, i=0):
        j = COL[name] + i
        return cols[:, j:j + 1]

    raw_loaded = [sig.sem(f"raw_loaded{s}") for s in range(2)]
    tiles_split = sig.sem("tiles_split")
    dense_out = sig.sem("dense_out")
    dense_free = [sig.sem(f"dense_free{b}") for b in range(2)]
    runs, ntiles = [], 0

    def run(pairs, src0, src1, nk0=KD, nk1=KD):
        nonlocal ntiles
        r = Run(ntiles, 2 * pairs, (src0, src1), (nk0, nk1))
        runs.append(r)
        ntiles += 2 * pairs
        return r

    def run_one(src):
        nonlocal ntiles
        r = Run(ntiles, 1, (src, None), (KD, KD))
        runs.append(r)
        ntiles += 1
        return r

    def weights(name, layer=0):
        w = A[name]
        w = w[layer] if len(w.shape) == 3 else w
        return w.rearrange("(k p) n -> p k n", p=P)

    def tiles_of(w, first, step=P):
        return lambda i: w[:, :, bass.ds(i * step + first, P)] if not isinstance(i, int) \
            else w[:, :, first + i * step:first + i * step + P]

    def both(w, first):
        return tiles_of(w, first, 2 * P), tiles_of(w, first + P, 2 * P)

    def rhs_h(part, k, b):
        return (h_hi, h_lo)[part][:, k, b * HALF:(b + 1) * HALF]

    def rhs_y(part, k, b):
        return (y_hi, y_lo)[part][:, k, b * HALF:(b + 1) * HALF]

    def mem_view(t, which):
        return t[:, 2 * which:2 * which + 2, :].rearrange("p a (b m) -> p (a b) m", m=MEM)

    def rhs_of_memory(which):
        return lambda part, k, b: mem_view((y_hi, y_lo)[part], which)[:, k, b * P:(b + 1) * P]
    keys_of = [rhs_of_memory(0), rhs_of_memory(1)]
    values_of = [rhs_of_memory(0), rhs_of_memory(1)]
    weights_moving = values_of

    engines = ("pe", "act", "dve")
    at_end = {e: sig.sem(f"{e}_at_section_end") for e in engines}
    sections = []

    def section():
        sections.append({"dense": [], "aux": [], "side": []})

    thread_now = ["dense"]

    def on(thread):
        thread_now[0] = thread

    def stage(name, us=5.0, ahead=(), **fns):
        sections[-1][thread_now[0]].append((name, us, fns, ahead))

    def solo_pe():
        return not any("pe" in st[2] for t in ("aux", "side") for st in sections[-1][t])

    class Chain:
        def __init__(self, eng, name):
            self.eng, self.sem, self.n = eng, sig.sem(name), 0

        def link(self, ins):
            self.eng.wait_ge(self.sem, self.mark(ins))

        def mark(self, ins):
            self.n += 1
            ins.then_inc(self.sem, 1)
            return self.n

        def after(self, n):
            self.eng.wait_ge(self.sem, n)

    chains = {}

    def dense_half(pe, t, b, slot, nk, rhs, n):
        pe.wait_ge(dense_free[b], t + 1)
        for k in range(nk):
            if k and k % 2 == 0:
                yield k / nk
            for q, (w, part) in enumerate(((w_hi, 0), (w_hi, 1), (w_lo, 0))):
                l, r = w[:, slot, k, :], rhs(part, k, b)
                if rhs in weights_moving:
                    l, r = r, l
                mm = nc.tensor.matmul(ps[:, b, 0:n], l, r, start=(k == 0 and q == 0),
                                      stop=(k == nk - 1 and q == 2))
        mm.then_inc(dense_out, 1)

    def when(r, j, b):
        done = sum(r.nk[q % 2] for q in range(j)) + r.nk[j % 2] * (b + 1) / 2
        return done / sum(r.nk[q % 2] for q in range(r.n))

    def dense_tile(pe, t, slot, nk, rhs, n=HALF):
        pe.wait_ge(tiles_split, t + 1)
        for b in range(2):
            for _ in dense_half(pe, t, b, slot, nk, rhs, n):
                pass

    def dense_run(pe, r, rhs0, rhs1, n=HALF):
        total, done = 2 * sum(r.nk[j % 2] for j in range(r.n)), 0
        for j in range(r.n):
            pe.wait_ge(tiles_split, r.t0 + j + 1)
            for b in range(2):
                yield done / total
                for part in dense_half(pe, r.t0 + j, b, (r.t0 + j) % 2, r.nk[j % 2], (rhs0, rhs1)[j % 2], n):
                    yield (done + part * r.nk[j % 2]) / total
                done += r.nk[j % 2]

    def dense_loop(pe, r, rhs0, rhs1):
        with pe.Fori(0, r.n // 2, 1) as i:
            for p, rhs in ((0, rhs0), (1, rhs1)):
                dense_tile(pe, r.t(i, p), (r.t0 + p) % 2, r.nk[p], rhs)

    def out_ready(eng, t, b):
        eng.wait_ge(dense_out, 2 * t + b + 1)

    def out_taken(eng, t, b):
        eng.wait_ge(dense_free[b], t + 2)

    def project(name, r, dst, bias=None, rhs=None, n=HALF, looped=False, before=None):
        def f_pe(pe):
            if looped:
                return dense_loop(pe, r, rhs or rhs_h, rhs or rhs_h)
            return dense_run(pe, r, rhs or rhs_h, rhs or rhs_h, n)

        def f_act(act):
            for j in range(r.n):
                for b in range(2):
                    yield when(r, j, b)
                    if before:
                        before(act, j, b)
                    out_ready(act, r.t0 + j, b)
                    if bias is None:
                        nc.scalar.activation(dst(j, b), ps[:, b, 0:n], ACT.Copy).then_inc(dense_free[b], 1)
                    else:
                        nc.scalar.activation(dst(j, b), ps[:, b, 0:n], ACT.Identity,
                                             bias=bias(j)).then_inc(dense_free[b], 1)
        stage(name, dense_us(r, n), ("pe",), pe=f_pe, act=f_act)

    def dense_us(r, n=HALF):
        return 1.3 * sum(r.nk[j % 2] for j in range(r.n)) * (1 if n == HALF else 0.5)

    def to_tiles(first):
        return lambda j, b: wt(first + j, b)

    def gate_z(name, r, o, bias, sz, yfirst=0, o_ready=None, looped=False):
        done = sig.take("y_done", 2 * r.n)

        def f_pe(pe):
            return (dense_loop if looped else dense_run)(pe, r, rhs_h, rhs_h)

        def f_act(act):
            for j in range(r.n):
                for b in range(2):
                    yield when(r, j, b)
                    out_ready(act, r.t0 + j, b)
                    if j >= 1:
                        act.wait_ge(done.sem, done.nth(2 * (j - 1) + b))
                    nc.scalar.activation(wt(sz, b), ps[:, b, :], ACT.Silu,
                                         bias=bias(j) if bias else 0.0).then_inc(dense_free[b], 1)

        def f_dve(dve):
            ch = chains["dve"]
            for j in range(r.n):
                for b in range(2):
                    yield when(r, j, b) + 1e-6
                    out_taken(dve, r.t0 + j, b)
                    if o_ready:
                        dve.wait_ge(*o_ready(j, b))
                    ch.link(nc.vector.tensor_tensor(o(j, b), o(j, b), wt(sz, b), ALU.mult))
                    hi = y_hi[:, yfirst + j, b * HALF:(b + 1) * HALF]
                    lo = y_lo[:, yfirst + j, b * HALF:(b + 1) * HALF]
                    ch.link(nc.vector.tensor_copy(hi, o(j, b)))
                    nc.vector.tensor_tensor(lo, o(j, b), hi.bitcast(F32), ALU.subtract).then_inc(done.sem, 1)
        stage(name, dense_us(r), ("pe",), pe=f_pe, act=f_act, dve=f_dve)

    def merge(name, r, gate_bias, first, gt, looped=False):
        done = sig.take("merged", 2 * r.pairs)

        def f_pe(pe):
            return (dense_loop if looped else dense_run)(pe, r, rhs_h, rhs_y)

        def f_act(act):
            for i in range(r.pairs):
                for b in range(2):
                    yield when(r, 2 * i, b)
                    out_ready(act, r.t(i, 0), b)
                    if i >= 1:
                        act.wait_ge(done.sem, done.nth(2 * (i - 1) + b))
                    nc.scalar.activation(wt(gt, b), ps[:, b, :], ACT.Sigmoid,
                                         bias=gate_bias(i)).then_inc(dense_free[b], 1)

        def f_dve(dve):
            ch = chains["dve"]
            for i in range(r.pairs):
                for b in range(2):
                    yield when(r, 2 * i + 1, b)
                    out_taken(dve, r.t(i, 0), b)
                    out_ready(dve, r.t(i, 1), b)
                    a = acc[:, i, b * HALF:(b + 1) * HALF]
                    if first:
                        nc.vector.tensor_tensor(a, ps[:, b, :], wt(gt, b), ALU.mult).then_inc(dense_free[b], 1)
                        dve.wait_ge(dense_free[b], r.t(i, 1) + 2)
                        nc.vector.engine_nop().then_inc(done.sem, 1)
                    else:
                        nc.vector.tensor_tensor(wt(gt, b), ps[:, b, :], wt(gt, b), ALU.mult).then_inc(dense_free[b], 1)
                        dve.wait_ge(dense_free[b], r.t(i, 1) + 2)
                        nc.vector.tensor_tensor(a, a, wt(gt, b), ALU.add).then_inc(done.sem, 1)
        stage(name, dense_us(r), pe=f_pe, act=f_act, dve=f_dve)

    def add_out(name, r, looped=False):
        def f_pe(pe):
            return (dense_loop if looped else dense_run)(pe, r, rhs_y, rhs_y)

        def f_dve(dve):
            for j in range(r.n):
                for b in range(2):
                    yield when(r, j, b)
                    out_ready(dve, r.t0 + j, b)
                    a = acc[:, j, b * HALF:(b + 1) * HALF]
                    nc.vector.tensor_tensor(a, a, ps[:, b, :], ALU.add).then_inc(dense_free[b], 1)
        stage(name, dense_us(r), pe=f_pe, dve=f_dve)

    def norm(name, src, n, emit, width=D, nk=KD, sq=0, rs=2, us=40.0):
        squared = sig.take("squared", 2 * nk)
        summed = sig.take("squares_summed", 2 * nk)
        root = sig.take("root", 2)

        def f_act(act):
            for b in range(2):
                for k in range(nk):
                    i = b * nk + k
                    yield (b + k / nk) * 0.35
                    if i >= 2:
                        act.wait_ge(summed.sem, summed.nth(i - 2))
                    nc.scalar.activation(wt(sq, i % 2)[:, 0:n], src(k, b), ACT.Square).then_inc(squared.sem, 1)
                yield (b + 1) * 0.35 - 1e-5
                act.wait_ge(summed.sem, summed.nth(b * nk + nk - 1))
                nc.scalar.activation(wt(rs, b)[:, 0:n], ps[:, 2 + b, 0:n], ACT.Sqrt, bias=EPS,
                                     scale=1.0 / width).then_inc(root.sem, 1)

        def f_pe(pe):
            for b in range(2):
                for k in range(nk):
                    i = b * nk + k
                    yield (b + k / nk) * 0.35 + 1e-6
                    pe.wait_ge(squared.sem, squared.nth(i))
                    nc.tensor.matmul(ps[:, 2 + b, 0:n], ones, wt(sq, i % 2)[:, 0:n], start=(k == 0),
                                     stop=(k == nk - 1)).then_inc(summed.sem, 1)

        def f_dve(dve):
            ch = chains["dve"]
            for b in range(2):
                yield 0.35 + b * 0.35
                dve.wait_ge(root.sem, root.nth(b))
                ch.link(nc.vector.reciprocal(wt(rs, b)[:, 0:n], wt(rs, b)[:, 0:n]))
                for k in range(nk):
                    yield 0.35 + (b + k / nk) * 0.35 * 0.99
                    emit(ch, k, b, wt(rs, b)[:, 0:n])
        stage(name, us, pe=f_pe, act=f_act, dve=f_dve)

    def split_emit(src, g, hi, lo, n, tmp=3):
        def emit(ch, k, b, root):
            t = wt(tmp, k % 2)[:, 0:n]
            ch.link(nc.vector.scalar_tensor_tensor(t, src(k, b), g(k), root, ALU.mult, ALU.mult))
            ch.link(nc.vector.tensor_copy(hi(k, b), t))
            ch.link(nc.vector.tensor_tensor(lo(k, b), t, hi(k, b).bitcast(F32), ALU.subtract))
        return emit

    def acc_at(k, b):
        return acc[:, k, b * HALF:(b + 1) * HALF]

    def norm_acc(name, g):
        norm(name, acc_at, HALF, split_emit(
            acc_at, lambda k: col(g, k), lambda k, b: h_hi[:, k, b * HALF:(b + 1) * HALF],
            lambda k, b: h_lo[:, k, b * HALF:(b + 1) * HALF], HALF))

    def head_norm(name, tile, n, scale, factor, sq=4, rs=6, us=80.0, ready=None):
        squared = sig.take("hn_squared", 2 * n)
        summed = sig.take("hn_summed", 2 * n)
        root = sig.take("hn_root", 2 * n)
        normed = sig.take("hn_normed", 2 * n)
        N = 2 * n + 2

        def f_act(act):
            for i in range(N):
                yield i / N
                if i < 2 * n:
                    if ready and i % 2 == 0:
                        act.wait_ge(*ready(i // 2))
                    if i >= 2:
                        act.wait_ge(summed.sem, summed.nth(i - 2))
                    nc.scalar.activation(wt(sq, i % 2), tile(i // 2, i % 2), ACT.Square).then_inc(squared.sem, 1)
                if i >= 2:
                    j = i - 2
                    act.wait_ge(summed.sem, summed.nth(j))
                    if j >= 2:
                        act.wait_ge(normed.sem, normed.nth(j - 2))
                    nc.scalar.activation(wt(rs, j % 2), ps[:, 2 + j % 4, :], ACT.Sqrt, bias=EPS,
                                         scale=scale).then_inc(root.sem, 1)

        def f_pe(pe):
            for i in range(2 * n):
                yield (i + 0.1) / N
                pe.wait_ge(squared.sem, squared.nth(i))
                if i >= 4:
                    pe.wait_ge(root.sem, root.nth(i - 4))
                nc.tensor.matmul(ps[:, 2 + i % 4, :], ones, wt(sq, i % 2), start=True,
                                 stop=True).then_inc(summed.sem, 1)

        def f_dve(dve):
            ch = chains["dve"]
            for i in range(2 * n):
                yield (i + 2.1) / N * 0.999
                dve.wait_ge(root.sem, root.nth(i))
                ch.link(nc.vector.reciprocal(wt(rs, i % 2), wt(rs, i % 2)))
                x = tile(i // 2, i % 2)
                nc.vector.scalar_tensor_tensor(x, x, factor(i // 2), wt(rs, i % 2), ALU.mult,
                                               ALU.mult).then_inc(normed.sem, 1)
        stage(name, us, pe=f_pe, act=f_act, dve=f_dve)
        return normed

    def conv(ch, tiles, dsts, taps, wcol, bcol=None):
        n = len(tiles)
        last = [0] * n
        for s in range(taps):
            for i in range(n):
                w = wcol(taps - 1 - s, i)
                if s == 0:
                    if bcol is None:
                        ins = nc.vector.tensor_scalar(dsts[i], tiles[i], w, None, ALU.mult)
                    else:
                        ins = nc.vector.tensor_scalar(dsts[i], tiles[i], w, bcol(i), ALU.mult, ALU.add)
                else:
                    ch.after(last[i])
                    ins = nc.vector.scalar_tensor_tensor(dsts[i][:, s:T], tiles[i][:, 0:T - s], w,
                                                         dsts[i][:, s:T], ALU.mult, ALU.add)
                last[i] = ch.mark(ins)
            yield s / taps
        ch.after(max(last))

    def layer_norm(name, tile, nk, width, g, tmp, finish=None, us=50.0):
        sq, rs = tmp
        total = sig.take("ln_total", 2)
        centered = sig.take("ln_centered", 2 * nk)
        squared = sig.take("ln_squared", 2 * nk)
        summed = sig.take("ln_summed", 2 * nk)
        root = sig.take("ln_root", 2)
        scaled = sig.take("ln_scaled", 2 * nk)

        at = lambda first, share, b, k: first + share * (b * nk + k) / (2 * nk)

        def f_pe(pe):
            for b in range(2):
                for k in range(nk):
                    yield at(0, 0.2, b, k)
                    mm = nc.tensor.matmul(ps[:, 4 + b, :], ones, tile(k, b), start=(k == 0), stop=(k == nk - 1))
                mm.then_inc(total.sem, 1)
            for b in range(2):
                for k in range(nk):
                    i = b * nk + k
                    yield at(0.3, 0.4, b, k) + 2e-6
                    pe.wait_ge(squared.sem, squared.nth(i))
                    nc.tensor.matmul(ps[:, 2 + b, :], ones, wt(sq, i % 2), start=(k == 0),
                                     stop=(k == nk - 1)).then_inc(summed.sem, 1)

        def f_act(act):
            for b in range(2):
                for k in range(nk):
                    i = b * nk + k
                    yield at(0.3, 0.4, b, k) + 1e-6
                    act.wait_ge(centered.sem, centered.nth(i))
                    if i >= 2:
                        act.wait_ge(summed.sem, summed.nth(i - 2))
                    nc.scalar.activation(wt(sq, i % 2), tile(k, b), ACT.Square).then_inc(squared.sem, 1)
                yield at(0.3, 0.4, b, nk) - 1e-6
                act.wait_ge(summed.sem, summed.nth(b * nk + nk - 1))
                nc.scalar.activation(wt(rs, b), ps[:, 2 + b, :], ACT.Sqrt, bias=EPS,
                                     scale=1.0 / width).then_inc(root.sem, 1)
            if finish:
                for b in range(2):
                    for k in range(nk):
                        yield at(0.7, 0.3, b, k + 1)
                        act.wait_ge(scaled.sem, scaled.nth(b * nk + k))
                        finish(k, b)

        def f_dve(dve):
            ch = chains["dve"]
            for b in range(2):
                yield at(0.2, 0.1, b, 0)
                dve.wait_ge(total.sem, total.nth(b))
                for k in range(nk):
                    nc.vector.scalar_tensor_tensor(tile(k, b), ps[:, 4 + b, :], -1.0 / width, tile(k, b),
                                                   ALU.mult, ALU.add).then_inc(centered.sem, 1)
            for b in range(2):
                yield at(0.7, 0.29, b, 0)
                dve.wait_ge(root.sem, root.nth(b))
                ch.link(nc.vector.reciprocal(wt(rs, b), wt(rs, b)))
                for k in range(nk):
                    yield at(0.7, 0.29, b, k)
                    nc.vector.scalar_tensor_tensor(tile(k, b), tile(k, b), g(k), wt(rs, b), ALU.mult,
                                                   ALU.mult).then_inc(scaled.sem, 1)
        stage(name, us, pe=f_pe, act=f_act, dve=f_dve)

    def softplus(name, a, e, z, z2, q):
        s_e = sig.take("softplus_exp", 1)

        def f_act(act):
            ch = chains["act"]
            ch.link(nc.scalar.activation(e, a, ACT.Abs))
            nc.scalar.activation(e, e, ACT.Exp, scale=-1.0).then_inc(s_e.sem, 1)

        def f_dve(dve):
            ch = chains["dve"]
            dve.wait_ge(s_e.sem, s_e.nth(0))
            ch.link(nc.vector.tensor_scalar(z, e, 2.0, None, ALU.add))
            ch.link(nc.vector.reciprocal(z, z))
            ch.link(nc.vector.tensor_tensor(z, e, z, ALU.mult))
            ch.link(nc.vector.tensor_tensor(z2, z, z, ALU.mult))
            ch.link(nc.vector.tensor_scalar(q, z2, 1.0 / 17, None, ALU.mult))
            for c in (15, 13, 11, 9, 7, 5, 3):
                ch.link(nc.vector.scalar_tensor_tensor(q, q, 1.0 / c, z2, ALU.add, ALU.mult))
            ch.link(nc.vector.scalar_tensor_tensor(q, q, 1.0, z, ALU.add, ALU.mult))
            ch.link(nc.vector.tensor_scalar(a, a, 0.0, None, ALU.max))
            ch.link(nc.vector.scalar_tensor_tensor(a, q, 2.0, a, ALU.mult, ALU.add))
        stage(name, 6.0, act=f_act, dve=f_dve)

    class Unit:
        def __init__(self, scores, bias, pv):
            self.scores, self.bias, self.pv = scores, bias, pv

    def attention(name, steps, width, scale, has_bias, normalize, spt, ptt, pv, take, sinks=None, stats=None, us=0):
        N = len(steps)
        per = 1.0 / (N + 0.1)
        nkb = width // P
        scored = sig.take("scored", N)
        maxed = sig.take("score_max", N)
        expd = sig.take("probs_exp", N)
        normd = sig.take("probs_ready", N)
        turned = sig.take("probs_turned", N)
        pt_ready = sig.take("turned_copied", N)
        mixed = sig.take("values_mixed", N)
        taken = sig.take("values_taken", N)
        S = ps[:, 2:4, :].rearrange("p a (u w) -> p (a u) w", w=256)
        PT = ps[:, 4:6, :].rearrange("p a w -> p (a w)").rearrange("p (k u w) -> p k u w", k=2, u=4)
        SB = wt(spt).rearrange("p (u w) -> p u w", u=4)
        PB = wt(ptt).rearrange("p (k u w) -> p k u w", k=2, u=4)
        lo = 256 - width
        mx, nmx, den, rden, esk = (small[:, 256 + 4 * q:260 + 4 * q] for q in range(5))

        def f_pe(pe):
            def scores(n):
                if n >= 1:
                    pe.wait_ge(expd.sem, expd.nth(n - 1))
                for u, unit in enumerate(steps[n]):
                    for c, l, r in unit.scores:
                        mm = nc.tensor.matmul(S[:, u, c], l, r, start=True, stop=True)
                mm.then_inc(scored.sem, 1)
            scores(0)
            for n in range(N):
                yield (n + 0.4) * per
                if n + 1 < N:
                    scores(n + 1)
                yield (n + 0.6) * per
                pe.wait_ge(normd.sem, normd.nth(n))
                if n >= 1:
                    pe.wait_ge(pt_ready.sem, pt_ready.nth(n - 1))
                for u in range(4):
                    for kb in range(nkb):
                        mm = nc.tensor.transpose(PT[:, kb, u, :], SB[:, u, lo + kb * P:lo + (kb + 1) * P], ident)
                mm.then_inc(turned.sem, 1)
                yield (n + 0.8) * per
                pe.wait_ge(pt_ready.sem, pt_ready.nth(n))
                if n >= 2:
                    pe.wait_ge(taken.sem, taken.nth(n - 2))
                mm = pv(pe, n, ps[:, 6 + n % 2, :], PB)
                mm.then_inc(mixed.sem, 1)

        def f_act(act):
            for n in range(N):
                yield (n + 0.3) * per
                act.wait_ge(maxed.sem, maxed.nth(n))
                for u in range(4):
                    src = SB[:, u, lo:256] if has_bias else S[:, u, lo:256]
                    ins = nc.scalar.activation(SB[:, u, lo:256], src, ACT.Exp, bias=nmx[:, u:u + 1],
                                               scale=1.0 if has_bias else scale, accum_out=den[:, u:u + 1])
                if sinks is not None:
                    nc.scalar.activation(esk, esk, ACT.Exp).then_inc(expd.sem, 1)
                else:
                    ins.then_inc(expd.sem, 1)
                yield (n + 0.7) * per
                act.wait_ge(turned.sem, turned.nth(n))
                if n >= 1:
                    act.wait_ge(mixed.sem, mixed.nth(n - 1))
                nc.scalar.activation(PB[:, 0:nkb], PT[:, 0:nkb], ACT.Copy).then_inc(pt_ready.sem, 1)

        def f_dve(dve):
            ch = chains["dve"]

            def take_away(n):
                dve.wait_ge(mixed.sem, mixed.nth(n))
                take(n, ps[:, 6 + n % 2, :]).then_inc(taken.sem, 1)
            for n in range(N):
                yield (n + 0.05) * per
                dve.wait_ge(scored.sem, scored.nth(n))
                if n >= 1:
                    dve.wait_ge(turned.sem, turned.nth(n - 1))
                if has_bias:
                    for u in range(4):
                        ins = nc.vector.scalar_tensor_tensor(SB[:, u, lo:256], S[:, u, lo:256], scale,
                                                             steps[n][u].bias, ALU.mult, ALU.add)
                    ch.link(ins)
                    ch.link(nc.vector.tensor_reduce(mx, SB[:, :, lo:256], AX, ALU.max))
                else:
                    ch.link(nc.vector.tensor_reduce(mx, S[:, :, lo:256], AX, ALU.max))
                if sinks is not None:
                    ch.link(nc.vector.tensor_tensor(mx, mx, sinks(n), ALU.max))
                    ch.link(nc.vector.tensor_tensor(esk, sinks(n), mx, ALU.subtract))
                if stats:
                    ch.link(nc.vector.tensor_copy(stats(n)[0], mx))
                nc.vector.tensor_scalar(nmx, mx, -1.0 if has_bias else -scale, None,
                                        ALU.mult).then_inc(maxed.sem, 1)
                if n >= 1:
                    yield (n + 0.2) * per
                    take_away(n - 1)
                yield (n + 0.45) * per
                dve.wait_ge(expd.sem, expd.nth(n))
                if not normalize:
                    nc.vector.tensor_copy(stats(n)[1], den).then_inc(normd.sem, 1)
                    continue
                if sinks is not None:
                    ch.link(nc.vector.tensor_tensor(den, den, esk, ALU.add))
                ch.link(nc.vector.reciprocal(rden, den))
                for u in range(4):
                    ins = nc.vector.tensor_scalar(SB[:, u, lo:256], SB[:, u, lo:256], rden[:, u:u + 1],
                                                  None, ALU.mult)
                ins.then_inc(normd.sem, 1)
            yield N * per
            take_away(N - 1)
        stage(name, us or 12.0 * N, pe=f_pe, act=f_act, dve=f_dve)

    loaded = sig.sem("loaded")
    nloads = [0]

    def load(act, dst, src):
        nloads[0] += 1
        act.dma_start(dst, src).then_inc(loaded, 16)

    def loads_done(act):
        act.wait_ge(loaded, 16 * nloads[0])

    section()
    on("dense")
    x_tiles = A["x"][0].rearrange("(n p) d -> n p d", p=P)
    a_small = small[:, 304:308]
    dt_small = small[:, 308:312]

    def load_inputs(act):
        load(act, cst[:], A["consts"])
        for table, row, k, ap in row_loads:
            dst = wt(0)[row:row + k, table * P:(table + 1) * P]
            if len(ap.shape) == 3:
                dst = dst.rearrange("p (u j) -> p u j", u=2)
            load(act, dst, ap)
        load(act, a_small, A["a_log"][0].partition_broadcast(P))
        load(act, dt_small, A["a_dt_bias"][0].partition_broadcast(P))
        for n in range(T // P):
            load(act, wt(1 + n), x_tiles[n])
        loads_done(act)
    stage("load", act=load_inputs)

    x_turned = sig.take("x_turned", T // P + 1)
    x_copied = sig.take("x_copied", T // P + 1)

    def turn_inputs(pe):
        for j, n in enumerate(TABLE_ROWS):
            mm = nc.tensor.transpose(ps[:, 2, j * P:j * P + n], wt(0)[0:n, j * P:(j + 1) * P], ident[0:n, 0:n])
        mm.then_inc(x_turned.sem, 1)
        for n in range(T // P):
            if n >= 2:
                pe.wait_ge(x_copied.sem, x_copied.nth(n - 2 + 1))
            for d in range(KD):
                mm = nc.tensor.transpose(ps[:, 4 + 2 * (n % 2) + d // 4, (d % 4) * P:(d % 4 + 1) * P],
                                         wt(1 + n)[:, d * P:(d + 1) * P], ident)
            mm.then_inc(x_turned.sem, 1)

    def copy_inputs(dve):
        dve.wait_ge(x_turned.sem, x_turned.nth(0))
        nc.vector.tensor_copy(cols[:, 0:nrows], ps[:, 2, 0:nrows]).then_inc(x_copied.sem, 1)
        for n in range(T // P):
            dve.wait_ge(x_turned.sem, x_turned.nth(n + 1))
            src = ps[:, 4 + 2 * (n % 2):6 + 2 * (n % 2), :].rearrange("p a (d t) -> p (a d) t", t=P)
            nc.vector.tensor_copy(acc[:, :, n * P:(n + 1) * P], src).then_inc(x_copied.sem, 1)
    stage("turn x", pe=turn_inputs, dve=copy_inputs)

    x_stored = sig.sem("x_stored")

    def store_x(act):
        act.dma_start(x_fm.rearrange("k p t -> p k t"), acc[:]).then_inc(x_stored, 16)
    stage("store x", act=store_x)
    norm_acc("norm x", "g_pre")
    w_in = weights("w_in")
    w_br = [A["w_br"][0, n].rearrange("(k p) n -> p k n", p=P) for n in range(5)]

    def pieces_of(w):
        return lambda i: w[:, :, bass.ds((i * 2) * (P // 2), P)]

    def wait_x(act):
        act.wait_ge(x_stored, 16)
    stage("x stored", act=wait_x)

    away = nc.dram_tensor("away", [40, P, T], F32, kind="Internal").ap()
    away_done = [sig.sem(f"away_done{b}") for b in range(2)]
    naway = [0, 0]
    next_away = [0]

    def send(act, dst, src, b):
        act.dma_start(dst, src).then_inc(away_done[b], 16)
        naway[b] += 1

    def room(act, b):
        if naway[b]:
            act.wait_ge(away_done[b], 16 * naway[b])

    def project_away(name, r, bias, func=None, first=None):
        at = next_away[0] if first is None else first
        next_away[0] = max(next_away[0], at + r.n)

        def f_pe(pe):
            return dense_run(pe, r, rhs_h, rhs_h)

        def f_act(act):
            for j in range(r.n):
                for b in range(2):
                    yield when(r, j, b)
                    room(act, b)
                    out_ready(act, r.t0 + j, b)
                    f = func(j) if func else ACT.Identity
                    ins = nc.scalar.activation(wt(10, b), ps[:, b, :], f if bias or f != ACT.Identity else ACT.Copy,
                                               bias=bias(j) if bias else 0.0)
                    ins.then_inc(dense_free[b], 1)
                    act.wait_ge(dense_free[b], r.t0 + j + 2)
                    send(act, away[at + j, :, b * HALF:(b + 1) * HALF], wt(10, b), b)
        stage(name, dense_us(r), ("pe",), pe=f_pe, act=f_act)
        return at

    def fetch(name, pairs, us=10.0, before=None):
        def f_act(act):
            for b in range(2):
                room(act, b)
            if before:
                before(act)
            for tile, place in pairs:
                load(act, wt(tile), away[place])
            yield 0.95
            loads_done(act)
        stage(name, us, act=f_act)

    def merge_run(n):
        return run(KD, tiles_of(w_in, C_GATE + n * D), pieces_of(w_br[n]), KD, 4)

    section()
    on("dense")

    def a_tile(j, b=None):
        if j < 8:
            return acc[:, j, :] if b is None else acc_at(j, b)
        return wt(j - 8, b)

    r_ba = run_one(tiles_of(w_in, C_BA))
    r_a = run(6, *both(w_in, C_AQKV))
    project("A beta alpha", r_ba, lambda j, b: wt(10, b), lambda j: col("b_ba", 0))
    project("A project", r_a, a_tile, lambda j: col("b_aqkv", j))
    logits_turned = sig.take("logits_turned", 1)

    def logits_wait(act):
        act.wait_ge(logits_turned.sem, logits_turned.nth(0))
    stage("A logits", 0.1, act=logits_wait)
    mem_normed = sig.take("mem_normed", 1)
    at_glu = project_away("B glu", run(4, *both(w_in, C_GLU)), lambda j: col("b_glu", j),
                          lambda j: ACT.Identity if j < 4 else ACT.Sigmoid)

    def memory_kv(name, w_kv, which):
        at = next_away[0]
        next_away[0] += 2
        for kind in range(2):
            r = run(2, *both(w_kv, kind * W))
            rhs = (keys_of, values_of)[kind][which]

            def f_pe(pe, r=r, rhs=rhs):
                pe.wait_ge(mem_normed.sem, mem_normed.nth(0))
                yield from dense_run(pe, r, rhs, rhs, P)

            def f_act(act, r=r, kind=kind):
                ch = chains["act"]
                for b in range(2):
                    room(act, b)
                for j in range(r.n):
                    for b in range(2):
                        yield when(r, j, b)
                        out_ready(act, r.t0 + j, b)
                        dst = wt(10)[:, j * MEM + b * P:j * MEM + (b + 1) * P] if kind == 0 else \
                            wt(10)[:, b * HALF + j * P:b * HALF + (j + 1) * P]
                        nc.scalar.activation(dst, ps[:, b, 0:P], ACT.Copy).then_inc(dense_free[b], 1)
                        act.wait_ge(dense_free[b], r.t0 + j + 2)
                for b in range(2):
                    send(act, away[at + kind, :, b * HALF:(b + 1) * HALF], wt(10, b), b)
            stage(name, dense_us(r, P), ("pe",), pe=f_pe, act=f_act)
        return at
    at_kv = [memory_kv("E k v", weights("w_mem_kv"), 0), memory_kv("even k v", weights("even_w_mem_kv_2"), 1),
             memory_kv("odd k v", weights("odd_w_mem_kv_2"), 1)]

    def swapped(w, first):
        v = w[:, :, first:first + W].rearrange("p k (u t j) -> p k u t j", u=2, j=64)
        return lambda i, p: ("columns", [v[:, :, u, 2 * i + p, :] for u in range(2)])
    cq = swapped(w_in, C_CQ)
    cz = swapped(w_in, C_CZ)
    at_cq = next_away[0]
    for i in range(2):
        project_away("C q", run(1, lambda _, i=i: cq(i, 0), lambda _, i=i: cq(i, 1)),
                     lambda j, i=i: col("b_cq", 2 * i + j))
    at_ckv = project_away("C k v", run(1, *both(w_in, C_CKV)), lambda j: col("b_ckv", j))
    at_dx = project_away("D x", run(2, *both(w_in, C_DX)), lambda j: col("b_dx", j))
    at_eq = project_away("E q", run(2, *both(w_in, C_EQ)), lambda j: col("b_eq", j))

    def stored_away(act):
        for b in range(2):
            room(act, b)
    stage("stored", 3.0, act=stored_away)

    on("aux")
    beta_t = small[:, 0:64].rearrange("p (n h) -> p n h", h=8)
    g_t = small[:, 64:128].rearrange("p (n h) -> p n h", h=8)
    gc_t = small[:, 128:192].rearrange("p (n h) -> p n h", h=8)

    def ba_turn(pe):
        yield 0.85
        out_taken(pe, r_ba.t0, 0)
        out_taken(pe, r_ba.t0, 1)
        for n in range(8):
            mm = nc.tensor.transpose(ps[:, 2, n * 8:n * 8 + 8], wt(10)[0:8, n * P:(n + 1) * P], ident[0:8, 0:8])
        mm.then_inc(logits_turned.sem, 1)
    stage("A turn", 24.0, pe=ba_turn)

    def ba_copy(dve):
        ch = chains["dve"]
        ch.link(nc.vector.tensor_copy(small[:, 0:64], ps[:, 2, 0:64]))
        nc.vector.tensor_tensor(g_t[:, :, 4:8], beta_t[:, :, 4:8],
                                dt_small.unsqueeze(1).to_broadcast([P, 8, 4]), ALU.add)
    stage("A turned", 3.0, dve=ba_copy)

    def ba_sig(act):
        nc.scalar.activation(beta_t[:, :, 0:4], beta_t[:, :, 0:4], ACT.Sigmoid)
        nc.scalar.activation(a_small, a_small, ACT.Exp)
    stage("A sigmoid", 5.0, act=ba_sig)
    four_small = [small[:, c:c + 32].rearrange("p (n h) -> p n h", h=4) for c in (128, 160, 192, 224)]
    softplus("A softplus", g_t[:, :, 4:8], *four_small)

    def ba_decay(dve):
        nc.vector.scalar_tensor_tensor(g_t[:, :, 4:8], g_t[:, :, 4:8], -1.0,
                                       a_small.unsqueeze(1).to_broadcast([P, 8, 4]), ALU.mult, ALU.mult)

    def ba_sum(pe):
        nc.tensor.matmul(ps[:, 4, 0:32], C("upto"), g_t[:, :, 4:8], start=True, stop=True)

    def ba_sum_copy(dve):
        nc.vector.tensor_copy(gc_t[:, :, 4:8], ps[:, 4, 0:32].rearrange("p (n h) -> p n h", h=4))
    stage("A decay", 1.0, dve=ba_decay)
    stage("A running sum", 1.0, pe=ba_sum)
    stage("A running sum copied", 1.0, dve=ba_sum_copy)

    for which, (mem, g_mem) in enumerate(((A["mem"], "g_mem"), (A["mem_2"], "g_mem_2"))):
        def m_load(act, mem=mem):
            for j in range(2):
                load(act, wt(6 + j), mem[0].rearrange("(n p) d -> n p d", p=P)[j])
            yield 0.9
            loads_done(act)
        stage("memory", 8.0, act=m_load)
        mem_t = wrk[:, 8:10, :].rearrange("p a (k m) -> p (a k) m", m=MEM)

        def m_turn(pe):
            for j in range(2):
                for k in range(KD):
                    nc.tensor.transpose(ps[:, 2 + k // 2, (k % 2) * MEM + j * P:(k % 2) * MEM + (j + 1) * P],
                                        wt(6 + j)[:, k * P:(k + 1) * P], ident)

        def m_copy(dve):
            nc.vector.tensor_copy(wrk[:, 8:10, :].rearrange("p a (b m) -> p (a b) m", m=HALF), ps[:, 2:6, :])
        stage("memory turned", 4.0, pe=m_turn)
        stage("memory copied", 3.0, dve=m_copy)
        src = lambda k, b: mem_t[:, k, b * P:(b + 1) * P]
        norm("memory norm", src, P, split_emit(
            src, lambda k, g=g_mem: col(g, k), lambda k, b, w=which: mem_view(y_hi, w)[:, k, b * P:(b + 1) * P],
            lambda k, b, w=which: mem_view(y_lo, w)[:, k, b * P:(b + 1) * P], P, tmp=5), sq=6, rs=7, us=30.0)

    def memories_there(dve):
        nc.vector.engine_nop().then_inc(mem_normed.sem, 1)
    stage("memories there", 0.5, dve=memories_there)

    conved = sig.take("a_conved", 6)
    silued = sig.take("a_silued", 12)

    def a_conv(dve):
        ch = chains["dve"]
        for i in range(6):
            j = 2 * i
            yield i / 7
            for jj in (j, j + 1):
                for b in range(2):
                    out_taken(dve, r_a.t0 + jj, b)
            if i >= 1:
                dve.wait_ge(silued.sem, silued.nth(j - 1))
            for part in conv(ch, [a_tile(j), a_tile(j + 1)], [wt(4), wt(5)], 4,
                             lambda tap, m, j=j: col("a_conv_w", tap * 12 + j + m)):
                yield (i + 0.7 * part) / 7
            nc.vector.engine_nop().then_inc(conved.sem, 1)

    def a_silu(act):
        for j in range(12):
            yield (j // 2 + 0.85) / 7
            act.wait_ge(conved.sem, conved.nth(j // 2))
            nc.scalar.activation(a_tile(j), wt(4 + j % 2), ACT.Silu).then_inc(silued.sem, 1)
    stage("A conv", 84.0, dve=a_conv, act=a_silu)
    head_norm("A norm q k", a_tile, 8, 1.0, lambda j: P ** -0.5 if j < 4 else 1.0)

    def slot(j):
        return wrk[:, 4 + j // 2, (j % 2) * HALF:(j % 2 + 1) * HALF].rearrange("p (h c) -> p h c", h=4)

    LT, AT, BT, ZZ, TT, UU, VB, KBE, KDEC, ATT, ST, EG = (slot(j) for j in range(12))
    dk, eg, nbeg, ekd = (small[:, 200 + 4 * q:204 + 4 * q] for q in range(4))

    def four(b):
        return ps[:, b, :].rearrange("p (h c) -> p h c", h=4)

    def all4(m):
        return m.unsqueeze(1).to_broadcast([P, 4, P])

    NPE, NACT, NDVE = 2 + 2 * NLEVEL, 3 + NLEVEL, 4 + 2 * NLEVEL
    gdn_pe = sig.take("gdn_pe", 8 * NPE)
    gdn_act = sig.take("gdn_act", 8 * NACT)
    gdn_dve = sig.take("gdn_dve", 8 * NDVE)
    L = NLEVEL
    lev_at = lambda lv: (9 + 4 * (lv - 1)) / 40

    def delta_chunk(n):
        c = slice(n * P, (n + 1) * P)
        step_pe = lambda i: (gdn_pe.sem, gdn_pe.nth(n * NPE + i))
        step_act = lambda i: (gdn_act.sem, gdn_act.nth(n * NACT + i))
        step_dve = lambda i: (gdn_dve.sem, gdn_dve.nth(n * NDVE + i))

        def f_pe(pe):
            def products(dst, lhsT, rhs):
                for h in range(4):
                    mm = nc.tensor.matmul(four(dst)[:, h, :], lhsT(h), rhs(h), start=True, stop=True)
                return mm
            for h in range(4):
                nc.tensor.transpose(four(2)[:, h, :], acc[:, 4 + h, c], ident)
                nc.tensor.transpose(four(3)[:, h, :], wt(h)[:, c], ident)
            products(4, lambda h: gc_t[:, n, 4 + h:5 + h].to_broadcast([P, P]), lambda h: ident)
            products(5, lambda h: beta_t[:, n, h:h + 1].to_broadcast([P, P]), lambda h: ident)
            products(6, lambda h: acc[:, 4 + h, c], lambda h: acc[:, 4 + h, c])
            products(7, lambda h: acc[:, 4 + h, c], lambda h: acc[:, h, c]).then_inc(gdn_pe.sem, 1)
            yield 6 / 40
            pe.wait_ge(*step_dve(3))
            pe.wait_ge(*step_act(2))
            for h in range(4):
                mm = nc.tensor.transpose(four(2)[:, h, :], BT[:, h, :], ident)
            mm.then_inc(gdn_pe.sem, 1)
            for lv in range(1, L):
                yield lev_at(lv)
                pe.wait_ge(*step_dve(3 + 2 * lv))
                products(2, lambda h: BT[:, h, :], lambda h: TT[:, h, :]).then_inc(gdn_pe.sem, 1)
                yield lev_at(lv) + 2 / 40
                pe.wait_ge(*step_act(2 + lv))
                if lv < L - 1:
                    products(3, lambda h: UU[:, h, :], lambda h: ZZ[:, h, :])
                products(4, lambda h: ZZ[:, h, :], lambda h: UU[:, h, :]).then_inc(gdn_pe.sem, 1)
            yield 33 / 40
            pe.wait_ge(*step_dve(2 + 2 * L))
            products(6, lambda h: KBE[:, h, :], lambda h: UU[:, h, :]).then_inc(gdn_pe.sem, 1)
            yield 35 / 40
            pe.wait_ge(*step_act(2 + L))
            for h in range(4):
                mm = nc.tensor.matmul(four(5)[:, h, :], UU[:, h, :], VB[:, h, :], start=True, stop=(n == 0))
                if n > 0:
                    mm = nc.tensor.matmul(four(5)[:, h, :], ZZ[:, h, :], ST[:, h, :], start=False, stop=True)
            mm.then_inc(gdn_pe.sem, 1)
            yield 37 / 40
            pe.wait_ge(*step_dve(3 + 2 * L))
            for h in range(4):
                if n > 0:
                    nc.tensor.matmul(four(7)[:, h, :], ST[:, h, :], acc[:, h, c], start=True, stop=False)
                nc.tensor.matmul(four(7)[:, h, :], TT[:, h, :], ATT[:, h, :], start=(n == 0), stop=True)
            products(2, lambda h: KDEC[:, h, :], lambda h: TT[:, h, :])

        def f_act(act):
            yield 2 / 40
            act.wait_ge(*step_pe(0))
            nc.scalar.activation(EG, four(4), ACT.Exp)
            nc.scalar.activation(eg, gc_t[:, n, 4:8], ACT.Exp).then_inc(gdn_act.sem, 1)
            yield 4 / 40
            act.wait_ge(*step_dve(0))
            nc.scalar.activation(ekd, dk, ACT.Exp)
            nc.scalar.activation(LT, LT, ACT.Exp).then_inc(gdn_act.sem, 1)
            act.wait_ge(*step_act(1))
            yield 5 / 40
            act.wait_ge(*step_dve(1))
            for h in range(4):
                nc.scalar.activation(VB[:, h, :], four(3)[:, h, :], ACT.Copy, scale=beta_t[:, n, h:h + 1])
                nc.scalar.activation(KBE[:, h, :], four(2)[:, h, :], ACT.Copy, scale=nbeg[:, h:h + 1])
                ins = nc.scalar.activation(KDEC[:, h, :], four(2)[:, h, :], ACT.Copy, scale=ekd[:, h:h + 1])
            ins.then_inc(gdn_act.sem, 1)
            for lv in range(1, L):
                yield lev_at(lv) + 1 / 40
                act.wait_ge(*step_pe(2 * lv))
                nc.scalar.activation(ZZ, four(2), ACT.Copy).then_inc(gdn_act.sem, 1)
            yield 34 / 40
            act.wait_ge(*step_pe(2 * L))
            nc.scalar.activation(ZZ, four(6), ACT.Copy).then_inc(gdn_act.sem, 1)

        def f_dve(dve):
            ch = chains["dve"]
            yield 3 / 40
            dve.wait_ge(*step_pe(0))
            dve.wait_ge(*step_act(0))
            for h in range(4):
                nc.vector.scalar_tensor_tensor(LT[:, h, :], four(4)[:, h, :], gc_t[:, n, 4 + h:5 + h],
                                               C("negafter"), ALU.subtract, ALU.add)
            nc.vector.tensor_tensor(dk, four(4)[:, :, P - 1], gc_t[:, n, 4:8], ALU.subtract).then_inc(gdn_dve.sem, 1)
            nc.vector.scalar_tensor_tensor(nbeg, eg, -1.0, beta_t[:, n, 0:4], ALU.mult,
                                           ALU.mult).then_inc(gdn_dve.sem, 1)
            ch.link(nc.vector.tensor_tensor(acc[:, 0:4, c], acc[:, 0:4, c], EG, ALU.mult))
            yield 5 / 40
            dve.wait_ge(*step_act(1))
            ch.link(nc.vector.tensor_tensor(AT, four(6), LT, ALU.mult))
            ch.link(nc.vector.tensor_tensor(AT, AT, four(5), ALU.mult))
            nc.vector.tensor_tensor(ATT, four(7), LT, ALU.mult).then_inc(gdn_dve.sem, 1)
            nc.vector.tensor_tensor(BT, AT, all4(C("lev0")), ALU.mult).then_inc(gdn_dve.sem, 1)
            dve.wait_ge(*step_dve(3))
            ch.link(nc.vector.tensor_tensor(UU, all4(ident), BT, ALU.subtract))
            yield 7 / 40
            dve.wait_ge(*step_pe(1))
            nc.vector.tensor_tensor(TT, all4(ident), four(2), ALU.subtract).then_inc(gdn_dve.sem, 1)
            nc.vector.tensor_tensor(BT, AT, all4(C("lev1")), ALU.mult).then_inc(gdn_dve.sem, 1)
            for lv in range(1, L):
                if lv < L - 1:
                    yield lev_at(lv) + 1 / 40
                    dve.wait_ge(*step_pe(2 * lv))
                    nc.vector.tensor_tensor(BT, AT, all4(C(f"lev{lv + 1}")), ALU.mult).then_inc(gdn_dve.sem, 1)
                yield lev_at(lv) + 3 / 40
                dve.wait_ge(*step_pe(2 * lv + 1))
                if lv < L - 1:
                    nc.vector.tensor_tensor(TT, TT, four(3), ALU.subtract)
                nc.vector.tensor_tensor(UU, UU, four(4), ALU.subtract).then_inc(gdn_dve.sem, 1)
            yield 36 / 40
            dve.wait_ge(*step_pe(2 * L + 1))
            nc.vector.tensor_copy(TT, four(5)).then_inc(gdn_dve.sem, 1)
        stage(f"A chunk {n}", CHUNK_TIME, pe=f_pe, act=f_act, dve=f_dve)

        def s_act(act):
            nc.scalar.activation(acc[:, 0:4, c], four(7), ACT.Copy)

        def s_dve(dve):
            for h in range(4):
                if n == 0:
                    nc.vector.tensor_copy(ST[:, h, :], four(2)[:, h, :])
                else:
                    nc.vector.scalar_tensor_tensor(ST[:, h, :], ST[:, h, :], EG[:, h, P - 1:P],
                                                   four(2)[:, h, :], ALU.mult, ALU.add)
        stage(f"A chunk {n} state", 2.0, act=s_act, dve=s_dve)

    for n in range(8):
        delta_chunk(n)

    section()
    on("aux")
    o_normed = head_norm("A norm out", a_tile, 4, 1.0 / P, lambda j: col("a_norm_g"), sq=8, rs=9, us=44.0)
    fetch("B glu", [(j, at_glu + j) for j in range(8)], 14.0)

    def b_mult(dve):
        for i in range(4):
            nc.vector.tensor_tensor(wt(i), wt(i), wt(4 + i), ALU.mult)
    stage("B gated", 6.0, dve=b_mult)

    def b_conv(dve):
        yield from conv(chains["dve"], [wt(i) for i in range(4)], [wt(4 + i) for i in range(4)], 31,
                        lambda tap, i: col("b_dw_w", tap * 4 + i), lambda i: col("b_dw_b", i))
    stage("B conv", 145.0, dve=b_conv)
    layer_norm("B norm", lambda k, b: wt(4 + k, b), 4, W, lambda k: col("b_ln_g", k), (8, 9),
               lambda k, b: nc.scalar.activation(wt(4 + k, b), wt(4 + k, b), ACT.Silu, bias=col("b_ln_b", k)))
    on("dense")
    stage("first outputs normed", 8.0)
    gate_z("A z", run(2, *both(w_in, C_AZ)), acc_at, lambda j: col("b_az", j), 10,
           o_ready=lambda j, b: (o_normed.sem, o_normed.nth(2 * j + b)))
    merge("A merge", merge_run(0), lambda i: col("b_gate", i), True, 10)

    section()
    on("dense")
    gate_z("B z", run(2, *both(w_in, C_BZ)), lambda j, b: wt(4 + j, b), lambda j: col("b_bz", j), 10)
    b_gated = sig.take("b_gated", 1)

    def b_gated_dve(dve):
        nc.vector.engine_nop().then_inc(b_gated.sem, 1)
    stage("B gated", 0.1, dve=b_gated_dve)
    merge("B merge", merge_run(1), lambda i: col("b_gate", 8 + i), False, 10)
    on("aux")

    def c_load(act):
        load(act, wt(0)[:, 0:896], A["bias_consts"])
        load(act, wt(1)[0:32, 0:8], A["rel_bias"])
        load(act, small[:, 304:312], A["c_sinks"][0].partition_broadcast(P))
        yield 0.9
        loads_done(act)
    stage("C load", 6.0, act=c_load)

    def c_rows_pe(pe):
        nc.tensor.matmul(ps[0:8, 2, 0:384], wt(1)[0:32, 0:8], wt(0)[0:32, 0:384], start=True, stop=True)

    def c_rows_dve(dve):
        nc.vector.tensor_tensor(wt(1)[0:8, 128:512], ps[0:8, 2, 0:384], wt(0)[0:8, 384:768], ALU.add)
    stage("C bias rows", 1.0, pe=c_rows_pe)
    stage("C bias rows", 1.0, dve=c_rows_dve)

    def c_skew(act):
        load(act, bias_rows.ap(), wt(1)[0:8, 128:512])
        yield 0.45
        loads_done(act)
        skew = bass.AP(tensor=bias_rows.ap().tensor, offset=0, ap=[[1, P], [384, 8], [1, 256]])
        load(act, wrk[:, 8:10, :].rearrange("p a (h j) -> p (a h) j", h=4), skew)
        yield 0.95
        loads_done(act)
    stage("C skew", 32.0, act=c_skew)

    def c_flip_pe(pe):
        for g in range(4):
            nc.tensor.matmul(ps[:, 4 + g, :], wt(0)[:, 768:896], wt(8 + g // 2, g % 2), start=True, stop=True)

    def c_flip_dve(dve):
        for g in range(4):
            nc.vector.tensor_copy(wt(8 + g // 2, g % 2), ps[:, 4 + g, :])
    stage("C flip", 4.0, pe=c_flip_pe)
    stage("C flipped", 3.0, dve=c_flip_dve)
    fetch("C q k v", [(j, at_cq + j) for j in range(4)] + [(4, at_ckv), (7, at_ckv + 1)], 14.0,
          lambda act: act.wait_ge(b_gated.sem, b_gated.nth(0)))

    def c_v_pe(pe):
        for n in range(8):
            nc.tensor.transpose(ps[:, 4 + n // 4, (n % 4) * P:(n % 4 + 1) * P], wt(7)[:, n * P:(n + 1) * P], ident)

    def c_v_dve(dve):
        nc.vector.tensor_copy(wt(6), ps[:, 4:6, :].rearrange("p a w -> p (a w)"))
    stage("C v turned", 2.0, pe=c_v_pe)
    stage("C v copied", 2.0, dve=c_v_dve)

    def c_attention():
        bias = wrk[:, 8:10, :].rearrange("p a (h j) -> p (a h) j", h=4)
        steps, where = [], []
        for n in range(8):
            for K in range(2):
                units = []
                for t in range(4):
                    rows = slice(64 * K, 64 * K + 64)
                    q = wt(t)[rows, n * P:(n + 1) * P]
                    if n == 0:
                        units.append(Unit([(slice(P, 256), q, wt(4)[rows, 0:P])], bias[:, 4 * K + t, P:256], None))
                    else:
                        sc = [(slice(0, 256), q, wt(4)[rows, (n - 1) * P:(n + 1) * P])]
                        units.append(Unit(sc, bias[:, 4 * K + t, :], None))
                steps.append(units)
                where.append((n, K))
        return steps, where

    c_steps, c_where = c_attention()

    def c_run(name, steps, where, width):
        def pv(pe, s, dst, PB):
            n, K = where[s]
            rows = slice(64 * K, 64 * K + 64)
            blocks = [n] if width == P else [n - 1, n]
            for kb, blk in enumerate(blocks):
                mm = nc.tensor.matmul(dst[rows, :], wt(6)[:, blk * P + 64 * K:blk * P + 64 * K + 64],
                                      PB[:, kb, :, :], start=(kb == 0), stop=(kb == len(blocks) - 1))
            return mm

        def take(s, src):
            n, K = where[s]
            rows = slice(64 * K, 64 * K + 64)
            return nc.vector.tensor_copy(wrk[rows, 0:4, n * P:(n + 1) * P],
                                         src[rows, :].rearrange("p (h c) -> p h c", h=4))
        attention(name, steps, width, 64 ** -0.5, True, True, 5, 7, pv, take,
                  sinks=lambda s: small[:, 304 + 4 * where[s][1]:308 + 4 * where[s][1]])
    c_run("C attention, first block", c_steps[:2], c_where[:2], P)
    c_run("C attention", c_steps[2:], c_where[2:], 256)

    section()
    on("dense")
    for i in range(2):
        r = run(1, lambda _, i=i: cz(i, 0), lambda _, i=i: cz(i, 1))
        gate_z("C z", r, lambda j, b, i=i: wt(2 * i + j, b), lambda j, i=i: col("b_cz", 2 * i + j), 10, 2 * i)
    c_gated = sig.take("c_gated", 1)

    def c_gated_dve(dve):
        nc.vector.engine_nop().then_inc(c_gated.sem, 1)
    stage("C gated", 0.1, dve=c_gated_dve)
    w_c = A["w_br"][0, 2].rearrange("(u k j) n -> u j k n", u=2, j=64)
    merge_c = run(KD, tiles_of(w_in, C_GATE + 2 * D),
                  lambda i: ("rows", [pieces_of(w_c[u])(i) for u in range(2)]), KD, 4)
    merge("C merge", merge_c, lambda i: col("b_gate", 16 + i), False, 10)
    on("aux")

    def d_zero(dve):
        ch = chains["dve"]
        nc.vector.memset(wt(9), 0.0)
        nc.vector.tensor_scalar(small[:, 320:324], cols[:, COL["d_lambda"]:COL["d_lambda"] + 4], -1.0, None, ALU.mult)

    def d_load(act):
        for half, name in ((0, "d_w_a"), (1, "d_w_x")):
            for u in range(2):
                load(act, wt(9, half)[64 * u:64 * u + 64].rearrange("c (t d) -> c t d", t=4)
                     [:, :, 64 * u:64 * u + 64],
                     A[name][0].rearrange("(t u) c d -> u c t d", u=2)[u])
        yield 0.9
        loads_done(act)
    stage("D zero", 2.0, dve=d_zero)
    stage("D load", 6.0, act=d_load)
    fetch("D x", [(4 + j, at_dx + j) for j in range(4)])
    softplus("D softplus", small[:, 320:324], small[:, 324:328], small[:, 328:332], small[:, 332:336],
             small[:, 336:340])

    def d_rate(dve):
        nc.vector.tensor_scalar(small[:, 324:328], small[:, 320:324], -8.0, None, ALU.mult)
        nc.vector.tensor_scalar(small[:, 328:332], small[:, 320:324], 8.0, None, ALU.mult)
    stage("D rate", 20.0, dve=d_rate)

    for i in range(4):
        def dc(dve, i=i):
            if i == 0:
                dve.wait_ge(c_gated.sem, c_gated.nth(0))
            yield from conv(chains["dve"], [wt(4 + i)], [wt(8)], 4, lambda tap, _: col("d_conv_w", tap * 4 + i),
                            lambda _: col("d_conv_b", i))
        stage("D conv", 18.0 if i == 0 else 6.0, dve=dc)

        def dg_pe(pe, i=i):
            for g in range(2):
                for b in range(2):
                    nc.tensor.matmul(ps[:, 2 + 2 * g + b, :], wt(9, g)[:, i * P:(i + 1) * P], wt(8, b),
                                     start=True, stop=True)
        stage("D gates", 4.0, pe=dg_pe)

        def dg_act(act, i=i):
            ch = chains["act"]
            flat = lambda b: ps[:, b:b + 2, :].rearrange("p a w -> p (a w)")
            ch.link(nc.scalar.activation(wt(0), flat(2), ACT.Sigmoid, bias=col("d_b_a", i)))
            nc.scalar.activation(wt(1), flat(4), ACT.Sigmoid, bias=col("d_b_x", i))
            yield 0.4
            nc.scalar.activation(wt(2), wt(0), ACT.Exp, scale=small[:, 324 + i:325 + i])
            nc.scalar.activation(wt(3), wt(0), ACT.Tanh, scale=small[:, 328 + i:329 + i])
        stage("D gate values", 8.0, act=dg_act)

        def dt_dve(dve, i=i):
            ch = chains["dve"]
            ch.link(nc.vector.tensor_scalar(wt(0), wt(3), 1.0, None, ALU.add))
            for b in range(2):
                yield 0.1 + 0.3 * b
                nc.vector.reciprocal(wt(0, b), wt(0, b))
            yield 0.7
            dve.drain()
            nc.vector.scalar_tensor_tensor(wt(3), wt(3), 2.0, wt(0), ALU.mult, ALU.mult)
            nc.vector.tensor_tensor(wt(1), wt(1), wt(8), ALU.mult)
        stage("D input factor", 13.0, dve=dt_dve)

        def dr_act(act):
            nc.scalar.activation(wt(3), wt(3), ACT.Sqrt)
        stage("D root", 3.0, act=dr_act)

        def ds_dve(dve, i=i):
            ch = chains["dve"]
            ch.link(nc.vector.tensor_tensor(wt(1), wt(1), wt(3), ALU.mult))
            nc.vector.tensor_tensor_scan(wt(4 + i), wt(2), wt(1), 0.0, ALU.mult, ALU.add)
        stage("D scan", 4.0, dve=ds_dve)

    def memory_attention(tag, q, kt, vt, spt, ptt, us=0):
        kv = wt(kt).rearrange("p (h m) -> p h m", m=MEM)
        v_t = wt(vt).rearrange("p (m c) -> p m c", m=2)
        steps = [[Unit([(slice(0, 256), wt(q + h)[:, (4 * s4 + u) * P:(4 * s4 + u + 1) * P], kv[:, h, :])],
                       None, None) for u in range(4)] for h in range(4) for s4 in range(2)]

        def pv(pe, s, dst, PB):
            h = s // 2
            for kb in range(2):
                mm = nc.tensor.matmul(dst, v_t[:, kb, h * P:(h + 1) * P], PB[:, kb, :, :],
                                      start=(kb == 0), stop=(kb == 1))
            return mm

        def take(s, src):
            return nc.vector.tensor_copy(wt(q + s // 2, s % 2), src)
        attention(tag + " attention", steps, 256, P ** -0.5, False, True, spt, ptt, pv, take, us=us)

    section()
    on("dense")
    gate_z("D z", run(2, *both(w_in, C_DZ)), lambda j, b: wt(4 + j, b), lambda j: col("b_dz", j), 10)
    d_gated = sig.take("d_gated", 1)

    def d_gated_dve(dve):
        nc.vector.engine_nop().then_inc(d_gated.sem, 1)
    stage("D gated", 0.1, dve=d_gated_dve)
    merge("D merge", merge_run(3), lambda i: col("b_gate", 24 + i), False, 10)
    on("aux")
    fetch("E q", [(j, at_eq + j) for j in range(4)] + [(8, at_kv[0]), (9, at_kv[0] + 1)], 50.0)

    def e_wait(dve):
        dve.wait_ge(d_gated.sem, d_gated.nth(0))
    stage("E scores' tiles", 0.5, dve=e_wait)
    memory_attention("E", 0, 8, 9, 4, 5, us=110.0)

    section()
    on("dense")
    gate_z("E z", run(2, *both(w_in, C_EZ)), wt, lambda j: col("b_ez", j), 10)
    merge("E merge", merge_run(4), lambda i: col("b_gate", 32 + i), False, 10)

    section()
    on("dense")

    def part_acc(dve):
        ch = chains["dve"]
        for k in range(KD):
            ch.link(nc.vector.tensor_copy(h_hi[:, k, :], acc[:, k, :]))
            nc.vector.tensor_tensor(h_lo[:, k, :], acc[:, k, :], h_hi[:, k, :].bitcast(F32), ALU.subtract)
    stage("merged, in parts", dve=part_acc)
    section()
    project("first block out", run(4, *both(weights("w_out"), 0)), acc_at)
    on("aux")

    def x_back(act):
        load(act, wrk[:, 0:8, :], x_fm.rearrange("k p t -> p k t"))
        yield 0.9
        loads_done(act)
    stage("x back", 20.0, act=x_back)
    section()
    on("dense")

    def post(ch, k, b, root):
        y = acc_at(k, b)
        ch.link(nc.vector.scalar_tensor_tensor(y, y, col("g_post", k), root, ALU.mult, ALU.mult))
        ch.link(nc.vector.tensor_tensor(y, y, wt(k, b), ALU.add))
    norm("post norm", acc_at, HALF, post, sq=8, rs=9)


    section()
    norm_acc("even norm", "even_norm_g_2")
    section()
    w2 = weights("even_w_in_2")
    w2o = A["even_w_out_2"][0].rearrange("(b k p) n -> b p k n", b=3, p=P)
    w2kv = weights("even_w_mem_kv_2")

    def r_load(act):
        load(act, wt(0).bitcast(I32)[0:32, :], A["positions_2"][0].partition_broadcast(32))
        loads_done(act)

    TWO_PI_1, TWO_PI_2, TWO_PI_3 = 6.28125, 1.9350051879882812e-03, 3.0199159819210e-07
    ri = wt(1).bitcast(I32)[0:32, :]

    def r_dve(dve):
        ch = chains["dve"]
        a, n, m = wt(2)[0:32, :], wt(3)[0:32, :], wt(4)[0:32, :]
        ch.link(nc.vector.tensor_copy(a, wt(0).bitcast(I32)[0:32, :]))
        ch.link(nc.vector.tensor_scalar(a, a, C("rope")[0:32, 0:1], None, ALU.mult))
        for dst, quarter in ((10, 0.0), (9, 0.25)):
            d = wt(dst)[0:32, :]
            ch.link(nc.vector.tensor_scalar(n, a, 0.15915494309189535, quarter, ALU.mult, ALU.add))
            ch.link(nc.vector.tensor_copy(ri, n))
            ch.link(nc.vector.tensor_copy(n, ri))
            ch.link(nc.vector.scalar_tensor_tensor(d, n, -TWO_PI_1, a, ALU.mult, ALU.add))
            ch.link(nc.vector.scalar_tensor_tensor(d, n, -TWO_PI_2, d, ALU.mult, ALU.add))
            ch.link(nc.vector.scalar_tensor_tensor(d, n, -TWO_PI_3, d, ALU.mult, ALU.add))
            ch.link(nc.vector.tensor_scalar(d, d, quarter * 6.283185307179586, None, ALU.add))
            for bound, op in ((3.14159265, ALU.is_gt), (-3.14159265, ALU.is_lt)):
                ch.link(nc.vector.tensor_scalar(m, d, bound, -6.283185307179586 if bound > 0 else
                                                6.283185307179586, op, ALU.mult))
                ch.link(nc.vector.tensor_tensor(d, d, m, ALU.add))
            ch.link(nc.vector.tensor_scalar(d, d, 3.1415925, -3.1415925, ALU.min, ALU.max))

    def r_sin(act):
        nc.scalar.activation(wt(10)[0:32, :], wt(10)[0:32, :], ACT.Sin)
        nc.scalar.activation(wt(9)[0:32, :], wt(9)[0:32, :], ACT.Sin)

    def r_sign(dve):
        nc.vector.tensor_scalar(wt(10)[0:32, :], wt(10)[0:32, :], C("rope")[0:32, 1:2], None, ALU.mult)
    stage("positions", act=r_load)
    stage("angles", dve=r_dve)
    stage("sines", act=r_sin)
    stage("signed sine", dve=r_sign)

    def rope(tiles):
        def f_pe(pe):
            for j, t in enumerate(tiles):
                for b in range(2):
                    nc.tensor.matmul(ps[0:32, 2 + 2 * j + b, :], C("perm")[0:32, :], wt(t, b)[0:32, :],
                                     start=True, stop=True)

        def f_dve(dve):
            ch = chains["dve"]
            for j, t in enumerate(tiles):
                sw = ps[0:32, 2 + 2 * j:4 + 2 * j, :].rearrange("p a w -> p (a w)")
                x, tmp = wt(t)[0:32, :], wt(7 + j)[0:32, :]
                ch.link(nc.vector.tensor_tensor(tmp, sw, wt(10)[0:32, :], ALU.mult))
                ch.link(nc.vector.tensor_tensor(x, x, wt(9)[0:32, :], ALU.mult))
                nc.vector.tensor_tensor(x, x, tmp, ALU.add)
        stage("rope swap", pe=f_pe)
        stage("rope", dve=f_dve)

    st_m = small[:, 0:24].rearrange("p (g u) -> p g u", g=3)
    st_d = small[:, 24:48].rearrange("p (g u) -> p g u", g=3)

    def dilated_head(h):
        cq2 = lambda g: g * 2 * W + h * P
        ck2 = lambda g: g * 2 * W + W + h * P
        one = lambda c: tiles_of(w2, c)
        r_a = run(1, one(C2_V + h * P), one(cq2(0)))
        r_b = run(1, one(ck2(0)), one(cq2(1)))
        r_c = run(1, one(ck2(1)), one(cq2(2)))
        r_d = run(1, one(ck2(2)), one(C2_Z + h * P))
        project("v q0", r_a, lambda j, b: wt((4, 0)[j], b))
        project("k0 q1", r_b, lambda j, b: wt((3, 1)[j], b))
        rope([0, 3])
        dilated_group(h, 0)
        project("k1 q2", r_c, lambda j, b: wt((3, 2)[j], b))
        rope([1, 3])
        dilated_group(h, 1)

        def f_pe(pe):
            return dense_run(pe, r_d, rhs_h, rhs_h)

        def f_act(act):
            for b in range(2):
                out_ready(act, r_d.t0, b)
                nc.scalar.activation(wt(3, b), ps[:, b, :], ACT.Copy).then_inc(dense_free[b], 1)
            for b in range(2):
                out_ready(act, r_d.t0 + 1, b)
                nc.scalar.activation(wt(6, b), ps[:, b, :], ACT.Silu).then_inc(dense_free[b], 1)
        stage("k2 z", pe=f_pe, act=f_act)
        rope([2, 3])
        dilated_group(h, 2)
        dilated_join(h)

    def token_view(ap, g):
        if g == 0:
            return ap.rearrange("p (u i) -> p u i", i=P)
        if g == 1:
            return ap.rearrange("p (n i r) -> p r n i", n=2, r=4)
        return ap.rearrange("p (i r) -> p r i", r=16)

    def queries(t, g, u):
        v = token_view(wt(t), g)
        if g == 0:
            return v[:, u, :]
        if g == 1:
            return v[:, u // 2, u % 2, :]
        return v[:, 2 * u:2 * u + 2, :]

    def dilated_group(h, g):
        def vt_pe(pe):
            for u in range(8):
                src = queries(4, g, u)
                if g == 2:
                    src = wt(7)[:, u * P:(u + 1) * P]
                nc.tensor.transpose(ps[:, 2 + u // 4, (u % 4) * P:(u % 4 + 1) * P], src, ident)

        def vt_dve(dve):
            nc.vector.tensor_copy(wt(5), ps[:, 2:4, :].rearrange("p a w -> p (a w)"))
        if g == 2:
            def regroup(dve):
                ch = chains["dve"]
                for t in (4, 2, 3):
                    ch.link(nc.vector.tensor_copy(wt(7).rearrange("p (r i) -> p r i", r=16), token_view(wt(t), 2)))
                    if t != 4:
                        ch.link(nc.vector.tensor_copy(wt(t), wt(7)))
            def regroup2(dve):
                ch = chains["dve"]
                for t in (2, 3):
                    ch.link(nc.vector.tensor_copy(wt(7).rearrange("p (r i) -> p r i", r=16), token_view(wt(t), 2)))
                    ch.link(nc.vector.tensor_copy(wt(t), wt(7)))
                ch.link(nc.vector.tensor_copy(wt(7).rearrange("p (r i) -> p r i", r=16), token_view(wt(4), 2)))
            stage("by residue", dve=regroup2)
        stage("v turned", pe=vt_pe)
        stage("v copied", dve=vt_dve)
        steps = []
        for s in range(2):
            units = []
            for u in range(4 * s, 4 * s + 4):
                if g == 2:
                    q, k = (wt(t)[:, u * P:(u + 1) * P] for t in (2, 3))
                    units.append(Unit([(slice(P, 256), q, k)], C("pair"), None))
                    continue
                q = queries(g, g, u)
                first = u == 0 if g == 0 else u % 2 == 0
                if first:
                    k = queries(3, g, u)
                    sc = [(slice(0, P), q, k), (slice(P, 256), q, k)]
                else:
                    sc = [(slice(0, P), q, queries(3, g, u - 1)), (slice(P, 256), q, queries(3, g, u))]
                units.append(Unit(sc, C("bandfirst") if first else C("band"), None))
            steps.append(units)
        width = P if g == 2 else 256

        def pv(pe, s, dst, PB):
            for u4 in range(4):
                u = 4 * s + u4
                first = u == 0 if g == 0 else u % 2 == 0
                blocks = [u] if g == 2 else [u if first else u - 1, u]
                for kb, blk in enumerate(blocks):
                    mm = nc.tensor.matmul(dst[:, u4 * P:(u4 + 1) * P], wt(5)[:, blk * P:(blk + 1) * P],
                                          PB[:, kb, u4, :], start=(kb == 0), stop=(kb == len(blocks) - 1))
            return mm

        def take(s, src):
            if g == 0:
                return nc.vector.tensor_copy(wt(0, s), src)
            if g == 1:
                return nc.vector.tensor_copy(token_view(wt(1), 1)[:, 2 * s:2 * s + 2],
                                             src.rearrange("p (r n i) -> p r n i", r=2, n=2))
            return nc.vector.tensor_copy(wt(2, s), src)
        attention(f"dilated {g}", steps, width, P ** -0.5, True, False, 7, 8, pv, take,
                  stats=lambda s: (st_m[:, g, 4 * s:4 * s + 4], st_d[:, g, 4 * s:4 * s + 4]))

    def spread(which, g):
        for u in range(8):
            nc.tensor.matmul(ps[:, 2 + 2 * g + u // 4, (u % 4) * P:(u % 4 + 1) * P],
                             which[:, g, u:u + 1].to_broadcast([P, P]), ident, start=True, stop=True)

    def dilated_join(h):
        def m_pe(pe):
            for g in range(3):
                spread(st_m, g)

        def grouped(g):
            flat = ps[:, 2 + 2 * g:4 + 2 * g, :].rearrange("p a w -> p (a w)")
            if g == 0:
                return flat
            if g == 1:
                return flat.rearrange("p (r n i) -> p r n i", r=4, n=2)
            return flat.rearrange("p (r i) -> p r i", r=16)

        def tok(t, g):
            return wt(t) if g == 0 else token_view(wt(t), g)

        def parts(g):
            if g == 1:
                return [(lambda ap, n=n: ap[:, :, n, :]) for n in range(2)]
            return [lambda ap: ap]

        def m_dve(dve):
            ch = chains["dve"]
            for g in range(3):
                for cut in parts(g):
                    ch.link(nc.vector.tensor_copy(cut(tok((3, 4, 5)[g], g)), cut(grouped(g))))
            ch.link(nc.vector.tensor_tensor(wt(7), wt(3), wt(4), ALU.max))
            ch.link(nc.vector.tensor_tensor(wt(7), wt(7), wt(5), ALU.max))
            for t in (3, 4, 5):
                ch.link(nc.vector.tensor_tensor(wt(t), wt(t), wt(7), ALU.subtract))
            ch.link(nc.vector.tensor_copy(wt(8), wt(2)))
            ch.link(nc.vector.tensor_copy(token_view(wt(2), 2), wt(8).rearrange("p (r i) -> p r i", r=16)))

        def w_act(act):
            for t in (3, 4, 5):
                nc.scalar.activation(wt(t), wt(t), ACT.Exp)

        def d_pe(pe):
            for g in range(3):
                spread(st_d, g)

        def d_dve(dve):
            ch = chains["dve"]
            for g in range(3):
                t = (7, 8, 8)[g]
                for cut in parts(g):
                    ch.link(nc.vector.tensor_tensor(cut(tok(t, g)), cut(grouped(g)), cut(tok((3, 4, 5)[g], g)), ALU.mult))
                if g:
                    ch.link(nc.vector.tensor_tensor(wt(7), wt(7), wt(8), ALU.add))
            ch.link(nc.vector.reciprocal(wt(7), wt(7)))
            ch.link(nc.vector.tensor_tensor(wt(7), wt(7), wt(6), ALU.mult))
            for g in range(3):
                ch.link(nc.vector.tensor_tensor(wt(g), wt(g), wt(3 + g), ALU.mult))
            ch.link(nc.vector.tensor_tensor(wt(0), wt(0), wt(1), ALU.add))
            ch.link(nc.vector.tensor_tensor(wt(0), wt(0), wt(2), ALU.add))
            ch.link(nc.vector.tensor_tensor(wt(0), wt(0), wt(7), ALU.mult))
            ch.link(nc.vector.tensor_copy(y_hi[:, h, :], wt(0)))
            nc.vector.tensor_tensor(y_lo[:, h, :], wt(0), y_hi[:, h, :].bitcast(F32), ALU.subtract)
        stage("maxima spread", pe=m_pe)
        stage("joint maximum", dve=m_dve)
        stage("group weights", act=w_act, pe=d_pe)
        stage("join", dve=d_dve)

    for h in range(4):
        dilated_head(h)
    add_out("even out A", run(4, *both(w2o[0], 0), 4, 4))

    project("pool x", run(2, *both(w2, C2_X)), to_tiles(0))

    def p_load(act):
        load(act, wt(10)[:, 0:HALF].rearrange("p (g d) -> p g d", g=4),
             A["even_w_pool_2"][0].rearrange("g c d -> c g d"))
        loads_done(act)

    def p_dve(dve):
        ch = chains["dve"]
        for i in range(4):
            src, s = wt(i), 1
            for lv in range(i + 1):
                dst = wt(5 + (lv % 2))
                ch.link(nc.vector.tensor_copy(dst[:, 0:s], src[:, 0:s]))
                ch.link(nc.vector.tensor_tensor(dst[:, s:T], src[:, s:T], src[:, 0:T - s], ALU.add))
                src, s = dst, 2 * s
            ch.link(nc.vector.tensor_tensor(small[:, 64:80], src[:, 0:16], C("icount")[:, 16 * i:16 * i + 16], ALU.mult))
            ch.link(nc.vector.tensor_tensor(small[:, 64:80], small[:, 64:80], wt(i)[:, 0:16], ALU.subtract))
            ch.link(nc.vector.scalar_tensor_tensor(wt(i), src, 1.0 / s, wt(i), ALU.mult, ALU.subtract))
            ch.link(nc.vector.tensor_copy(wt(i)[:, 0:16], small[:, 64:80]))
    stage("pool sums", act=p_load, dve=p_dve)
    pooled = sig.take("pool_out", 8)
    ptaken = sig.take("pool_taken", 8)

    def p_pe(pe):
        for i in range(8):
            if i >= 4:
                pe.wait_ge(ptaken.sem, ptaken.nth(i - 4))
            nc.tensor.matmul(ps[:, 2 + i % 4, :], wt(10)[:, (i // 2) * P:(i // 2 + 1) * P], wt(i // 2, i % 2),
                             start=True, stop=True).then_inc(pooled.sem, 1)

    def p_act(act):
        for i in range(8):
            act.wait_ge(pooled.sem, pooled.nth(i))
            nc.scalar.activation(wt(i // 2, i % 2), ps[:, 2 + i % 4, :], ACT.Copy,
                                 scale=col("even_pool_scale_2", i // 2)).then_inc(ptaken.sem, 1)
    stage("pool mix", pe=p_pe, act=p_act)
    gate_z("pool z", run(2, *both(w2, C2_Z + W)), wt, None, 4)
    add_out("even out B", run(4, *both(w2o[1], 0), 4, 4))

    project("even q", run(2, *both(w2, C2_Q)), to_tiles(0))
    fetch("even k v", [(8, at_kv[1]), (9, at_kv[1] + 1)])
    memory_attention("even", 0, 8, 9, 4, 5)
    gate_z("even memory z", run(2, *both(w2, C2_Z + 2 * W)), wt, None, 4)
    add_out("even out M", run(4, *both(w2o[2], 0), 4, 4))

    norm_acc("odd norm", "odd_norm_g_2")
    section()
    w3 = weights("odd_w_in_2")
    w3o = A["odd_w_out_2"][0].rearrange("(b k p) n -> b p k n", b=3, p=P)
    project("odd v", run(4, *both(w3, C3_V)), to_tiles(0))
    layer_norm("odd ln", lambda k, b: wt(k, b), KD, D, lambda k: col("odd_ln_g_2", k), (8, 9),
               lambda k, b: nc.scalar.activation(wt(k, b), wt(k, b), ACT.Identity, bias=col("odd_ln_b_2", k)))

    def s_load(act):
        load(act, wt(8).rearrange("p (g s) -> p g s", g=8), A["odd_w_s_2"][0].rearrange("g t s -> t g s"))
        load(act, wt(10).rearrange("p (g s) -> p g s", g=8), A["odd_b_s_2"][0].partition_broadcast(P))
        loads_done(act)

    def s_pe(pe):
        for g in range(8):
            nc.tensor.transpose(ps[:, 2 + g // 4, (g % 4) * P:(g % 4 + 1) * P], wt(8)[:, g * P:(g + 1) * P], ident)

    def s_dve(dve):
        nc.vector.tensor_tensor(wt(9).rearrange("p (g t) -> p g t", g=8),
                                ps[:, 2:4, :].rearrange("p a (g t) -> p (a g) t", g=4),
                                C("upto").unsqueeze(1).to_broadcast([P, 8, P]), ALU.mult)
    stage("mix load", act=s_load)
    stage("mix turned", pe=s_pe)
    stage("mix masked", dve=s_dve)

    vturned = sig.take("sg_turned", 8)
    vcopied = sig.take("sg_copied", 8)
    smixed = sig.take("sg_mixed", 8)
    sadded = sig.take("sg_added", 8)

    def g_pe(pe):
        for g in range(8):
            if g >= 1:
                pe.wait_ge(vcopied.sem, vcopied.nth(g - 1))
            for n in range(8):
                mm = nc.tensor.transpose(ps[:, 2 + n // 4, (n % 4) * P:(n % 4 + 1) * P], wt(g)[:, n * P:(n + 1) * P], ident)
            mm.then_inc(vturned.sem, 1)
            pe.wait_ge(vcopied.sem, vcopied.nth(g))
            if g >= 1:
                pe.wait_ge(sadded.sem, sadded.nth(g - 1))
            for n in range(8):
                mm = nc.tensor.matmul(ps[:, 4 + n // 4, (n % 4) * P:(n % 4 + 1) * P], wt(8)[:, n * P:(n + 1) * P],
                                      wt(9)[:, g * P:(g + 1) * P], start=True, stop=True)
            mm.then_inc(smixed.sem, 1)

    def g_act(act):
        for g in range(8):
            act.wait_ge(vturned.sem, vturned.nth(g))
            if g >= 1:
                act.wait_ge(smixed.sem, smixed.nth(g - 1))
            nc.scalar.activation(wt(8), ps[:, 2:4, :].rearrange("p a w -> p (a w)"), ACT.Copy).then_inc(vcopied.sem, 1)

    def g_dve(dve):
        for g in range(8):
            dve.wait_ge(smixed.sem, smixed.nth(g))
            nc.vector.tensor_tensor(wt(g).rearrange("p (n t) -> p n t", n=8),
                                    ps[:, 4:6, :].rearrange("p a (n t) -> p (a n) t", n=4),
                                    wt(10)[:, g * P:(g + 1) * P].unsqueeze(1).to_broadcast([P, 8, P]),
                                    ALU.add).then_inc(sadded.sem, 1)
    stage("mix", pe=g_pe, act=g_act, dve=g_dve)

    r_u = run(4, *both(w3, C3_U))

    def u_pe(pe):
        return dense_run(pe, r_u, rhs_h, rhs_h)

    def u_dve(dve):
        for j in range(8):
            for b in range(2):
                out_ready(dve, r_u.t0 + j, b)
                nc.vector.tensor_tensor(wt(j, b), wt(j, b), ps[:, b, :], ALU.mult).then_inc(dense_free[b], 1)
    stage("odd u", pe=u_pe, dve=u_dve)
    for part in range(2):
        gate_z("odd z", run(2, *both(w3, C3_Z + part * W)), lambda j, b, part=part: wt(4 * part + j, b), None, 8)
        add_out("odd out", run(4, *both(w3o[part], 0), 4, 4))
    project("odd q", run(2, *both(w3, C3_Q)), to_tiles(0))
    fetch("odd k v", [(8, at_kv[2]), (9, at_kv[2] + 1)])
    memory_attention("odd", 0, 8, 9, 4, 5)
    gate_z("odd memory z", run(2, *both(w3, C3_Z + 2 * W)), wt, None, 4)
    add_out("odd out M", run(4, *both(w3o[2], 0), 4, 4))

    def last(ch, k, b, root):
        y = acc_at(k, b)
        ch.link(nc.vector.scalar_tensor_tensor(y, y, col("final_norm_g_2", k), root, ALU.mult, ALU.mult))
    norm("final norm", acc_at, HALF, last, sq=8, rs=9)
    oturned = sig.take("out_turned", KD)
    ocopied = sig.take("out_copied", KD)

    def o_pe(pe):
        for k in range(KD):
            if k >= 2:
                pe.wait_ge(ocopied.sem, ocopied.nth(k - 2))
            for n in range(8):
                mm = nc.tensor.transpose(ps[:, 2 + 2 * (k % 2) + n // 4, (n % 4) * P:(n % 4 + 1) * P],
                                         acc[:, k, n * P:(n + 1) * P], ident)
            mm.then_inc(oturned.sem, 1)

    def o_dve(dve):
        for k in range(KD):
            dve.wait_ge(oturned.sem, oturned.nth(k))
            b = 2 + 2 * (k % 2)
            nc.vector.tensor_copy(wrk[:, 0:8, k * P:(k + 1) * P],
                                  ps[:, b:b + 2, :].rearrange("p a (n d) -> p (a n) d", n=4)).then_inc(ocopied.sem, 1)
    stage("out turned", pe=o_pe, dve=o_dve)

    def o_store(act):
        load(act, out[0].rearrange("(n p) d -> p n d", p=P), wrk[:, 0:8, :])
        loads_done(act)
    stage("out", act=o_store)


    stage_done = {(t, e): sig.sem(f"{t}_{e}_stage_done") for t in ("dense", "aux", "side") for e in engines}
    done_before = {k: 0 for k in stage_done}
    plans = []
    for sec in sections:
        plan = {}
        for t, row in sec.items():
            start, plan[t] = 0.0, []
            for name, us, fns, ahead in row:
                waits = {e: done_before[t, e] for e in engines}
                plan[t].append((start, us, fns, ahead, waits))
                for e in fns:
                    done_before[t, e] += 1
                start += us
        plans.append(plan)

    def thread_part(name, eng, t, row):
        for start, us, fns, ahead, waits in row:
            if name not in fns:
                continue
            yield start
            for other in engines:
                if other != name and waits[other] and name not in ahead:
                    eng.wait_ge(stage_done[t, other], waits[other])
            parts = fns[name](eng)
            if parts is not None:
                for fraction in parts:
                    yield start + fraction * us
            eng.drain().then_inc(stage_done[t, name], 1)

    def play(name, eng):
        chains[name] = Chain(eng, f"{name}_chain")
        for n, plan in enumerate(plans):
            threads = [thread_part(name, eng, t, row) for t, row in plan.items()]
            due = [next(th, None) for th in threads]
            while any(d is not None for d in due):
                i = min((d, i) for i, d in enumerate(due) if d is not None)[1]
                due[i] = next(threads[i], None)
            eng.drain().then_inc(at_end[name], 1)
            for other in engines:
                if other != name:
                    eng.wait_ge(at_end[other], n + 1)

    block = ctx.enter_context(nc.Block())

    @block.sync
    def _(sp):
        def load_tile(slot_, nk, src):
            if not isinstance(src, tuple):
                sp.dma_start(w_raw[:, slot_, 0:nk, :], src).then_inc(raw_loaded[slot_], 32)
                return
            kind, pieces = src
            for u, piece in enumerate(pieces):
                dst = w_raw[:, slot_, 0:nk, 64 * u:64 * u + 64] if kind == "columns" else \
                    w_raw[64 * u:64 * u + 64, slot_, 0:nk, :]
                sp.dma_start(dst, piece).then_inc(raw_loaded[slot_], 16)

        for r in runs:
            def body(i, r=r):
                for p in range(min(2, r.n)):
                    t, src = r.t(i, p), r.src[p](i)
                    if not isinstance(t, int) or t >= 2:
                        sp.wait_ge(tiles_split, t - 1)
                    load_tile(r.t(0, p) % 2, r.nk[p], src)
            if r.n <= 2:
                body(0)
            elif r.t0 < 2:
                body(0)
                with sp.Fori(2, r.pairs + 1, 1) as i:
                    body(i - 1)
            else:
                with sp.Fori(1, r.pairs + 1, 1) as i:
                    body(i - 1)

    @block.gpsimd
    def _(pool):
        def split(t, s, raw_count):
            pool.wait_ge(raw_loaded[s], raw_count)
            nc.gpsimd.tensor_tensor(w_hi[:, s], w_raw[:, s], one, ALU.mult).then_inc(hi_ready, 1)
            pool.wait_ge(hi_ready, t + 2)
            nc.gpsimd.tensor_tensor(w_lo[:, s], w_raw[:, s], w_hi[:, s].bitcast(F32),
                                    ALU.subtract).then_inc(tiles_split, 1)
        hi_ready = sig.sem("hi_ready")
        nc.gpsimd.memset(pool_one[:], 1.0).then_inc(hi_ready, 1)
        pool.wait_ge(hi_ready, 1)
        one = pool_one[:].unsqueeze(2).to_broadcast([P, KD, P])
        for s in range(2):
            split(s, s, 32)
        with pool.Fori(1, ntiles // 2, 1) as i:
            for s in range(2):
                pool.wait_ge(dense_out, 2 * (2 * i + s) - 2)
                split(2 * i + s, s, 32 * i + 32)
        if ntiles % 2:
            pool.wait_ge(dense_out, 2 * (ntiles - 1) - 2)
            split(ntiles - 1, 0, 32 * (ntiles // 2) + 32)

    @block.scalar
    def _(act):
        play("act", act)

    @block.vector
    def _(dve):
        for b in range(2):
            nc.vector.engine_nop().then_inc(dense_free[b], 1)
        play("dve", dve)

    @block.tensor
    def _(pe):
        play("pe", pe)


_OUT = (1, T, D)


def kernel(**inputs):
    import concourse.bacc as _bacc
    from concourse.bass_utils import run_bass_kernel_spmd as _run

    nc = _bacc.Bacc("TRN2", target_bir_lowering=False, num_devices=1)
    arrays = {k: np.ascontiguousarray(v) for k, v in inputs.items()}
    arrays["consts"] = np.ascontiguousarray(constants()[0])
    arrays["bias_consts"] = bias_parts()
    A = {k: nc.dram_tensor(f"in_{k}", v.shape, mybir.dt.from_np(v.dtype), kind="ExternalInput").ap()
         for k, v in arrays.items()}
    out = nc.dram_tensor("out", _OUT, F32, kind="ExternalOutput").ap()
    hybrid_program(nc, A, out)
    r = _run(nc, [{f"in_{k}": v for k, v in arrays.items()}], core_ids=[0])
    return r.results[0]["out"]
```

```python
from contextlib import ExitStack

import numpy as np
import concourse.bass as bass
from concourse import mybir

F32 = mybir.dt.float32
F32R = mybir.dt.float32r
I32 = mybir.dt.int32
ACT = mybir.ActivationFunctionType
ALU = mybir.AluOpType
AX = mybir.AxisListType.X

P = 128
T = 1024
D = 1024
KD = D // P
HALF = 512
W = 512
MEM = 256
NEG = -1.0e30
EPS = 1e-6

C_AQKV, C_AZ, C_BA = 0, 1536, 2048
C_GLU, C_BZ = 2056, 3080
C_CQ, C_CKV, C_CZ = 3592, 4104, 4360
C_DX, C_DZ, C_EQ, C_EZ, C_GATE = 4872, 5384, 5896, 6408, 6920
C2_V, C2_X, C2_Q, C2_Z = 3072, 3584, 4096, 4608
C3_U, C3_V, C3_Q, C3_Z = 0, 1024, 2048, 2560

REL_BUCKETS, REL_MAX_DIST, WINDOW = 32, 128, 128
NLEVEL = 7
CHUNK_TIME = 70.0
ATT_TIME = 20.0
A_PACE = 0.6
B_PACE = 1.85
C_PACE = 1.3
D_PACE = 0.8
HEAD_PACE = 1.3
E_ATT_TIME = 90.0
AHEAD_PACE = 2.0


def bucket_of(dist):
    n = np.maximum(dist, 0)
    exact = REL_BUCKETS // 2
    large = exact + (np.log(np.maximum(n, 1) / exact) / np.log(REL_MAX_DIST / exact)
                     * (REL_BUCKETS - exact)).astype(np.int32)
    return np.where(n < exact, n, np.minimum(large, REL_BUCKETS - 1))


def constant_parts():
    i = np.arange(P)[:, None]
    j = np.arange(P)[None, :]
    c = {}
    c["ident"] = (i == j)
    c["ones"] = np.ones((P, P))
    c["upto"] = (i <= j)
    c["negafter"] = np.where(i > j, NEG, 0.0)
    for lv in range(NLEVEL):
        s = 1 << lv
        c[f"lev{lv}"] = ((i // (2 * s)) == (j // (2 * s))) & ((i // s) % 2 == 0) & ((j // s) % 2 == 1)
    k2 = np.arange(2 * P)[None, :]
    ok = (k2 >= i) & (k2 <= i + P)
    c["band"] = np.where(ok, 0.0, NEG)
    c["bandfirst"] = np.where(ok & (k2 >= P), 0.0, NEG)
    c["pair"] = np.where(((i // 64) == (j // 64)) & (j <= i), 0.0, NEG)
    inv = np.zeros((P, 2))
    inv[:32, 0] = np.tile(500000.0 ** (-np.arange(0, 32, 2, dtype=np.float32) / np.float32(32)), 2)
    inv[:32, 1] = np.where(np.arange(32) < 16, -1.0, 1.0)
    c["rope"] = inv
    c["icount"] = np.broadcast_to(np.concatenate(
        [1.0 / np.minimum(np.arange(16) + 1, w) for w in (2, 4, 8, 16)])[None], (P, 64))
    return {k: np.ascontiguousarray(np.asarray(v, np.float32)) for k, v in c.items()}


def bias_parts():
    pos = np.arange(384)
    dist = 255 - pos
    ok = (dist >= 0) & (dist < WINDOW)
    hot = np.zeros((P, 384), np.float32)
    hot[bucket_of(dist)[ok], pos[ok]] = 1.0
    mask = np.zeros((P, 384), np.float32)
    mask[:8] = np.where(ok, 0.0, NEG)
    flip = np.eye(P, dtype=np.float32)[::-1]
    return np.ascontiguousarray(np.concatenate([hot, mask, flip], axis=1))


def constants():
    parts = constant_parts()
    at, n = {}, 0
    for k, v in parts.items():
        at[k] = (n, v.shape[1])
        n += v.shape[1]
    return np.concatenate(list(parts.values()), axis=1), at, n


class Event:
    def __init__(self, sem, base):
        self.sem, self.base = sem, base

    def nth(self, i):
        return self.base + i + 1


class Signals:
    def __init__(self, nc, ctx):
        self.nc, self.ctx, self.sems, self.next = nc, ctx, {}, {}

    def sem(self, name):
        if name not in self.sems:
            self.sems[name] = self.ctx.enter_context(self.nc.semaphore(name))
            self.next[name] = 0
        return self.sems[name]

    def take(self, name, n):
        sem = self.sem(name)
        base = self.next[name]
        self.next[name] = base + n
        return Event(sem, base)


class Run:
    def __init__(self, t0, n, src, nk):
        self.t0, self.n, self.src, self.nk = t0, n, src, nk
        self.pairs = n // 2

    def t(self, i, p):
        return self.t0 + 2 * i + p


def rows128(v):
    return v.rearrange("(n p) -> n p", p=P)


def hybrid_program(nc, A, out):
    ctx = ExitStack()
    with ctx:
        _hybrid(nc, ctx, A, out)


def _hybrid(nc, ctx, A, out):
    def sb(name, shape, dt=F32):
        return ctx.enter_context(nc.sbuf_tensor(name, shape, dt))

    sig = Signals(nc, ctx)
    _, CAT, NCONST = constants()

    h_hi = sb("h_hi", [P, KD, T], F32R)
    h_lo = sb("h_lo", [P, KD, T], F32R)
    y_hi = sb("y_hi", [P, 4, T], F32R)
    y_lo_at = nc.sbuf_base
    y_lo = sb("y_lo", [P, 4, T], F32R)
    y_spare = nc.alloc_sbuf_tensor_at("y_spare", [P, 4, T], F32, offset=y_lo_at)
    acc = sb("acc", [P, KD, T])
    w_raw = sb("w_raw", [P, 2, KD, P])
    w_hi = sb("w_hi", [P, 2, KD, P], F32R)
    w_lo = sb("w_lo", [P, 2, KD, P], F32R)
    wrk = sb("wrk", [P, 11, T])
    cst = sb("cst", [P, NCONST])
    cols = sb("cols", [P, 392])
    small = sb("small", [P, 344])
    pool_one = sb("pool_one", [P, 1])
    ps = ctx.enter_context(nc.psum_tensor("ps", [P, 8, HALF], F32))
    x_fm = nc.dram_tensor("x_fm", [KD, P, T], F32, kind="Internal").ap()
    bias_rows = nc.dram_tensor("bias_rows", [8, 384], F32, kind="Internal")

    def C(name):
        a, n = CAT[name]
        return cst[:, a:a + n]

    ident, ones = C("ident"), C("ones")

    def wt(j, half=None):
        return wrk[:, j, :] if half is None else wrk[:, j, half * HALF:(half + 1) * HALF]

    b_in = A["b_in"][0]
    segs = []

    def seg(name, ap):
        segs.append((name, ap))

    seg("b_aqkv", rows128(b_in[C_AQKV:C_AZ]))
    seg("b_az", rows128(b_in[C_AZ:C_BA]))
    seg("b_ba", rows128(b_in[C_BA:C_BA + P]))
    seg("b_glu", rows128(b_in[C_GLU:C_BZ]))
    seg("b_bz", rows128(b_in[C_BZ:C_CQ]))
    seg("b_cq", b_in[C_CQ:C_CKV].rearrange("(u t j) -> t u j", u=2, j=64))
    seg("b_ckv", rows128(b_in[C_CKV:C_CZ]))
    seg("b_cz", b_in[C_CZ:C_DX].rearrange("(u t j) -> t u j", u=2, j=64))
    seg("b_dx", rows128(b_in[C_DX:C_DZ]))
    seg("b_dz", rows128(b_in[C_DZ:C_EQ]))
    seg("b_eq", rows128(b_in[C_EQ:C_EZ]))
    seg("b_ez", rows128(b_in[C_EZ:C_GATE]))
    seg("b_gate", rows128(b_in[C_GATE:C_GATE + 5 * D]))
    for name in ("g_pre", "g_post", "g_mem", "b_dw_b", "b_ln_g", "b_ln_b", "d_conv_b", "d_b_a", "d_b_x",
                 "d_lambda", "a_norm_g", "even_norm_g_2", "odd_norm_g_2", "even_pool_scale_2",
                 "odd_ln_g_2", "odd_ln_b_2"):
        seg(name, rows128(A[name][0]))
    seg("g_mem_2", rows128(A["g_mem_2"]))
    seg("final_norm_g_2", rows128(A["final_norm_g_2"]))
    for name in ("a_conv_w", "d_conv_w", "b_dw_w"):
        seg(name, A[name][0].rearrange("k (n p) -> (k n) p", p=P))
    COL, nrows = {}, 0
    row_loads = []
    for name, ap in segs:
        COL[name] = nrows
        n, done = ap.shape[0], 0
        while done < n:
            k = min(n - done, P - nrows % P)
            row_loads.append((nrows // P, nrows % P, k, ap[done:done + k]))
            done += k
            nrows += k
    TABLE_ROWS = [min(P, nrows - P * j) for j in range(-(-nrows // P))]
    assert nrows <= 392, nrows

    def col(name, i=0):
        j = COL[name] + i
        return cols[:, j:j + 1]

    raw_loaded = [sig.sem(f"raw_loaded{s}") for s in range(2)]
    tiles_split = sig.sem("tiles_split")
    dense_out = sig.sem("dense_out")
    dense_free = [sig.sem(f"dense_free{b}") for b in range(2)]
    runs, ntiles = [], 0

    def run(pairs, src0, src1, nk0=KD, nk1=KD):
        nonlocal ntiles
        r = Run(ntiles, 2 * pairs, (src0, src1), (nk0, nk1))
        runs.append(r)
        ntiles += 2 * pairs
        return r

    def run_one(src):
        nonlocal ntiles
        r = Run(ntiles, 1, (src, None), (KD, KD))
        runs.append(r)
        ntiles += 1
        return r

    def weights(name, layer=0):
        w = A[name]
        w = w[layer] if len(w.shape) == 3 else w
        return w.rearrange("(k p) n -> p k n", p=P)

    def tiles_of(w, first, step=P):
        return lambda i: w[:, :, bass.ds(i * step + first, P)] if not isinstance(i, int) \
            else w[:, :, first + i * step:first + i * step + P]

    def both(w, first):
        return tiles_of(w, first, 2 * P), tiles_of(w, first + P, 2 * P)

    def rhs_h(part, k, b):
        return (h_hi, h_lo)[part][:, k, b * HALF:(b + 1) * HALF]

    def rhs_y(part, k, b):
        return (y_hi, y_lo)[part][:, k, b * HALF:(b + 1) * HALF]

    def mem_view(t, which):
        return t[:, 2 * which:2 * which + 2, :].rearrange("p a (b m) -> p (a b) m", m=MEM)

    def rhs_of_memory(which):
        return lambda part, k, b: mem_view((y_hi, y_lo)[part], which)[:, k, b * P:(b + 1) * P]
    keys_of = [rhs_of_memory(0), rhs_of_memory(1)]
    values_of = [rhs_of_memory(0), rhs_of_memory(1)]
    weights_moving = values_of

    engines = ("pe", "act", "dve")
    at_end = {e: sig.sem(f"{e}_at_section_end") for e in engines}
    sections = []

    def section():
        sections.append({"dense": [], "aux": [], "side": []})

    thread_now = ["dense"]

    def on(thread):
        thread_now[0] = thread

    def stage(name, us=5.0, ahead=(), **fns):
        sections[-1][thread_now[0]].append((name, us, fns, ahead))

    class Chain:
        def __init__(self, eng, name):
            self.eng, self.sem, self.n = eng, sig.sem(name), 0

        def link(self, ins):
            self.eng.wait_ge(self.sem, self.mark(ins))

        def mark(self, ins):
            self.n += 1
            ins.then_inc(self.sem, 1)
            return self.n

        def after(self, n):
            self.eng.wait_ge(self.sem, n)

    chains = {}

    def dense_half(pe, t, b, slot, nk, rhs, n, ready=None):
        pe.wait_ge(dense_free[b], t + 1)
        for k in range(nk):
            if k and k % 2 == 0:
                yield k / nk
            if ready:
                ready(pe, k, b)
            for q, (w, part) in enumerate(((w_hi, 0), (w_hi, 1), (w_lo, 0))):
                l, r = w[:, slot, k, :], rhs(part, k, b)
                if rhs in weights_moving:
                    l, r = r, l
                mm = nc.tensor.matmul(ps[:, b, 0:n], l, r, start=(k == 0 and q == 0),
                                      stop=(k == nk - 1 and q == 2))
        mm.then_inc(dense_out, 1)

    def when(r, j, b):
        done = sum(r.nk[q % 2] for q in range(j)) + r.nk[j % 2] * (b + 1) / 2
        return done / sum(r.nk[q % 2] for q in range(r.n))

    def dense_run(pe, r, rhs0, rhs1, n=HALF, ready=None):
        total, done = 2 * sum(r.nk[j % 2] for j in range(r.n)), 0
        for j in range(r.n):
            pe.wait_ge(tiles_split, r.t0 + j + 1)
            for b in range(2):
                yield done / total
                for part in dense_half(pe, r.t0 + j, b, (r.t0 + j) % 2, r.nk[j % 2], (rhs0, rhs1)[j % 2], n,
                                       ready if j == 0 else None):
                    yield (done + part * r.nk[j % 2]) / total
                done += r.nk[j % 2]

    def out_ready(eng, t, b):
        eng.wait_ge(dense_out, 2 * t + b + 1)

    def out_taken(eng, t, b):
        eng.wait_ge(dense_free[b], t + 2)

    def project(name, r, dst, bias=None, rhs=None, n=HALF, before=None, ready=None):
        def f_pe(pe):
            return dense_run(pe, r, rhs or rhs_h, rhs or rhs_h, n, ready)

        def f_act(act):
            for j in range(r.n):
                for b in range(2):
                    yield when(r, j, b)
                    if before:
                        before(act, j, b)
                    out_ready(act, r.t0 + j, b)
                    if bias is None:
                        nc.scalar.activation(dst(j, b), ps[:, b, 0:n], ACT.Copy).then_inc(dense_free[b], 1)
                    else:
                        nc.scalar.activation(dst(j, b), ps[:, b, 0:n], ACT.Identity,
                                             bias=bias(j)).then_inc(dense_free[b], 1)
        stage(name, dense_us(r, n), ("pe",), pe=f_pe, act=f_act)

    def dense_us(r, n=HALF):
        return 1.3 * sum(r.nk[j % 2] for j in range(r.n)) * (1 if n == HALF else 0.5)

    def to_tiles(first):
        return lambda j, b: wt(first + j, b)

    def gate_z(name, r, o, bias, sz, yfirst=0, o_ready=None):
        done = sig.take("y_done", 2 * r.n)

        def f_pe(pe):
            return dense_run(pe, r, rhs_h, rhs_h)

        def f_act(act):
            for j in range(r.n):
                for b in range(2):
                    yield when(r, j, b)
                    out_ready(act, r.t0 + j, b)
                    if j >= 1:
                        act.wait_ge(done.sem, done.nth(2 * (j - 1) + b))
                    nc.scalar.activation(wt(sz, b), ps[:, b, :], ACT.Silu,
                                         bias=bias(j) if bias else 0.0).then_inc(dense_free[b], 1)

        def f_dve(dve):
            ch = chains["dve"]
            for j in range(r.n):
                for b in range(2):
                    yield when(r, j, b) + 1e-6
                    out_taken(dve, r.t0 + j, b)
                    if o_ready:
                        dve.wait_ge(*o_ready(j, b))
                    ch.link(nc.vector.tensor_tensor(o(j, b), o(j, b), wt(sz, b), ALU.mult))
                    hi = y_hi[:, yfirst + j, b * HALF:(b + 1) * HALF]
                    lo = y_lo[:, yfirst + j, b * HALF:(b + 1) * HALF]
                    ch.link(nc.vector.tensor_copy(hi, o(j, b)))
                    nc.vector.tensor_tensor(lo, o(j, b), hi.bitcast(F32), ALU.subtract).then_inc(done.sem, 1)
        stage(name, dense_us(r), ("pe",), pe=f_pe, act=f_act, dve=f_dve)

    def merge(name, r, gate_bias, first, gt, pace=1.0, y_ready=None):
        done = sig.take("merged", 2 * r.pairs)

        def f_pe(pe):
            parts = dense_run(pe, r, rhs_h, rhs_y)
            yield next(parts)
            for at in parts:
                if y_ready and at > 0.99 * r.nk[0] / sum(r.nk[q % 2] for q in range(r.n)):
                    break
                yield at
            if y_ready:
                pe.wait_ge(y_ready.sem, y_ready.nth(7))
                yield at
            yield from parts

        def f_act(act):
            for i in range(r.pairs):
                for b in range(2):
                    yield when(r, 2 * i, b)
                    out_ready(act, r.t(i, 0), b)
                    if i >= 1:
                        act.wait_ge(done.sem, done.nth(2 * (i - 1) + b))
                    nc.scalar.activation(wt(gt, b), ps[:, b, :], ACT.Sigmoid,
                                         bias=gate_bias(i)).then_inc(dense_free[b], 1)

        def f_dve(dve):
            ch = chains["dve"]
            for i in range(r.pairs):
                for b in range(2):
                    yield when(r, 2 * i + 1, b)
                    out_taken(dve, r.t(i, 0), b)
                    out_ready(dve, r.t(i, 1), b)
                    a = acc[:, i, b * HALF:(b + 1) * HALF]
                    if first:
                        nc.vector.tensor_tensor(a, ps[:, b, :], wt(gt, b), ALU.mult).then_inc(dense_free[b], 1)
                        dve.wait_ge(dense_free[b], r.t(i, 1) + 2)
                        nc.vector.engine_nop().then_inc(done.sem, 1)
                    else:
                        nc.vector.tensor_tensor(wt(gt, b), ps[:, b, :], wt(gt, b), ALU.mult).then_inc(dense_free[b], 1)
                        dve.wait_ge(dense_free[b], r.t(i, 1) + 2)
                        nc.vector.tensor_tensor(a, a, wt(gt, b), ALU.add).then_inc(done.sem, 1)
        stage(name, pace * dense_us(r), ("pe",) if y_ready else (), pe=f_pe, act=f_act, dve=f_dve)

    def add_out(name, r):
        def f_pe(pe):
            return dense_run(pe, r, rhs_y, rhs_y)

        def f_dve(dve):
            for j in range(r.n):
                for b in range(2):
                    yield when(r, j, b)
                    out_ready(dve, r.t0 + j, b)
                    a = acc[:, j, b * HALF:(b + 1) * HALF]
                    nc.vector.tensor_tensor(a, a, ps[:, b, :], ALU.add).then_inc(dense_free[b], 1)
        stage(name, dense_us(r), pe=f_pe, dve=f_dve)

    def norm(name, src, n, emit, width=D, nk=KD, sq=0, rs=2, us=40.0, bank=2, after=None, finish=None):
        squared = sig.take("squared", 2 * nk)
        summed = sig.take("squares_summed", 2 * nk)
        root = sig.take("root", 2)

        def f_act(act):
            for b in range(2):
                for k in range(nk):
                    i = b * nk + k
                    yield (b + k / nk) * 0.35
                    if i >= 2:
                        act.wait_ge(summed.sem, summed.nth(i - 2))
                    nc.scalar.activation(wt(sq, i % 2)[:, 0:n], src(k, b), ACT.Square).then_inc(squared.sem, 1)
                yield (b + 1) * 0.35 - 1e-5
                act.wait_ge(summed.sem, summed.nth(b * nk + nk - 1))
                nc.scalar.activation(wt(rs, b)[:, 0:n], ps[:, bank + b, 0:n], ACT.Sqrt, bias=EPS,
                                     scale=1.0 / width).then_inc(root.sem, 1)

        def f_act_all(act):
            yield from f_act(act)
            if after:
                after(act)

        def f_pe(pe):
            for b in range(2):
                for k in range(nk):
                    i = b * nk + k
                    yield (b + k / nk) * 0.35 + 1e-6
                    pe.wait_ge(squared.sem, squared.nth(i))
                    nc.tensor.matmul(ps[:, bank + b, 0:n], ones, wt(sq, i % 2)[:, 0:n], start=(k == 0),
                                     stop=(k == nk - 1)).then_inc(summed.sem, 1)

        def f_dve(dve):
            ch = chains["dve"]
            for b in range(2):
                yield 0.35 + b * 0.35
                dve.wait_ge(root.sem, root.nth(b))
                ch.link(nc.vector.reciprocal(wt(rs, b)[:, 0:n], wt(rs, b)[:, 0:n]))
                for k in range(nk):
                    yield 0.35 + (b + k / nk) * 0.35 * 0.99
                    emit(ch, k, b, wt(rs, b)[:, 0:n])
                if finish:
                    finish(dve, b)
        stage(name, us, pe=f_pe, act=f_act_all, dve=f_dve)

    def split_emit(src, g, hi, lo, n, tmp=3, first=0):
        def emit(ch, k, b, root):
            t = wt(tmp, k % 2)[:, first:first + n]
            ch.link(nc.vector.scalar_tensor_tensor(t, src(k, b), g(k), root, ALU.mult, ALU.mult))
            ch.link(nc.vector.tensor_copy(hi(k, b), t))
            ch.link(nc.vector.tensor_tensor(lo(k, b), t, hi(k, b).bitcast(F32), ALU.subtract))
        return emit

    def acc_at(k, b):
        return acc[:, k, b * HALF:(b + 1) * HALF]

    def norm_acc(name, g):
        scaled = sig.take("h_scaled", 2 * KD)
        rounded = sig.take("h_rounded", 2 * KD)
        parted = sig.take("h_parted", 2 * KD)
        slot_of = lambda i: wt(3 + (i % 8) // 2, i % 2)
        part = lambda h, i: h[:, i % KD, (i // KD) * HALF:(i // KD + 1) * HALF]

        def second_part(dve, i):
            dve.wait_ge(rounded.sem, rounded.nth(i))
            nc.vector.tensor_tensor(part(h_lo, i), slot_of(i), part(h_hi, i).bitcast(F32),
                                    ALU.subtract).then_inc(parted.sem, 1)

        def emit(ch, k, b, root):
            i = b * KD + k
            if i >= 8:
                ch.eng.wait_ge(parted.sem, parted.nth(i - 8))
            nc.vector.scalar_tensor_tensor(slot_of(i), acc_at(k, b), col(g, k), root, ALU.mult,
                                           ALU.mult).then_inc(scaled.sem, 1)
            if i >= 2:
                second_part(ch.eng, i - 2)

        def finish(dve, b):
            if b == 1:
                second_part(dve, 2 * KD - 2)
                second_part(dve, 2 * KD - 1)

        def after(act):
            for i in range(2 * KD):
                act.wait_ge(scaled.sem, scaled.nth(i))
                nc.scalar.activation(part(h_hi, i), slot_of(i), ACT.Copy).then_inc(rounded.sem, 1)
        norm(name, acc_at, HALF, emit, after=after, finish=finish)
        return parted

    def part_ready(parted):
        return lambda pe, k, b: pe.wait_ge(parted.sem, parted.nth(b * KD + k))

    def head_norm(name, tile, n, scale, factor, sq=4, rs=6, us=80.0, ready=None):
        squared = sig.take("hn_squared", 2 * n)
        summed = sig.take("hn_summed", 2 * n)
        root = sig.take("hn_root", 2 * n)
        normed = sig.take("hn_normed", 2 * n)
        N = 2 * n + 2

        def f_act(act):
            for i in range(N):
                yield i / N
                if i < 2 * n:
                    if ready and i % 2 == 0:
                        act.wait_ge(*ready(i // 2))
                    if i >= 2:
                        act.wait_ge(summed.sem, summed.nth(i - 2))
                    nc.scalar.activation(wt(sq, i % 2), tile(i // 2, i % 2), ACT.Square).then_inc(squared.sem, 1)
                if i >= 2:
                    j = i - 2
                    act.wait_ge(summed.sem, summed.nth(j))
                    if j >= 2:
                        act.wait_ge(normed.sem, normed.nth(j - 2))
                    nc.scalar.activation(wt(rs, j % 2), ps[:, 2 + j % 4, :], ACT.Sqrt, bias=EPS,
                                         scale=scale).then_inc(root.sem, 1)

        def f_pe(pe):
            for i in range(2 * n):
                yield (i + 0.1) / N
                pe.wait_ge(squared.sem, squared.nth(i))
                if i >= 4:
                    pe.wait_ge(root.sem, root.nth(i - 4))
                nc.tensor.matmul(ps[:, 2 + i % 4, :], ones, wt(sq, i % 2), start=True,
                                 stop=True).then_inc(summed.sem, 1)

        def f_dve(dve):
            ch = chains["dve"]
            for i in range(2 * n):
                yield (i + 2.1) / N * 0.999
                dve.wait_ge(root.sem, root.nth(i))
                ch.link(nc.vector.reciprocal(wt(rs, i % 2), wt(rs, i % 2)))
                x = tile(i // 2, i % 2)
                nc.vector.scalar_tensor_tensor(x, x, factor(i // 2), wt(rs, i % 2), ALU.mult,
                                               ALU.mult).then_inc(normed.sem, 1)
        stage(name, us, pe=f_pe, act=f_act, dve=f_dve)
        return normed

    def conv(ch, tiles, dsts, taps, wcol, bcol=None):
        n = len(tiles)
        last = [0] * n
        for s in range(taps):
            for i in range(n):
                w = wcol(taps - 1 - s, i)
                if s == 0:
                    if bcol is None:
                        ins = nc.vector.tensor_scalar(dsts[i], tiles[i], w, None, ALU.mult)
                    else:
                        ins = nc.vector.tensor_scalar(dsts[i], tiles[i], w, bcol(i), ALU.mult, ALU.add)
                else:
                    ch.after(last[i])
                    ins = nc.vector.scalar_tensor_tensor(dsts[i][:, s:T], tiles[i][:, 0:T - s], w,
                                                         dsts[i][:, s:T], ALU.mult, ALU.add)
                last[i] = ch.mark(ins)
            yield s / taps
        ch.after(max(last))

    def layer_norm(name, tile, nk, width, g, tmp, finish=None, us=50.0):
        sq, rs = tmp
        total = sig.take("ln_total", 2)
        centered = sig.take("ln_centered", 2 * nk)
        squared = sig.take("ln_squared", 2 * nk)
        summed = sig.take("ln_summed", 2 * nk)
        root = sig.take("ln_root", 2)
        scaled = sig.take("ln_scaled", 2 * nk)

        at = lambda first, share, b, k: first + share * (b * nk + k) / (2 * nk)

        def f_pe(pe):
            for b in range(2):
                for k in range(nk):
                    yield at(0, 0.2, b, k)
                    mm = nc.tensor.matmul(ps[:, 4 + b, :], ones, tile(k, b), start=(k == 0), stop=(k == nk - 1))
                mm.then_inc(total.sem, 1)
            for b in range(2):
                for k in range(nk):
                    i = b * nk + k
                    yield at(0.3, 0.4, b, k) + 2e-6
                    pe.wait_ge(squared.sem, squared.nth(i))
                    nc.tensor.matmul(ps[:, 2 + b, :], ones, wt(sq, i % 2), start=(k == 0),
                                     stop=(k == nk - 1)).then_inc(summed.sem, 1)

        def f_act(act):
            for b in range(2):
                for k in range(nk):
                    i = b * nk + k
                    yield at(0.3, 0.4, b, k) + 1e-6
                    act.wait_ge(centered.sem, centered.nth(i))
                    if i >= 2:
                        act.wait_ge(summed.sem, summed.nth(i - 2))
                    nc.scalar.activation(wt(sq, i % 2), tile(k, b), ACT.Square).then_inc(squared.sem, 1)
                yield at(0.3, 0.4, b, nk) - 1e-6
                act.wait_ge(summed.sem, summed.nth(b * nk + nk - 1))
                nc.scalar.activation(wt(rs, b), ps[:, 2 + b, :], ACT.Sqrt, bias=EPS,
                                     scale=1.0 / width).then_inc(root.sem, 1)
            if finish:
                for b in range(2):
                    for k in range(nk):
                        yield at(0.7, 0.3, b, k + 1)
                        act.wait_ge(scaled.sem, scaled.nth(b * nk + k))
                        finish(k, b)

        def f_dve(dve):
            ch = chains["dve"]
            for b in range(2):
                yield at(0.2, 0.1, b, 0)
                dve.wait_ge(total.sem, total.nth(b))
                for k in range(nk):
                    nc.vector.scalar_tensor_tensor(tile(k, b), ps[:, 4 + b, :], -1.0 / width, tile(k, b),
                                                   ALU.mult, ALU.add).then_inc(centered.sem, 1)
            for b in range(2):
                yield at(0.7, 0.29, b, 0)
                dve.wait_ge(root.sem, root.nth(b))
                ch.link(nc.vector.reciprocal(wt(rs, b), wt(rs, b)))
                for k in range(nk):
                    yield at(0.7, 0.29, b, k)
                    nc.vector.scalar_tensor_tensor(tile(k, b), tile(k, b), g(k), wt(rs, b), ALU.mult,
                                                   ALU.mult).then_inc(scaled.sem, 1)
        stage(name, us, pe=f_pe, act=f_act, dve=f_dve)

    def softplus(name, a, e, z, z2, q):
        s_e = sig.take("softplus_exp", 1)

        def f_act(act):
            ch = chains["act"]
            ch.link(nc.scalar.activation(e, a, ACT.Abs))
            nc.scalar.activation(e, e, ACT.Exp, scale=-1.0).then_inc(s_e.sem, 1)

        def f_dve(dve):
            ch = chains["dve"]
            dve.wait_ge(s_e.sem, s_e.nth(0))
            ch.link(nc.vector.tensor_scalar(z, e, 2.0, None, ALU.add))
            ch.link(nc.vector.reciprocal(z, z))
            ch.link(nc.vector.tensor_tensor(z, e, z, ALU.mult))
            ch.link(nc.vector.tensor_tensor(z2, z, z, ALU.mult))
            ch.link(nc.vector.tensor_scalar(q, z2, 1.0 / 17, None, ALU.mult))
            for c in (15, 13, 11, 9, 7, 5, 3):
                ch.link(nc.vector.scalar_tensor_tensor(q, q, 1.0 / c, z2, ALU.add, ALU.mult))
            ch.link(nc.vector.scalar_tensor_tensor(q, q, 1.0, z, ALU.add, ALU.mult))
            ch.link(nc.vector.tensor_scalar(a, a, 0.0, None, ALU.max))
            ch.link(nc.vector.scalar_tensor_tensor(a, q, 2.0, a, ALU.mult, ALU.add))
        stage(name, 6.0, act=f_act, dve=f_dve)

    class Unit:
        def __init__(self, scores, bias, pv):
            self.scores, self.bias, self.pv = scores, bias, pv

    def attention(name, steps, width, scale, has_bias, normalize, spt, ptt, pv, take, sinks=None, stats=None, us=0):
        N = len(steps)
        per = 1.0 / (N + 0.1)
        nkb = width // P
        scored = sig.take("scored", N)
        maxed = sig.take("score_max", N)
        expd = sig.take("probs_exp", N)
        normd = sig.take("probs_ready", N)
        turned = sig.take("probs_turned", N)
        pt_ready = sig.take("turned_copied", N)
        mixed = sig.take("values_mixed", N)
        taken = sig.take("values_taken", N)
        S = ps[:, 2:4, :].rearrange("p a (u w) -> p (a u) w", w=256)
        PT = ps[:, 4:6, :].rearrange("p a w -> p (a w)").rearrange("p (k u w) -> p k u w", k=2, u=4)
        SB = wt(spt).rearrange("p (u w) -> p u w", u=4)
        PB = wt(ptt).rearrange("p (k u w) -> p k u w", k=2, u=4)
        lo = 256 - width
        mx, nmx, den, rden, esk = (small[:, 256 + 4 * q:260 + 4 * q] for q in range(5))

        def f_pe(pe):
            def scores(n):
                if n >= 1:
                    pe.wait_ge(expd.sem, expd.nth(n - 1))
                for u, unit in enumerate(steps[n]):
                    for c, l, r in unit.scores:
                        mm = nc.tensor.matmul(S[:, u, c], l, r, start=True, stop=True)
                mm.then_inc(scored.sem, 1)
            scores(0)
            for n in range(N):
                yield (n + 0.4) * per
                if n + 1 < N:
                    scores(n + 1)
                yield (n + 0.6) * per
                pe.wait_ge(normd.sem, normd.nth(n))
                if n >= 1:
                    pe.wait_ge(pt_ready.sem, pt_ready.nth(n - 1))
                for u in range(4):
                    for kb in range(nkb):
                        mm = nc.tensor.transpose(PT[:, kb, u, :], SB[:, u, lo + kb * P:lo + (kb + 1) * P], ident)
                mm.then_inc(turned.sem, 1)
                yield (n + 0.8) * per
                pe.wait_ge(pt_ready.sem, pt_ready.nth(n))
                if n >= 2:
                    pe.wait_ge(taken.sem, taken.nth(n - 2))
                mm = pv(pe, n, ps[:, 6 + n % 2, :], PB)
                mm.then_inc(mixed.sem, 1)

        def f_act(act):
            for n in range(N):
                yield (n + 0.3) * per
                act.wait_ge(maxed.sem, maxed.nth(n))
                for u in range(4):
                    src = SB[:, u, lo:256] if has_bias else S[:, u, lo:256]
                    ins = nc.scalar.activation(SB[:, u, lo:256], src, ACT.Exp, bias=nmx[:, u:u + 1],
                                               scale=1.0 if has_bias else scale, accum_out=den[:, u:u + 1])
                if sinks is not None:
                    nc.scalar.activation(esk, esk, ACT.Exp).then_inc(expd.sem, 1)
                else:
                    ins.then_inc(expd.sem, 1)
                yield (n + 0.7) * per
                act.wait_ge(turned.sem, turned.nth(n))
                if n >= 1:
                    act.wait_ge(mixed.sem, mixed.nth(n - 1))
                nc.scalar.activation(PB[:, 0:nkb], PT[:, 0:nkb], ACT.Copy).then_inc(pt_ready.sem, 1)

        def f_dve(dve):
            ch = chains["dve"]

            def take_away(n):
                dve.wait_ge(mixed.sem, mixed.nth(n))
                take(n, ps[:, 6 + n % 2, :]).then_inc(taken.sem, 1)
            for n in range(N):
                yield (n + 0.05) * per
                dve.wait_ge(scored.sem, scored.nth(n))
                if n >= 1:
                    dve.wait_ge(turned.sem, turned.nth(n - 1))
                if has_bias:
                    for u in range(4):
                        ins = nc.vector.scalar_tensor_tensor(SB[:, u, lo:256], S[:, u, lo:256], scale,
                                                             steps[n][u].bias, ALU.mult, ALU.add)
                    ch.link(ins)
                    ch.link(nc.vector.tensor_reduce(mx, SB[:, :, lo:256], AX, ALU.max))
                else:
                    ch.link(nc.vector.tensor_reduce(mx, S[:, :, lo:256], AX, ALU.max))
                if sinks is not None:
                    ch.link(nc.vector.tensor_tensor(mx, mx, sinks(n), ALU.max))
                    ch.link(nc.vector.tensor_tensor(esk, sinks(n), mx, ALU.subtract))
                if stats:
                    ch.link(nc.vector.tensor_copy(stats(n)[0], mx))
                nc.vector.tensor_scalar(nmx, mx, -1.0 if has_bias else -scale, None,
                                        ALU.mult).then_inc(maxed.sem, 1)
                if n >= 1:
                    yield (n + 0.2) * per
                    take_away(n - 1)
                yield (n + 0.45) * per
                dve.wait_ge(expd.sem, expd.nth(n))
                if not normalize:
                    nc.vector.tensor_copy(stats(n)[1], den).then_inc(normd.sem, 1)
                    continue
                if sinks is not None:
                    ch.link(nc.vector.tensor_tensor(den, den, esk, ALU.add))
                ch.link(nc.vector.reciprocal(rden, den))
                for u in range(4):
                    ins = nc.vector.tensor_scalar(SB[:, u, lo:256], SB[:, u, lo:256], rden[:, u:u + 1],
                                                  None, ALU.mult)
                ins.then_inc(normd.sem, 1)
            yield N * per
            take_away(N - 1)
        stage(name, us or 12.0 * N, pe=f_pe, act=f_act, dve=f_dve)

    loaded = sig.sem("loaded")
    nloads = [0]

    def load(act, dst, src):
        nloads[0] += 1
        act.dma_start(dst, src).then_inc(loaded, 16)

    def loads_done(act):
        act.wait_ge(loaded, 16 * nloads[0])

    section()
    on("dense")
    x_tiles = A["x"][0].rearrange("(n p) d -> n p d", p=P)
    a_small = small[:, 304:308]
    dt_small = small[:, 308:312]

    def load_inputs(act):
        load(act, cst[:], A["consts"])
        for table, row, k, ap in row_loads:
            dst = wt(0)[row:row + k, table * P:(table + 1) * P]
            if len(ap.shape) == 3:
                dst = dst.rearrange("p (u j) -> p u j", u=2)
            load(act, dst, ap)
        load(act, a_small, A["a_log"][0].partition_broadcast(P))
        load(act, dt_small, A["a_dt_bias"][0].partition_broadcast(P))
        for n in range(T // P):
            act.dma_start(wt(1 + n), x_tiles[n]).then_inc(x_loaded[n], 16)
        loads_done(act)
        act.drain().then_inc(rows_loaded.sem, 1)

    rows_loaded = sig.take("rows_loaded", 1)
    x_loaded = [sig.sem(f"x_loaded{n}") for n in range(T // P)]
    stage("load", act=load_inputs)

    x_turned = sig.take("x_turned", T // P + 1)
    x_copied = sig.take("x_copied", T // P + 1)

    def turn_inputs(pe):
        pe.wait_ge(rows_loaded.sem, rows_loaded.nth(0))
        for j, n in enumerate(TABLE_ROWS):
            mm = nc.tensor.transpose(ps[:, 2, j * P:j * P + n], wt(0)[0:n, j * P:(j + 1) * P], ident[0:n, 0:n])
        mm.then_inc(x_turned.sem, 1)
        for n in range(T // P):
            pe.wait_ge(x_loaded[n], 16)
            if n >= 2:
                pe.wait_ge(x_copied.sem, x_copied.nth(n - 2 + 1))
            for d in range(KD):
                mm = nc.tensor.transpose(ps[:, 4 + 2 * (n % 2) + d // 4, (d % 4) * P:(d % 4 + 1) * P],
                                         wt(1 + n)[:, d * P:(d + 1) * P], ident)
            mm.then_inc(x_turned.sem, 1)

    def copy_inputs(dve):
        dve.wait_ge(x_turned.sem, x_turned.nth(0))
        nc.vector.tensor_copy(cols[:, 0:nrows], ps[:, 2, 0:nrows]).then_inc(x_copied.sem, 1)
        for n in range(T // P):
            dve.wait_ge(x_turned.sem, x_turned.nth(n + 1))
            src = ps[:, 4 + 2 * (n % 2):6 + 2 * (n % 2), :].rearrange("p a (d t) -> p (a d) t", t=P)
            nc.vector.tensor_copy(acc[:, :, n * P:(n + 1) * P], src).then_inc(x_copied.sem, 1)
    stage("turn x", 5.0, ("pe", "dve"), pe=turn_inputs, dve=copy_inputs)

    x_stored = sig.sem("x_stored")

    def store_x(act):
        act.dma_start(x_fm.rearrange("k p t -> p k t"), acc[:]).then_inc(x_stored, 16)
    stage("store x", act=store_x)
    norm_acc("norm x", "g_pre")
    w_in = weights("w_in")
    w_br = [A["w_br"][0, n].rearrange("(k p) n -> p k n", p=P) for n in range(5)]

    def pieces_of(w):
        return lambda i: w[:, :, bass.ds((i * 2) * (P // 2), P)]

    def wait_x(act):
        act.wait_ge(x_stored, 16)
    stage("x stored", 1.0, act=wait_x)

    away = nc.dram_tensor("away", [48, P, T], F32, kind="Internal").ap()
    away_done = [sig.sem(f"away_done{b}") for b in range(2)]
    naway = [0, 0]
    next_away = [0]

    def send(act, dst, src, b):
        act.dma_start(dst, src).then_inc(away_done[b], 16)
        naway[b] += 1

    def room(act, b):
        if naway[b]:
            act.wait_ge(away_done[b], 16 * naway[b])

    def project_away(name, r, bias, func=None, pace=AHEAD_PACE):
        at = next_away[0]
        next_away[0] += r.n

        def f_pe(pe):
            return dense_run(pe, r, rhs_h, rhs_h)

        def f_act(act):
            for j in range(r.n):
                for b in range(2):
                    yield when(r, j, b)
                    room(act, b)
                    out_ready(act, r.t0 + j, b)
                    f = func(j) if func else ACT.Identity
                    ins = nc.scalar.activation(wt(10, b), ps[:, b, :], f if bias or f != ACT.Identity else ACT.Copy,
                                               bias=bias(j) if bias else 0.0)
                    ins.then_inc(dense_free[b], 1)
                    act.wait_ge(dense_free[b], r.t0 + j + 2)
                    send(act, away[at + j, :, b * HALF:(b + 1) * HALF], wt(10, b), b)
        stage(name, pace * dense_us(r), ("pe",), pe=f_pe, act=f_act)
        return at

    def fetch(name, pairs, us=10.0, before=None):
        def f_act(act):
            for b in range(2):
                room(act, b)
            if before:
                before(act)
            for tile, place in pairs:
                load(act, wt(tile), away[place])
            yield 0.95
            loads_done(act)
        stage(name, us, act=f_act)

    gate_loaded = [sig.sem(f"gate_loaded{b}") for b in range(2)]
    ngates = [0, 0]

    def gate_stored(name, o, place, us=18.0):
        done = sig.take("y_done", 8)

        def f_act(act):
            for b in range(2):
                room(act, b)
            for j in range(4):
                for b in range(2):
                    yield (2 * j + b) / 10
                    if j >= 1:
                        act.wait_ge(done.sem, done.nth(2 * (j - 1) + b))
                    act.dma_start(wt(10, b), away[place + j, :, b * HALF:(b + 1) * HALF]).then_inc(gate_loaded[b], 16)

        def f_dve(dve):
            ch = chains["dve"]
            for j in range(4):
                for b in range(2):
                    yield (2 * j + b + 1.5) / 10
                    ngates[b] += 1
                    dve.wait_ge(gate_loaded[b], 16 * ngates[b])
                    ch.link(nc.vector.tensor_tensor(o(j, b), o(j, b), wt(10, b), ALU.mult))
                    hi = y_hi[:, j, b * HALF:(b + 1) * HALF]
                    ch.link(nc.vector.tensor_copy(hi, o(j, b)))
                    nc.vector.tensor_tensor(y_lo[:, j, b * HALF:(b + 1) * HALF], o(j, b), hi.bitcast(F32),
                                            ALU.subtract).then_inc(done.sem, 1)
        stage(name, us, act=f_act, dve=f_dve)
        return done

    def merge_run(n):
        return run(KD, tiles_of(w_in, C_GATE + n * D), pieces_of(w_br[n]), KD, 4)

    section()
    on("dense")

    def a_tile(j, b=None):
        if j < 8:
            return acc[:, j, :] if b is None else acc_at(j, b)
        return wt(j - 8, b)

    r_ba = run_one(tiles_of(w_in, C_BA))
    r_a = run(6, *both(w_in, C_AQKV))
    project("A beta alpha", r_ba, lambda j, b: wt(10, b), lambda j: col("b_ba", 0))
    project("A project", r_a, a_tile, lambda j: col("b_aqkv", j))
    logits_turned = sig.take("logits_turned", 1)

    def logits_wait(act):
        act.wait_ge(logits_turned.sem, logits_turned.nth(0))
    stage("A logits", 0.1, act=logits_wait)
    mem_normed = sig.take("mem_normed", 1)
    at_glu = project_away("B glu", run(4, *both(w_in, C_GLU)), lambda j: col("b_glu", j),
                          lambda j: ACT.Identity if j < 4 else ACT.Sigmoid)

    def memory_kv(name, w_kv, which):
        at = next_away[0]
        next_away[0] += 2
        for kind in range(2):
            r = run(2, *both(w_kv, kind * W))
            rhs = (keys_of, values_of)[kind][which]

            def f_pe(pe, r=r, rhs=rhs):
                pe.wait_ge(mem_normed.sem, mem_normed.nth(0))
                yield from dense_run(pe, r, rhs, rhs, P)

            def f_act(act, r=r, kind=kind):
                ch = chains["act"]
                for b in range(2):
                    room(act, b)
                for j in range(r.n):
                    for b in range(2):
                        yield when(r, j, b)
                        out_ready(act, r.t0 + j, b)
                        dst = wt(10)[:, j * MEM + b * P:j * MEM + (b + 1) * P] if kind == 0 else \
                            wt(10)[:, b * HALF + j * P:b * HALF + (j + 1) * P]
                        nc.scalar.activation(dst, ps[:, b, 0:P], ACT.Copy).then_inc(dense_free[b], 1)
                        act.wait_ge(dense_free[b], r.t0 + j + 2)
                for b in range(2):
                    send(act, away[at + kind, :, b * HALF:(b + 1) * HALF], wt(10, b), b)
            stage(name, AHEAD_PACE * dense_us(r, P), ("pe",), pe=f_pe, act=f_act)
        return at
    at_kv = [memory_kv("E k v", weights("w_mem_kv"), 0), memory_kv("even k v", weights("even_w_mem_kv_2"), 1),
             memory_kv("odd k v", weights("odd_w_mem_kv_2"), 1)]

    def swapped(w, first):
        v = w[:, :, first:first + W].rearrange("p k (u t j) -> p k u t j", u=2, j=64)
        return lambda i, p: ("columns", [v[:, :, u, 2 * i + p, :] for u in range(2)])
    cq = swapped(w_in, C_CQ)
    cz = swapped(w_in, C_CZ)
    at_cq = next_away[0]
    for i in range(2):
        project_away("C q", run(1, lambda _, i=i: cq(i, 0), lambda _, i=i: cq(i, 1)),
                     lambda j, i=i: col("b_cq", 2 * i + j))
    at_ckv = project_away("C k v", run(1, *both(w_in, C_CKV)), lambda j: col("b_ckv", j))
    at_dx = project_away("D x", run(2, *both(w_in, C_DX)), lambda j: col("b_dx", j))
    at_eq = project_away("E q", run(2, *both(w_in, C_EQ)), lambda j: col("b_eq", j))


    def stored_away(act):
        for b in range(2):
            room(act, b)
    stage("stored", 3.0, act=stored_away)

    on("aux")
    beta_t = small[:, 0:64].rearrange("p (n h) -> p n h", h=8)
    g_t = small[:, 64:128].rearrange("p (n h) -> p n h", h=8)
    gc_t = small[:, 128:192].rearrange("p (n h) -> p n h", h=8)

    def ba_turn(pe):
        yield 0.85
        out_taken(pe, r_ba.t0, 0)
        out_taken(pe, r_ba.t0, 1)
        for n in range(8):
            mm = nc.tensor.transpose(ps[:, 2, n * 8:n * 8 + 8], wt(10)[0:8, n * P:(n + 1) * P], ident[0:8, 0:8])
        mm.then_inc(logits_turned.sem, 1)
    stage("A turn", 24.0, pe=ba_turn)

    def ba_copy(dve):
        ch = chains["dve"]
        ch.link(nc.vector.tensor_copy(small[:, 0:64], ps[:, 2, 0:64]))
        nc.vector.tensor_tensor(g_t[:, :, 4:8], beta_t[:, :, 4:8],
                                dt_small.unsqueeze(1).to_broadcast([P, 8, 4]), ALU.add)
    stage("A turned", 3.0, dve=ba_copy)

    def ba_sig(act):
        nc.scalar.activation(beta_t[:, :, 0:4], beta_t[:, :, 0:4], ACT.Sigmoid)
        nc.scalar.activation(a_small, a_small, ACT.Exp)
    stage("A sigmoid", 5.0, act=ba_sig)
    four_small = [small[:, c:c + 32].rearrange("p (n h) -> p n h", h=4) for c in (128, 160, 192, 224)]
    softplus("A softplus", g_t[:, :, 4:8], *four_small)

    def ba_decay(dve):
        nc.vector.scalar_tensor_tensor(g_t[:, :, 4:8], g_t[:, :, 4:8], -1.0,
                                       a_small.unsqueeze(1).to_broadcast([P, 8, 4]), ALU.mult, ALU.mult)

    def ba_sum(pe):
        nc.tensor.matmul(ps[:, 4, 0:32], C("upto"), g_t[:, :, 4:8], start=True, stop=True)

    def ba_sum_copy(dve):
        nc.vector.tensor_copy(gc_t[:, :, 4:8], ps[:, 4, 0:32].rearrange("p (n h) -> p n h", h=4))
    stage("A decay", 1.0, dve=ba_decay)
    stage("A running sum", 1.0, pe=ba_sum)
    stage("A running sum copied", 1.0, dve=ba_sum_copy)

    on("side")
    for which, (mem, g_mem) in enumerate(((A["mem"], "g_mem"), (A["mem_2"], "g_mem_2"))):
        def m_load(act, mem=mem):
            for j in range(2):
                load(act, wt(6 + j), mem[0].rearrange("(n p) d -> n p d", p=P)[j])
            yield 0.9
            loads_done(act)
        stage("memory", 8.0, act=m_load)
        mem_t = wrk[:, 8:10, :].rearrange("p a (k m) -> p (a k) m", m=MEM)
        for part in range(2):
            def m_turn(pe, part=part):
                for j in range(2):
                    for k in range(4):
                        nc.tensor.transpose(ps[:, 6 + k // 2, (k % 2) * MEM + j * P:(k % 2) * MEM + (j + 1) * P],
                                            wt(6 + j)[:, (4 * part + k) * P:(4 * part + k + 1) * P], ident)

            def m_copy(dve, part=part):
                nc.vector.tensor_copy(wt(8 + part).rearrange("p (b m) -> p b m", m=HALF), ps[:, 6:8, :])
            stage("memory turned", 2.5, pe=m_turn)
            stage("memory copied", 2.0, dve=m_copy)
        src = lambda k, b: mem_t[:, k, b * P:(b + 1) * P]
        norm("memory norm", src, P, split_emit(
            src, lambda k, g=g_mem: col(g, k), lambda k, b, w=which: mem_view(y_hi, w)[:, k, b * P:(b + 1) * P],
            lambda k, b, w=which: mem_view(y_lo, w)[:, k, b * P:(b + 1) * P], P, tmp=7, first=2 * P),
             sq=6, rs=7, us=30.0, bank=6)

    def memories_there(dve):
        nc.vector.engine_nop().then_inc(mem_normed.sem, 1)
    stage("memories there", 0.5, dve=memories_there)

    on("aux")
    conved = sig.take("a_conved", 6)
    silued = sig.take("a_silued", 12)

    def a_conv(dve):
        ch = chains["dve"]
        for i in range(6):
            j = 2 * i
            yield i / 7
            for jj in (j, j + 1):
                for b in range(2):
                    out_taken(dve, r_a.t0 + jj, b)
            if i >= 1:
                dve.wait_ge(silued.sem, silued.nth(j - 1))
            for part in conv(ch, [a_tile(j), a_tile(j + 1)], [wt(4), wt(5)], 4,
                             lambda tap, m, j=j: col("a_conv_w", tap * 12 + j + m)):
                yield (i + 0.7 * part) / 7
            nc.vector.engine_nop().then_inc(conved.sem, 1)

    def a_silu(act):
        for j in range(12):
            yield (j // 2 + 0.85) / 7
            act.wait_ge(conved.sem, conved.nth(j // 2))
            nc.scalar.activation(a_tile(j), wt(4 + j % 2), ACT.Silu).then_inc(silued.sem, 1)
    stage("A conv", 147.0, dve=a_conv, act=a_silu)
    head_norm("A norm q k", a_tile, 8, 1.0, lambda j: P ** -0.5 if j < 4 else 1.0, sq=4, rs=5)

    def memories_wait(eng):
        eng.wait_ge(mem_normed.sem, mem_normed.nth(0))
    stage("memories done", 0.5, pe=memories_wait, act=memories_wait)

    def slot(j):
        return wrk[:, 4 + j // 2, (j % 2) * HALF:(j % 2 + 1) * HALF].rearrange("p (h c) -> p h c", h=4)

    LT, AT, BT, ZZ, TT, UU, VB, KBE, KDEC, ATT, ST, EG = (slot(j) for j in range(12))
    dk, eg, nbeg, ekd = (small[:, 200 + 4 * q:204 + 4 * q] for q in range(4))

    def four(b):
        return ps[:, b, :].rearrange("p (h c) -> p h c", h=4)

    def all4(m):
        return m.unsqueeze(1).to_broadcast([P, 4, P])

    NPE, NACT, NDVE = 2 + 2 * NLEVEL, 3 + NLEVEL, 4 + 2 * NLEVEL
    gdn_pe = sig.take("gdn_pe", 8 * NPE)
    gdn_act = sig.take("gdn_act", 8 * NACT)
    gdn_dve = sig.take("gdn_dve", 8 * NDVE)
    L = NLEVEL
    lev_at = lambda lv: (9 + 4 * (lv - 1)) / 40

    def delta_chunk(n):
        c = slice(n * P, (n + 1) * P)
        step_pe = lambda i: (gdn_pe.sem, gdn_pe.nth(n * NPE + i))
        step_act = lambda i: (gdn_act.sem, gdn_act.nth(n * NACT + i))
        step_dve = lambda i: (gdn_dve.sem, gdn_dve.nth(n * NDVE + i))

        def f_pe(pe):
            def products(dst, lhsT, rhs):
                for h in range(4):
                    mm = nc.tensor.matmul(four(dst)[:, h, :], lhsT(h), rhs(h), start=True, stop=True)
                return mm
            for h in range(4):
                nc.tensor.transpose(four(2)[:, h, :], acc[:, 4 + h, c], ident)
                nc.tensor.transpose(four(3)[:, h, :], wt(h)[:, c], ident)
            products(4, lambda h: gc_t[:, n, 4 + h:5 + h].to_broadcast([P, P]), lambda h: ident)
            products(5, lambda h: beta_t[:, n, h:h + 1].to_broadcast([P, P]), lambda h: ident)
            products(6, lambda h: acc[:, 4 + h, c], lambda h: acc[:, 4 + h, c])
            products(7, lambda h: acc[:, 4 + h, c], lambda h: acc[:, h, c]).then_inc(gdn_pe.sem, 1)
            yield 6 / 40
            pe.wait_ge(*step_dve(3))
            pe.wait_ge(*step_act(2))
            for h in range(4):
                mm = nc.tensor.transpose(four(2)[:, h, :], BT[:, h, :], ident)
            mm.then_inc(gdn_pe.sem, 1)
            for lv in range(1, L):
                yield lev_at(lv)
                pe.wait_ge(*step_dve(3 + 2 * lv))
                products(2, lambda h: BT[:, h, :], lambda h: TT[:, h, :]).then_inc(gdn_pe.sem, 1)
                yield lev_at(lv) + 2 / 40
                pe.wait_ge(*step_act(2 + lv))
                if lv < L - 1:
                    products(3, lambda h: UU[:, h, :], lambda h: ZZ[:, h, :])
                products(4, lambda h: ZZ[:, h, :], lambda h: UU[:, h, :]).then_inc(gdn_pe.sem, 1)
            yield 33 / 40
            pe.wait_ge(*step_dve(2 + 2 * L))
            products(6, lambda h: KBE[:, h, :], lambda h: UU[:, h, :]).then_inc(gdn_pe.sem, 1)
            yield 35 / 40
            pe.wait_ge(*step_act(2 + L))
            for h in range(4):
                mm = nc.tensor.matmul(four(5)[:, h, :], UU[:, h, :], VB[:, h, :], start=True, stop=(n == 0))
                if n > 0:
                    mm = nc.tensor.matmul(four(5)[:, h, :], ZZ[:, h, :], ST[:, h, :], start=False, stop=True)
            mm.then_inc(gdn_pe.sem, 1)
            yield 37 / 40
            pe.wait_ge(*step_dve(3 + 2 * L))
            for h in range(4):
                if n > 0:
                    nc.tensor.matmul(four(7)[:, h, :], ST[:, h, :], acc[:, h, c], start=True, stop=False)
                nc.tensor.matmul(four(7)[:, h, :], TT[:, h, :], ATT[:, h, :], start=(n == 0), stop=True)
            products(2, lambda h: KDEC[:, h, :], lambda h: TT[:, h, :])

        def f_act(act):
            yield 2 / 40
            act.wait_ge(*step_pe(0))
            nc.scalar.activation(EG, four(4), ACT.Exp)
            nc.scalar.activation(eg, gc_t[:, n, 4:8], ACT.Exp).then_inc(gdn_act.sem, 1)
            yield 4 / 40
            act.wait_ge(*step_dve(0))
            nc.scalar.activation(ekd, dk, ACT.Exp)
            nc.scalar.activation(LT, LT, ACT.Exp).then_inc(gdn_act.sem, 1)
            act.wait_ge(*step_act(1))
            yield 5 / 40
            act.wait_ge(*step_dve(1))
            for h in range(4):
                nc.scalar.activation(VB[:, h, :], four(3)[:, h, :], ACT.Copy, scale=beta_t[:, n, h:h + 1])
                nc.scalar.activation(KBE[:, h, :], four(2)[:, h, :], ACT.Copy, scale=nbeg[:, h:h + 1])
                ins = nc.scalar.activation(KDEC[:, h, :], four(2)[:, h, :], ACT.Copy, scale=ekd[:, h:h + 1])
            ins.then_inc(gdn_act.sem, 1)
            for lv in range(1, L):
                yield lev_at(lv) + 1 / 40
                act.wait_ge(*step_pe(2 * lv))
                nc.scalar.activation(ZZ, four(2), ACT.Copy).then_inc(gdn_act.sem, 1)
            yield 34 / 40
            act.wait_ge(*step_pe(2 * L))
            nc.scalar.activation(ZZ, four(6), ACT.Copy).then_inc(gdn_act.sem, 1)

        def f_dve(dve):
            ch = chains["dve"]
            yield 3 / 40
            dve.wait_ge(*step_pe(0))
            dve.wait_ge(*step_act(0))
            for h in range(4):
                nc.vector.scalar_tensor_tensor(LT[:, h, :], four(4)[:, h, :], gc_t[:, n, 4 + h:5 + h],
                                               C("negafter"), ALU.subtract, ALU.add)
            nc.vector.tensor_tensor(dk, four(4)[:, :, P - 1], gc_t[:, n, 4:8], ALU.subtract).then_inc(gdn_dve.sem, 1)
            nc.vector.scalar_tensor_tensor(nbeg, eg, -1.0, beta_t[:, n, 0:4], ALU.mult,
                                           ALU.mult).then_inc(gdn_dve.sem, 1)
            ch.link(nc.vector.tensor_tensor(acc[:, 0:4, c], acc[:, 0:4, c], EG, ALU.mult))
            yield 5 / 40
            dve.wait_ge(*step_act(1))
            ch.link(nc.vector.tensor_tensor(AT, four(6), LT, ALU.mult))
            ch.link(nc.vector.tensor_tensor(AT, AT, four(5), ALU.mult))
            nc.vector.tensor_tensor(ATT, four(7), LT, ALU.mult).then_inc(gdn_dve.sem, 1)
            nc.vector.tensor_tensor(BT, AT, all4(C("lev0")), ALU.mult).then_inc(gdn_dve.sem, 1)
            dve.wait_ge(*step_dve(3))
            ch.link(nc.vector.tensor_tensor(UU, all4(ident), BT, ALU.subtract))
            yield 7 / 40
            dve.wait_ge(*step_pe(1))
            nc.vector.tensor_tensor(TT, all4(ident), four(2), ALU.subtract).then_inc(gdn_dve.sem, 1)
            nc.vector.tensor_tensor(BT, AT, all4(C("lev1")), ALU.mult).then_inc(gdn_dve.sem, 1)
            for lv in range(1, L):
                if lv < L - 1:
                    yield lev_at(lv) + 1 / 40
                    dve.wait_ge(*step_pe(2 * lv))
                    nc.vector.tensor_tensor(BT, AT, all4(C(f"lev{lv + 1}")), ALU.mult).then_inc(gdn_dve.sem, 1)
                yield lev_at(lv) + 3 / 40
                dve.wait_ge(*step_pe(2 * lv + 1))
                if lv < L - 1:
                    nc.vector.tensor_tensor(TT, TT, four(3), ALU.subtract)
                nc.vector.tensor_tensor(UU, UU, four(4), ALU.subtract).then_inc(gdn_dve.sem, 1)
            yield 36 / 40
            dve.wait_ge(*step_pe(2 * L + 1))
            nc.vector.tensor_copy(TT, four(5)).then_inc(gdn_dve.sem, 1)
        stage(f"A chunk {n}", CHUNK_TIME, pe=f_pe, act=f_act, dve=f_dve)

        def s_act(act):
            nc.scalar.activation(acc[:, 0:4, c], four(7), ACT.Copy)

        def s_dve(dve):
            for h in range(4):
                if n == 0:
                    nc.vector.tensor_copy(ST[:, h, :], four(2)[:, h, :])
                else:
                    nc.vector.scalar_tensor_tensor(ST[:, h, :], ST[:, h, :], EG[:, h, P - 1:P],
                                                   four(2)[:, h, :], ALU.mult, ALU.add)
        stage(f"A chunk {n} state", 2.0, act=s_act, dve=s_dve)

    for n in range(8):
        delta_chunk(n)

    section()
    on("aux")
    o_normed = head_norm("A norm out", a_tile, 4, 1.0 / P, lambda j: col("a_norm_g"), sq=8, rs=9, us=44.0)
    fetch("B glu", [(j, at_glu + j) for j in range(8)], 14.0)

    def b_mult(dve):
        for i in range(4):
            nc.vector.tensor_tensor(wt(i), wt(i), wt(4 + i), ALU.mult)
    stage("B gated", 6.0, dve=b_mult)

    def b_conv(dve):
        yield from conv(chains["dve"], [wt(i) for i in range(4)], [wt(4 + i) for i in range(4)], 31,
                        lambda tap, i: col("b_dw_w", tap * 4 + i), lambda i: col("b_dw_b", i))
    stage("B conv", 145.0, dve=b_conv)
    layer_norm("B norm", lambda k, b: wt(4 + k, b), 4, W, lambda k: col("b_ln_g", k), (8, 9),
               lambda k, b: nc.scalar.activation(wt(4 + k, b), wt(4 + k, b), ACT.Silu, bias=col("b_ln_b", k)))
    on("dense")
    stage("first outputs normed", 8.0)
    gate_z("A z", run(2, *both(w_in, C_AZ)), acc_at, lambda j: col("b_az", j), 10,
           o_ready=lambda j, b: (o_normed.sem, o_normed.nth(2 * j + b)))
    merge("A merge", merge_run(0), lambda i: col("b_gate", i), True, 10, pace=A_PACE)
    at_dz = project_away("D z", run(2, *both(w_in, C_DZ)), lambda j: col("b_dz", j), lambda j: ACT.Silu, pace=1.0)
    at_ez = project_away("E z", run(2, *both(w_in, C_EZ)), lambda j: col("b_ez", j), lambda j: ACT.Silu, pace=1.0)
    stage("stored", 1.0, act=stored_away)

    section()
    on("dense")
    gate_z("B z", run(2, *both(w_in, C_BZ)), lambda j, b: wt(4 + j, b), lambda j: col("b_bz", j), 10)
    b_gated = sig.take("b_gated", 1)

    def b_gated_dve(dve):
        nc.vector.engine_nop().then_inc(b_gated.sem, 1)
    stage("B gated", 0.1, dve=b_gated_dve)
    merge("B merge", merge_run(1), lambda i: col("b_gate", 8 + i), False, 10, pace=B_PACE)
    on("aux")

    def c_load(act):
        load(act, wt(0)[:, 0:896], A["bias_consts"])
        load(act, wt(1)[0:32, 0:8], A["rel_bias"])
        load(act, small[:, 304:312], A["c_sinks"][0].partition_broadcast(P))
        yield 0.9
        loads_done(act)
    stage("C load", 6.0, act=c_load)

    def c_rows_pe(pe):
        nc.tensor.matmul(ps[0:8, 2, 0:384], wt(1)[0:32, 0:8], wt(0)[0:32, 0:384], start=True, stop=True)

    def c_rows_dve(dve):
        nc.vector.tensor_tensor(wt(1)[0:8, 128:512], ps[0:8, 2, 0:384], wt(0)[0:8, 384:768], ALU.add)
    stage("C bias rows", 1.0, pe=c_rows_pe)
    stage("C bias rows", 1.0, dve=c_rows_dve)

    def c_skew(act):
        load(act, bias_rows.ap(), wt(1)[0:8, 128:512])
        yield 0.45
        loads_done(act)
        skew = bass.AP(tensor=bias_rows.ap().tensor, offset=0, ap=[[1, P], [384, 8], [1, 256]])
        load(act, wrk[:, 8:10, :].rearrange("p a (h j) -> p (a h) j", h=4), skew)
        yield 0.95
        loads_done(act)
    stage("C skew", 32.0, act=c_skew)

    def c_flip_pe(pe):
        for g in range(4):
            nc.tensor.matmul(ps[:, 4 + g, :], wt(0)[:, 768:896], wt(8 + g // 2, g % 2), start=True, stop=True)

    def c_flip_dve(dve):
        for g in range(4):
            nc.vector.tensor_copy(wt(8 + g // 2, g % 2), ps[:, 4 + g, :])
    stage("C flip", 4.0, pe=c_flip_pe)
    stage("C flipped", 3.0, dve=c_flip_dve)
    fetch("C q k v", [(j, at_cq + j) for j in range(4)] + [(4, at_ckv), (7, at_ckv + 1)], 14.0,
          lambda act: act.wait_ge(b_gated.sem, b_gated.nth(0)))

    def c_v_pe(pe):
        for n in range(8):
            nc.tensor.transpose(ps[:, 4 + n // 4, (n % 4) * P:(n % 4 + 1) * P], wt(7)[:, n * P:(n + 1) * P], ident)

    def c_v_dve(dve):
        nc.vector.tensor_copy(wt(6), ps[:, 4:6, :].rearrange("p a w -> p (a w)"))
    stage("C v turned", 2.0, pe=c_v_pe)
    stage("C v copied", 2.0, dve=c_v_dve)

    def c_attention():
        bias = wrk[:, 8:10, :].rearrange("p a (h j) -> p (a h) j", h=4)
        steps, where = [], []
        for n in range(8):
            for K in range(2):
                units = []
                for t in range(4):
                    rows = slice(64 * K, 64 * K + 64)
                    q = wt(t)[rows, n * P:(n + 1) * P]
                    if n == 0:
                        units.append(Unit([(slice(P, 256), q, wt(4)[rows, 0:P])], bias[:, 4 * K + t, P:256], None))
                    else:
                        sc = [(slice(0, 256), q, wt(4)[rows, (n - 1) * P:(n + 1) * P])]
                        units.append(Unit(sc, bias[:, 4 * K + t, :], None))
                steps.append(units)
                where.append((n, K))
        return steps, where

    c_steps, c_where = c_attention()

    def c_run(name, steps, where, width):
        def pv(pe, s, dst, PB):
            n, K = where[s]
            rows = slice(64 * K, 64 * K + 64)
            blocks = [n] if width == P else [n - 1, n]
            for kb, blk in enumerate(blocks):
                mm = nc.tensor.matmul(dst[rows, :], wt(6)[:, blk * P + 64 * K:blk * P + 64 * K + 64],
                                      PB[:, kb, :, :], start=(kb == 0), stop=(kb == len(blocks) - 1))
            return mm

        def take(s, src):
            n, K = where[s]
            rows = slice(64 * K, 64 * K + 64)
            return nc.vector.tensor_copy(wrk[rows, 0:4, n * P:(n + 1) * P],
                                         src[rows, :].rearrange("p (h c) -> p h c", h=4))
        attention(name, steps, width, 64 ** -0.5, True, True, 5, 7, pv, take,
                  sinks=lambda s: small[:, 304 + 4 * where[s][1]:308 + 4 * where[s][1]])
    c_run("C attention, first block", c_steps[:2], c_where[:2], P)
    c_run("C attention", c_steps[2:], c_where[2:], 256)

    section()
    on("dense")
    for i in range(2):
        r = run(1, lambda _, i=i: cz(i, 0), lambda _, i=i: cz(i, 1))
        gate_z("C z", r, lambda j, b, i=i: wt(2 * i + j, b), lambda j, i=i: col("b_cz", 2 * i + j), 10, 2 * i)
    c_gated = sig.take("c_gated", 1)

    def c_gated_dve(dve):
        nc.vector.engine_nop().then_inc(c_gated.sem, 1)
    stage("C gated", 0.1, dve=c_gated_dve)
    w_c = A["w_br"][0, 2].rearrange("(u k j) n -> u j k n", u=2, j=64)
    merge_c = run(KD, tiles_of(w_in, C_GATE + 2 * D),
                  lambda i: ("rows", [pieces_of(w_c[u])(i) for u in range(2)]), KD, 4)
    merge("C merge", merge_c, lambda i: col("b_gate", 16 + i), False, 10, pace=C_PACE)
    on("aux")

    def d_zero(dve):
        ch = chains["dve"]
        nc.vector.memset(wt(9), 0.0)
        nc.vector.tensor_scalar(small[:, 320:324], cols[:, COL["d_lambda"]:COL["d_lambda"] + 4], -1.0, None, ALU.mult)

    def d_load(act):
        for half, name in ((0, "d_w_a"), (1, "d_w_x")):
            for u in range(2):
                load(act, wt(9, half)[64 * u:64 * u + 64].rearrange("c (t d) -> c t d", t=4)
                     [:, :, 64 * u:64 * u + 64],
                     A[name][0].rearrange("(t u) c d -> u c t d", u=2)[u])
        yield 0.9
        loads_done(act)
    stage("D zero", 2.0, dve=d_zero)
    stage("D load", 6.0, act=d_load)
    fetch("D x", [(4 + j, at_dx + j) for j in range(4)])
    softplus("D softplus", small[:, 320:324], small[:, 324:328], small[:, 328:332], small[:, 332:336],
             small[:, 336:340])

    def d_rate(dve):
        nc.vector.tensor_scalar(small[:, 324:328], small[:, 320:324], -8.0, None, ALU.mult)
        nc.vector.tensor_scalar(small[:, 328:332], small[:, 320:324], 8.0, None, ALU.mult)
    stage("D rate", 20.0, dve=d_rate)

    for i in range(4):
        def dc(dve, i=i):
            if i == 0:
                dve.wait_ge(c_gated.sem, c_gated.nth(0))
            yield from conv(chains["dve"], [wt(4 + i)], [wt(8)], 4, lambda tap, _: col("d_conv_w", tap * 4 + i),
                            lambda _: col("d_conv_b", i))
        stage("D conv", 18.0 if i == 0 else 6.0, dve=dc)

        def dg_pe(pe, i=i):
            for g in range(2):
                for b in range(2):
                    nc.tensor.matmul(ps[:, 2 + 2 * g + b, :], wt(9, g)[:, i * P:(i + 1) * P], wt(8, b),
                                     start=True, stop=True)
        stage("D gates", 4.0, pe=dg_pe)

        def dg_act(act, i=i):
            ch = chains["act"]
            flat = lambda b: ps[:, b:b + 2, :].rearrange("p a w -> p (a w)")
            ch.link(nc.scalar.activation(wt(0), flat(2), ACT.Sigmoid, bias=col("d_b_a", i)))
            nc.scalar.activation(wt(1), flat(4), ACT.Sigmoid, bias=col("d_b_x", i))
            yield 0.4
            nc.scalar.activation(wt(2), wt(0), ACT.Exp, scale=small[:, 324 + i:325 + i])
            nc.scalar.activation(wt(3), wt(0), ACT.Tanh, scale=small[:, 328 + i:329 + i])
        stage("D gate values", 8.0, act=dg_act)

        def dt_dve(dve, i=i):
            ch = chains["dve"]
            ch.link(nc.vector.tensor_scalar(wt(0), wt(3), 1.0, None, ALU.add))
            for b in range(2):
                yield 0.1 + 0.3 * b
                nc.vector.reciprocal(wt(0, b), wt(0, b))
            yield 0.7
            dve.drain()
            nc.vector.scalar_tensor_tensor(wt(3), wt(3), 2.0, wt(0), ALU.mult, ALU.mult)
            nc.vector.tensor_tensor(wt(1), wt(1), wt(8), ALU.mult)
        stage("D input factor", 13.0, dve=dt_dve)

        def dr_act(act):
            nc.scalar.activation(wt(3), wt(3), ACT.Sqrt)
        stage("D root", 3.0, act=dr_act)

        def ds_dve(dve, i=i):
            ch = chains["dve"]
            ch.link(nc.vector.tensor_tensor(wt(1), wt(1), wt(3), ALU.mult))
            nc.vector.tensor_tensor_scan(wt(4 + i), wt(2), wt(1), 0.0, ALU.mult, ALU.add)
        stage("D scan", 4.0, dve=ds_dve)

    def memory_attention(tag, q, kt, vt, spt, ptt, us=0):
        kv = wt(kt).rearrange("p (h m) -> p h m", m=MEM)
        v_t = wt(vt).rearrange("p (m c) -> p m c", m=2)
        steps = [[Unit([(slice(0, 256), wt(q + h)[:, (4 * s4 + u) * P:(4 * s4 + u + 1) * P], kv[:, h, :])],
                       None, None) for u in range(4)] for h in range(4) for s4 in range(2)]

        def pv(pe, s, dst, PB):
            h = s // 2
            for kb in range(2):
                mm = nc.tensor.matmul(dst, v_t[:, kb, h * P:(h + 1) * P], PB[:, kb, :, :],
                                      start=(kb == 0), stop=(kb == 1))
            return mm

        def take(s, src):
            return nc.vector.tensor_copy(wt(q + s // 2, s % 2), src)
        attention(tag + " attention", steps, 256, P ** -0.5, False, True, spt, ptt, pv, take, us=us)

    section()
    on("dense")
    d_done = gate_stored("D gate", lambda j, b: wt(4 + j, b), at_dz)
    d_gated = sig.take("d_gated", 1)

    def d_gated_dve(dve):
        nc.vector.engine_nop().then_inc(d_gated.sem, 1)
    stage("D gated", 0.1, dve=d_gated_dve)
    merge("D merge", merge_run(3), lambda i: col("b_gate", 24 + i), False, 10, pace=D_PACE, y_ready=d_done)
    on("aux")
    fetch("E q", [(j, at_eq + j) for j in range(4)] + [(8, at_kv[0]), (9, at_kv[0] + 1)], 22.0)

    def e_wait(dve):
        dve.wait_ge(d_gated.sem, d_gated.nth(0))
    stage("E scores' tiles", 0.5, dve=e_wait)
    memory_attention("E", 0, 8, 9, 4, 5, us=E_ATT_TIME)

    section()
    on("dense")
    e_done = gate_stored("E gate", wt, at_ez)
    merge("E merge", merge_run(4), lambda i: col("b_gate", 32 + i), False, 10, y_ready=e_done)
    on("aux")

    at_rope = next_away[0]
    next_away[0] += 2

    def r_load(act):
        load(act, wt(4).bitcast(I32)[0:32, :], A["positions_2"][0].partition_broadcast(32))
        yield 0.9
        loads_done(act)

    TWO_PI_1, TWO_PI_2, TWO_PI_3 = 6.28125, 1.9350051879882812e-03, 3.0199159819210e-07
    ri = wt(5).bitcast(I32)[0:32, :]

    def r_start(dve):
        ch = chains["dve"]
        ch.link(nc.vector.tensor_copy(wt(6)[0:32, :], wt(4).bitcast(I32)[0:32, :]))
        nc.vector.tensor_scalar(wt(6)[0:32, :], wt(6)[0:32, :], C("rope")[0:32, 0:1], None, ALU.mult)

    def r_dve(dve):
        ch = chains["dve"]
        a, n, m = wt(6)[0:32, :], wt(7)[0:32, :], wt(8)[0:32, :]
        for k, (dst, quarter) in enumerate(((9, 0.0), (4, 0.25))):
            yield k / 2
            d = wt(dst)[0:32, :]
            ch.link(nc.vector.tensor_scalar(n, a, 0.15915494309189535, quarter, ALU.mult, ALU.add))
            ch.link(nc.vector.tensor_copy(ri, n))
            ch.link(nc.vector.tensor_copy(n, ri))
            ch.link(nc.vector.scalar_tensor_tensor(d, n, -TWO_PI_1, a, ALU.mult, ALU.add))
            ch.link(nc.vector.scalar_tensor_tensor(d, n, -TWO_PI_2, d, ALU.mult, ALU.add))
            ch.link(nc.vector.scalar_tensor_tensor(d, n, -TWO_PI_3, d, ALU.mult, ALU.add))
            ch.link(nc.vector.tensor_scalar(d, d, quarter * 6.283185307179586, None, ALU.add))
            yield k / 2 + 0.25
            for bound, op in ((3.14159265, ALU.is_gt), (-3.14159265, ALU.is_lt)):
                ch.link(nc.vector.tensor_scalar(m, d, bound, -6.283185307179586 if bound > 0 else
                                                6.283185307179586, op, ALU.mult))
                ch.link(nc.vector.tensor_tensor(d, d, m, ALU.add))
            ch.link(nc.vector.tensor_scalar(d, d, 3.1415925, -3.1415925, ALU.min, ALU.max))

    def r_sin(act):
        nc.scalar.activation(wt(9)[0:32, :], wt(9)[0:32, :], ACT.Sin)
        nc.scalar.activation(wt(4)[0:32, :], wt(4)[0:32, :], ACT.Sin)

    def r_sign(dve):
        nc.vector.tensor_scalar(wt(9)[0:32, :], wt(9)[0:32, :], C("rope")[0:32, 1:2], None, ALU.mult)

    def r_store(act):
        send(act, away[at_rope, 0:32, :], wt(4)[0:32, :], 0)
        send(act, away[at_rope + 1, 0:32, :], wt(9)[0:32, :], 0)
        yield 0.95
        room(act, 0)
    stage("positions", 8.0, act=r_load)
    stage("angles", 3.0, dve=r_start)
    stage("angles", 40.0, dve=r_dve)
    stage("sines", 6.0, act=r_sin)
    stage("signed sine", 3.0, dve=r_sign)
    stage("rotary tables stored", 8.0, act=r_store)

    section()
    on("dense")

    def part_acc(dve):
        ch = chains["dve"]
        for k in range(KD):
            ch.link(nc.vector.tensor_copy(h_hi[:, k, :], acc[:, k, :]))
            nc.vector.tensor_tensor(h_lo[:, k, :], acc[:, k, :], h_hi[:, k, :].bitcast(F32),
                                    ALU.subtract).then_inc(merged_parted.sem, 1)
    merged_parted = sig.take("merged_parted", KD)
    stage("merged, in parts", 4.0, dve=part_acc)
    project("first block out", run(4, *both(weights("w_out"), 0)), acc_at,
            ready=lambda pe, k, b: pe.wait_ge(merged_parted.sem, merged_parted.nth(k)))
    on("aux")

    def x_back(act):
        load(act, wrk[:, 0:8, :], x_fm.rearrange("k p t -> p k t"))
        yield 0.9
        loads_done(act)
    stage("x back", 20.0, act=x_back)
    section()
    on("dense")

    def post(ch, k, b, root):
        y = acc_at(k, b)
        ch.link(nc.vector.scalar_tensor_tensor(y, y, col("g_post", k), root, ALU.mult, ALU.mult))
        ch.link(nc.vector.tensor_tensor(y, y, wt(k, b), ALU.add))
    norm("post norm", acc_at, HALF, post, sq=8, rs=9)


    section()
    on("dense")
    h_parted = norm_acc("even norm", "even_norm_g_2")
    on("aux")

    def spill(act):
        act.dma_start(x_fm.rearrange("k p t -> p k t"), acc[:]).then_inc(x_stored, 16)
        load(act, wt(9)[0:32, :], away[at_rope, 0:32, :])
        load(act, wt(10)[0:32, :], away[at_rope + 1, 0:32, :])
        yield 0.95
        act.wait_ge(x_stored, 32)
        loads_done(act)
    stage("x stored, rotary tables back", 30.0, act=spill)
    w2 = weights("even_w_in_2")
    w2o = A["even_w_out_2"][0].rearrange("(b k p) n -> b p k n", b=3, p=P)

    def head_tile(h, j):
        return acc[:, j, :] if h % 2 == 0 else wt(j)

    def by_residue(ap):
        return ap.rearrange("p (i r) -> p r i", r=16)

    def project_head(h, pace=1.0, ready=None):
        r_v = run_one(tiles_of(w2, C2_V + h * P))
        r_qk = run(3, tiles_of(w2, h * P, 2 * W), tiles_of(w2, W + h * P, 2 * W))
        project("head v", r_v, lambda j, b: head_tile(h, 6)[:, b * HALF:(b + 1) * HALF],
                ready=ready)

        def f_pe(pe):
            return dense_run(pe, r_qk, rhs_h, rhs_h)

        def f_act(act):
            for j in range(6):
                g, tile = j // 2, head_tile(h, j // 2 + 3 * (j % 2))
                for b in range(2):
                    yield when(r_qk, j, b)
                    out_ready(act, r_qk.t0 + j, b)
                    dst, src = tile[:, b * HALF:(b + 1) * HALF], ps[:, b, :]
                    if g == 2:
                        dst = tile.rearrange("p (r i) -> p i r", r=16)[:, 32 * b:32 * b + 32, :]
                        src = src.rearrange("p (i r) -> p i r", r=16)
                    nc.scalar.activation(dst, src, ACT.Copy).then_inc(dense_free[b], 1)
        stage("head q k", pace * dense_us(r_qk), ("pe",), pe=f_pe, act=f_act)
        return r_qk

    SWAP = [(m + 16) % 32 for m in range(32)]

    def rope(h, r_qk, start, pace=1.0):
        tmp = y_spare[0:32, h, :]
        us = start + pace * dense_us(r_qk) + 12.0

        def f_dve(dve):
            ch = chains["dve"]
            for j in range(6):
                yield (start + pace * 10.4 * (j + 1) + 2.0) / us
                for b in range(2):
                    out_taken(dve, r_qk.t0 + j, b)
                x = head_tile(h, j // 2 + 3 * (j % 2))[0:32, :]
                cos, sin, x_v, tmp_v = wt(9)[0:32, :], wt(10)[0:32, :], x, tmp
                if j // 2 == 2:
                    cos, sin = by_residue(cos), by_residue(sin)
                    x_v, tmp_v = (ap.rearrange("p (r i) -> p r i", r=16) for ap in (x, tmp))
                ch.link(nc.vector.stream_shuffle(tmp, x, SWAP))
                ch.link(nc.vector.tensor_tensor(x_v, x_v, cos, ALU.mult))
                ch.link(nc.vector.tensor_tensor(tmp_v, tmp_v, sin, ALU.mult))
                ch.link(nc.vector.tensor_tensor(x, x, tmp, ALU.add))
        stage("rope", us, dve=f_dve)

    st_m = small[:, 0:24].rearrange("p (g u) -> p g u", g=3)
    st_d = small[:, 24:48].rearrange("p (g u) -> p g u", g=3)

    def token_view(ap, g):
        if g == 0:
            return ap.rearrange("p (u i) -> p u i", i=P)
        if g == 1:
            return ap.rearrange("p (n i r) -> p r n i", n=2, r=4)
        return by_residue(ap)

    def queries(tile, g, u):
        if g == 0 or g == 2:
            return tile[:, u * P:(u + 1) * P]
        return token_view(tile, 1)[:, u // 2, u % 2, :]

    v_tok = acc[:, 7, :]

    def dilated_group(h, g):
        q_t, k_t, v_t = head_tile(h, g), head_tile(h, 3 + g), head_tile(h, 6)
        if g == 2:
            def v_by_residue(dve):
                nc.vector.tensor_copy(wt(7).rearrange("p (r i) -> p r i", r=16), by_residue(v_t))
            stage("v by residue", 2.0, dve=v_by_residue)

        def vt_pe(pe):
            for u in range(8):
                nc.tensor.transpose(ps[:, 2 + u // 4, (u % 4) * P:(u % 4 + 1) * P],
                                    queries(wt(7) if g == 2 else v_t, g, u), ident)

        def vt_act(act):
            nc.scalar.activation(v_tok, ps[:, 2:4, :].rearrange("p a w -> p (a w)"), ACT.Copy)
        stage("v turned", 2.5, pe=vt_pe)
        stage("v copied", 2.0, act=vt_act)
        steps = []
        for s in range(2):
            units = []
            for u in range(4 * s, 4 * s + 4):
                q, k = queries(q_t, g, u), queries(k_t, g, u)
                if g == 2:
                    units.append(Unit([(slice(P, 256), q, k)], C("pair"), None))
                    continue
                first = u == 0 if g == 0 else u % 2 == 0
                before = k if first else queries(k_t, g, u - 1)
                units.append(Unit([(slice(0, P), q, before), (slice(P, 256), q, k)],
                                  C("bandfirst") if first else C("band"), None))
            steps.append(units)
        width = P if g == 2 else 256

        def pv(pe, s, dst, PB):
            for u4 in range(4):
                u = 4 * s + u4
                first = u == 0 if g == 0 else u % 2 == 0
                blocks = [u] if g == 2 else [u if first else u - 1, u]
                for kb, blk in enumerate(blocks):
                    mm = nc.tensor.matmul(dst[:, u4 * P:(u4 + 1) * P], v_tok[:, blk * P:(blk + 1) * P],
                                          PB[:, kb, u4, :], start=(kb == 0), stop=(kb == len(blocks) - 1))
            return mm

        def take(s, src):
            if g == 0:
                return nc.vector.tensor_copy(q_t[:, s * HALF:(s + 1) * HALF], src)
            if g == 1:
                return nc.vector.tensor_copy(token_view(q_t, 1)[:, 2 * s:2 * s + 2],
                                             src.rearrange("p (r n i) -> p r n i", r=2, n=2))
            return nc.vector.tensor_copy(by_residue(q_t)[:, 8 * s:8 * s + 8, :],
                                         src.rearrange("p (r i) -> p r i", r=8))
        attention(f"dilated {g}", steps, width, P ** -0.5, True, False, 7, 8, pv, take,
                  stats=lambda s: (st_m[:, g, 4 * s:4 * s + 4], st_d[:, g, 4 * s:4 * s + 4]), us=ATT_TIME)

    def dilated_join(h, r_z):
        out_t = [head_tile(h, g) for g in range(3)]
        wgt = [head_tile(h, 3 + g) for g in range(3)]
        tmp = head_tile(h, 6)

        def spread(pe, which):
            for g in range(3):
                yield g / 3
                for u in range(8):
                    nc.tensor.matmul(ps[:, 2 + 2 * g + u // 4, (u % 4) * P:(u % 4 + 1) * P],
                                     which[:, g, u:u + 1].to_broadcast([P, P]), ident, start=True, stop=True)

        def grouped(g):
            flat = ps[:, 2 + 2 * g:4 + 2 * g, :].rearrange("p a w -> p (a w)")
            if g == 0:
                return flat
            if g == 1:
                return flat.rearrange("p (r n i) -> p r n i", r=4, n=2)
            return flat.rearrange("p (r i) -> p r i", r=16)

        def tok(tile, g):
            return tile if g == 0 else token_view(tile, g)

        def parts(g):
            if g == 1:
                return [(lambda ap, n=n: ap[:, :, n, :]) for n in range(2)]
            return [lambda ap: ap]

        def m_act(act):
            for g in range(3):
                for cut in parts(g):
                    nc.scalar.activation(cut(tok(wgt[g], g)), cut(grouped(g)), ACT.Copy)

        def m_dve(dve):
            ch = chains["dve"]
            ch.link(nc.vector.tensor_tensor(tmp, wgt[0], wgt[1], ALU.max))
            ch.link(nc.vector.tensor_tensor(tmp, tmp, wgt[2], ALU.max))
            for g in range(3):
                nc.vector.tensor_tensor(wgt[g], wgt[g], tmp, ALU.subtract)

        def w_act(act):
            for g in range(3):
                nc.scalar.activation(wgt[g], wgt[g], ACT.Exp)

        def d_dve(dve):
            ch = chains["dve"]
            for g in range(3):
                yield g * 0.12
                t = tmp if g == 0 else wt(8)
                for cut in parts(g):
                    ins = nc.vector.tensor_tensor(cut(tok(t, g)), cut(grouped(g)), cut(tok(wgt[g], g)), ALU.mult)
                    ch.link(ins)
                if g:
                    ch.link(nc.vector.tensor_tensor(tmp, tmp, wt(8), ALU.add))
            for b in range(2):
                yield 0.4 + b * 0.12
                ch.link(nc.vector.reciprocal(tmp[:, b * HALF:(b + 1) * HALF], tmp[:, b * HALF:(b + 1) * HALF]))
            yield 0.65
            silu_z = y_spare[:, h, :]
            for b in range(2):
                out_taken(dve, r_z.t0, b)
            for g in range(3):
                ins = nc.vector.tensor_tensor(out_t[g], out_t[g], wgt[g], ALU.mult)
            ch.link(ins)
            ch.link(nc.vector.tensor_tensor(tmp, tmp, silu_z, ALU.mult))
            yield 0.8
            ch.link(nc.vector.tensor_tensor(out_t[0], out_t[0], out_t[1], ALU.add))
            ch.link(nc.vector.tensor_tensor(out_t[0], out_t[0], out_t[2], ALU.add))
            ch.link(nc.vector.tensor_tensor(out_t[0], out_t[0], tmp, ALU.mult))
            yield 0.9
            ch.link(nc.vector.tensor_copy(y_hi[:, h, :], out_t[0]))
            nc.vector.tensor_tensor(y_lo[:, h, :], out_t[0], y_hi[:, h, :].bitcast(F32), ALU.subtract)
        stage("maxima spread", 6.0, pe=lambda pe: spread(pe, st_m))
        stage("maxima copied", 4.5, act=m_act)
        stage("joint maximum", 6.0, dve=m_dve)
        stage("group weights", 6.0, act=w_act, pe=lambda pe: spread(pe, st_d))
        stage("join", 28.0, dve=d_dve)

    on("dense")
    r_qk = project_head(0, ready=part_ready(h_parted))
    on("side")
    rope(0, r_qk, 50.4)
    for h in range(4):
        section()
        on("dense")
        r_z = run_one(tiles_of(w2, C2_Z + h * P))

        def z_act(act, r_z=r_z, h=h):
            for b in range(2):
                yield when(r_z, 0, b)
                out_ready(act, r_z.t0, b)
                nc.scalar.activation(y_spare[:, h, b * HALF:(b + 1) * HALF], ps[:, b, :],
                                     ACT.Silu).then_inc(dense_free[b], 1)
        stage("head z", dense_us(r_z), ("pe",), pe=lambda pe, r_z=r_z: dense_run(pe, r_z, rhs_h, rhs_h), act=z_act)
        if h < 3:
            r_qk = project_head(h + 1, HEAD_PACE)
            on("side")
            rope(h + 1, r_qk, 20.8, HEAD_PACE)
        else:
            project("pool x", run(2, *both(w2, C2_X)), acc_at)
        on("aux")
        for g in range(3):
            dilated_group(h, g)
        dilated_join(h, r_z)

    section()
    on("dense")
    project("even q", run(2, *both(w2, C2_Q)), to_tiles(4))
    on("aux")

    def p_load(act):
        load(act, wt(9)[:, 0:HALF].rearrange("p (g d) -> p g d", g=4),
             A["even_w_pool_2"][0].rearrange("g c d -> c g d"))
        yield 0.9
        loads_done(act)
        load(act, acc[:, 4:8, :], x_fm.rearrange("k p t -> p k t")[:, 4:8, :])

    def p_dve(dve):
        ch = chains["dve"]
        for i in range(4):
            yield i / 4
            x, src, s = acc[:, i, :], acc[:, i, :], 1
            for lv in range(i + 1):
                dst = wt((8, 10)[lv % 2])
                nc.vector.tensor_copy(dst[:, 0:s], src[:, 0:s])
                ch.link(nc.vector.tensor_tensor(dst[:, s:T], src[:, s:T], src[:, 0:T - s], ALU.add))
                src, s = dst, 2 * s
            ch.link(nc.vector.tensor_tensor(small[:, 64:80], src[:, 0:16], C("icount")[:, 16 * i:16 * i + 16], ALU.mult))
            ch.link(nc.vector.scalar_tensor_tensor(wt(i), src, 1.0 / s, x, ALU.mult, ALU.subtract))
            ch.link(nc.vector.tensor_tensor(wt(i)[:, 0:16], small[:, 64:80], x[:, 0:16], ALU.subtract))
    stage("pool weights", 5.0, act=p_load)
    stage("pool sums", 26.0, dve=p_dve)

    def x_restore(act):
        load(act, acc[:, 0:4, :], x_fm.rearrange("k p t -> p k t")[:, 0:4, :])
        yield 0.95
        loads_done(act)
    stage("x back", 10.0, act=x_restore)

    section()
    on("dense")
    add_out("even out A", run(4, *both(w2o[0], 0), 4, 4))
    on("aux")
    pooled = sig.take("pool_out", 8)
    ptaken = sig.take("pool_taken", 8)

    def p_pe(pe):
        for i in range(8):
            yield i / 10
            if i >= 4:
                pe.wait_ge(ptaken.sem, ptaken.nth(i - 4))
            nc.tensor.matmul(ps[:, 2 + i % 4, :], wt(9)[:, (i // 2) * P:(i // 2 + 1) * P], wt(i // 2, i % 2),
                             start=True, stop=True).then_inc(pooled.sem, 1)

    def p_act(act):
        for i in range(8):
            yield (i + 0.9) / 10
            act.wait_ge(pooled.sem, pooled.nth(i))
            nc.scalar.activation(wt(i // 2, i % 2), ps[:, 2 + i % 4, :], ACT.Copy,
                                 scale=col("even_pool_scale_2", i // 2)).then_inc(ptaken.sem, 1)
    stage("pool mix", 20.0, pe=p_pe, act=p_act)
    on("dense")
    gate_z("pool z", run(2, *both(w2, C2_Z + W)), wt, None, 10,
           o_ready=lambda j, b: (ptaken.sem, ptaken.nth(2 * j + b)))

    section()
    on("dense")
    add_out("even out B", run(4, *both(w2o[1], 0), 4, 4))
    on("aux")
    fetch("even k v", [(8, at_kv[1]), (9, at_kv[1] + 1)], 6.0)
    memory_attention("even", 4, 8, 9, 0, 1, us=75.0)
    section()
    on("dense")
    gate_z("even memory z", run(2, *both(w2, C2_Z + 2 * W)), lambda j, b: wt(4 + j, b), None, 10)
    add_out("even out M", run(4, *both(w2o[2], 0), 4, 4))

    section()
    on("dense")
    h_parted = norm_acc("odd norm", "odd_norm_g_2")
    w3 = weights("odd_w_in_2")
    w3o = A["odd_w_out_2"][0].rearrange("(b k p) n -> b p k n", b=3, p=P)
    project("odd v", run(4, *both(w3, C3_V)), to_tiles(0), ready=part_ready(h_parted))
    section()
    on("dense")
    at_oq = project_away("odd q", run(2, *both(w3, C3_Q)), None)
    stage("stored", 3.0, act=stored_away)
    on("aux")
    layer_norm("odd ln", lambda k, b: wt(k, b), KD, D, lambda k: col("odd_ln_g_2", k), (8, 9),
               lambda k, b: nc.scalar.activation(wt(k, b), wt(k, b), ACT.Identity, bias=col("odd_ln_b_2", k)))

    section()
    on("aux")
    w_s, b_s, w_masked = wt(8), wt(10), wt(9)

    def s_load(act):
        load(act, w_s.rearrange("p (g s) -> p g s", g=8), A["odd_w_s_2"][0].rearrange("g t s -> t g s"))
        load(act, b_s.rearrange("p (g s) -> p g s", g=8), A["odd_b_s_2"][0].partition_broadcast(P))
        yield 0.9
        loads_done(act)

    def s_pe(pe):
        for g in range(8):
            nc.tensor.transpose(ps[:, 2 + g // 4, (g % 4) * P:(g % 4 + 1) * P], w_s[:, g * P:(g + 1) * P], ident)

    def s_dve(dve):
        nc.vector.tensor_tensor(w_masked.rearrange("p (g t) -> p g t", g=8),
                                ps[:, 2:4, :].rearrange("p a (g t) -> p (a g) t", g=4),
                                C("upto").unsqueeze(1).to_broadcast([P, 8, P]), ALU.mult)
    stage("mix load", 6.0, act=s_load)
    stage("mix turned", 2.5, pe=s_pe)
    stage("mix masked", 2.0, dve=s_dve)

    vturned = sig.take("sg_turned", 8)
    vcopied = sig.take("sg_copied", 8)
    smixed = sig.take("sg_mixed", 8)
    sadded = sig.take("sg_added", 8)

    def g_pe(pe):
        for g in range(8):
            yield g / 8
            if g >= 1:
                pe.wait_ge(vcopied.sem, vcopied.nth(g - 1))
            for n in range(8):
                mm = nc.tensor.transpose(ps[:, 2 + n // 4, (n % 4) * P:(n % 4 + 1) * P], wt(g)[:, n * P:(n + 1) * P], ident)
            mm.then_inc(vturned.sem, 1)
            yield (g + 0.6) / 8
            pe.wait_ge(vcopied.sem, vcopied.nth(g))
            if g >= 1:
                pe.wait_ge(sadded.sem, sadded.nth(g - 1))
            for n in range(8):
                mm = nc.tensor.matmul(ps[:, 4 + n // 4, (n % 4) * P:(n % 4 + 1) * P], wt(8)[:, n * P:(n + 1) * P],
                                      w_masked[:, g * P:(g + 1) * P], start=True, stop=True)
            mm.then_inc(smixed.sem, 1)

    def g_act(act):
        for g in range(8):
            yield (g + 0.3) / 8
            act.wait_ge(vturned.sem, vturned.nth(g))
            if g >= 1:
                act.wait_ge(smixed.sem, smixed.nth(g - 1))
            nc.scalar.activation(wt(8), ps[:, 2:4, :].rearrange("p a w -> p (a w)"), ACT.Copy).then_inc(vcopied.sem, 1)

    def g_dve(dve):
        for g in range(8):
            yield (g + 0.9) / 8
            dve.wait_ge(smixed.sem, smixed.nth(g))
            nc.vector.tensor_tensor(wt(g).rearrange("p (n t) -> p n t", n=8),
                                    ps[:, 4:6, :].rearrange("p a (n t) -> p (a n) t", n=4),
                                    b_s[:, g * P:(g + 1) * P].unsqueeze(1).to_broadcast([P, 8, P]),
                                    ALU.add).then_inc(sadded.sem, 1)
    stage("mix", 72.0, pe=g_pe, act=g_act, dve=g_dve)
    on("dense")
    stage("first group mixed", 18.0)
    r_u = run(4, *both(w3, C3_U))

    def u_pe(pe):
        return dense_run(pe, r_u, rhs_h, rhs_h)

    def u_dve(dve):
        for j in range(8):
            for b in range(2):
                yield when(r_u, j, b)
                out_ready(dve, r_u.t0 + j, b)
                dve.wait_ge(sadded.sem, sadded.nth(j))
                nc.vector.tensor_tensor(wt(j, b), wt(j, b), ps[:, b, :], ALU.mult).then_inc(dense_free[b], 1)
    stage("odd u", dense_us(r_u), pe=u_pe, dve=u_dve)

    section()
    on("dense")
    gate_z("odd z", run(2, *both(w3, C3_Z)), wt, None, 10)
    add_out("odd out", run(4, *both(w3o[0], 0), 4, 4))
    section()
    on("dense")
    gate_z("odd z", run(2, *both(w3, C3_Z + W)), lambda j, b: wt(4 + j, b), None, 10)
    odd_gated = sig.take("odd_gated", 1)

    def odd_gated_dve(dve):
        nc.vector.engine_nop().then_inc(odd_gated.sem, 1)
    stage("odd gated", 0.1, dve=odd_gated_dve)
    add_out("odd out", run(4, *both(w3o[1], 0), 4, 4))
    on("aux")
    fetch("odd q k v", [(j, at_oq + j) for j in range(4)] + [(8, at_kv[2]), (9, at_kv[2] + 1)], 44.0)

    def odd_wait(dve):
        dve.wait_ge(odd_gated.sem, odd_gated.nth(0))
    stage("odd scores' tiles", 0.5, dve=odd_wait)
    memory_attention("odd", 0, 8, 9, 4, 5, us=75.0)
    section()
    on("dense")
    gate_z("odd memory z", run(2, *both(w3, C3_Z + 2 * W)), wt, None, 10)
    add_out("odd out M", run(4, *both(w3o[2], 0), 4, 4))
    section()
    def last(ch, k, b, root):
        y = acc_at(k, b)
        ch.link(nc.vector.scalar_tensor_tensor(y, y, col("final_norm_g_2", k), root, ALU.mult, ALU.mult))
    norm("final norm", acc_at, HALF, last, sq=8, rs=9)
    oturned = sig.take("out_turned", KD)
    ocopied = sig.take("out_copied", KD)

    def o_pe(pe):
        for n in range(8):
            if n >= 2:
                pe.wait_ge(ocopied.sem, ocopied.nth(n - 2))
            for k in range(KD):
                mm = nc.tensor.transpose(ps[:, 2 + 2 * (n % 2) + k // 4, (k % 4) * P:(k % 4 + 1) * P],
                                         acc[:, k, n * P:(n + 1) * P], ident)
            mm.then_inc(oturned.sem, 1)

    def o_dve(dve):
        for n in range(8):
            dve.wait_ge(oturned.sem, oturned.nth(n))
            b = 2 + 2 * (n % 2)
            nc.vector.tensor_copy(wt(n), ps[:, b:b + 2, :].rearrange("p a w -> p (a w)")).then_inc(ocopied.sem, 1)

    def o_store(act):
        for n in range(8):
            act.wait_ge(ocopied.sem, ocopied.nth(n))
            load(act, out[0].rearrange("(n p) d -> n p d", p=P)[n], wt(n))
        loads_done(act)
    stage("out turned", pe=o_pe, dve=o_dve, act=o_store)


    stage_done = {(t, e): sig.sem(f"{t}_{e}_stage_done") for t in ("dense", "aux", "side") for e in engines}
    done_before = {k: 0 for k in stage_done}
    plans = []
    for sec in sections:
        plan = {}
        for t, row in sec.items():
            start, plan[t] = 0.0, []
            for name, us, fns, ahead in row:
                waits = {e: done_before[t, e] for e in engines}
                plan[t].append((start, us, fns, ahead, waits))
                for e in fns:
                    done_before[t, e] += 1
                start += us
        plans.append(plan)

    def thread_part(name, eng, t, row):
        for start, us, fns, ahead, waits in row:
            if name not in fns:
                continue
            yield start
            for other in engines:
                if other != name and waits[other] and name not in ahead:
                    eng.wait_ge(stage_done[t, other], waits[other])
            parts = fns[name](eng)
            if parts is not None:
                for fraction in parts:
                    yield start + fraction * us
            eng.drain().then_inc(stage_done[t, name], 1)

    def play(name, eng):
        chains[name] = Chain(eng, f"{name}_chain")
        for n, plan in enumerate(plans):
            threads = [thread_part(name, eng, t, row) for t, row in plan.items()]
            due = [next(th, None) for th in threads]
            while any(d is not None for d in due):
                i = min((d, i) for i, d in enumerate(due) if d is not None)[1]
                due[i] = next(threads[i], None)
            eng.drain().then_inc(at_end[name], 1)
            for other in engines:
                if other != name:
                    eng.wait_ge(at_end[other], n + 1)

    block = ctx.enter_context(nc.Block())

    @block.sync
    def _(sp):
        def load_tile(slot_, nk, src):
            if not isinstance(src, tuple):
                sp.dma_start(w_raw[:, slot_, 0:nk, :], src).then_inc(raw_loaded[slot_], 32)
                return
            kind, pieces = src
            for u, piece in enumerate(pieces):
                dst = w_raw[:, slot_, 0:nk, 64 * u:64 * u + 64] if kind == "columns" else \
                    w_raw[64 * u:64 * u + 64, slot_, 0:nk, :]
                sp.dma_start(dst, piece).then_inc(raw_loaded[slot_], 16)

        for r in runs:
            def body(i, r=r):
                for p in range(min(2, r.n)):
                    t, src = r.t(i, p), r.src[p](i)
                    if not isinstance(t, int) or t >= 2:
                        sp.wait_ge(tiles_split, t - 1)
                    load_tile(r.t(0, p) % 2, r.nk[p], src)
            if r.n <= 2:
                body(0)
            elif r.t0 < 2:
                body(0)
                with sp.Fori(2, r.pairs + 1, 1) as i:
                    body(i - 1)
            else:
                with sp.Fori(1, r.pairs + 1, 1) as i:
                    body(i - 1)

    @block.gpsimd
    def _(pool):
        def split(t, s, raw_count):
            pool.wait_ge(raw_loaded[s], raw_count)
            nc.gpsimd.tensor_tensor(w_hi[:, s], w_raw[:, s], one, ALU.mult).then_inc(hi_ready, 1)
            pool.wait_ge(hi_ready, t + 2)
            nc.gpsimd.tensor_tensor(w_lo[:, s], w_raw[:, s], w_hi[:, s].bitcast(F32),
                                    ALU.subtract).then_inc(tiles_split, 1)
        hi_ready = sig.sem("hi_ready")
        nc.gpsimd.memset(pool_one[:], 1.0).then_inc(hi_ready, 1)
        pool.wait_ge(hi_ready, 1)
        one = pool_one[:].unsqueeze(2).to_broadcast([P, KD, P])
        for s in range(2):
            split(s, s, 32)
        with pool.Fori(1, ntiles // 2, 1) as i:
            for s in range(2):
                pool.wait_ge(dense_out, 2 * (2 * i + s) - 2)
                split(2 * i + s, s, 32 * i + 32)
        if ntiles % 2:
            pool.wait_ge(dense_out, 2 * (ntiles - 1) - 2)
            split(ntiles - 1, 0, 32 * (ntiles // 2) + 32)

    @block.scalar
    def _(act):
        play("act", act)

    @block.vector
    def _(dve):
        for b in range(2):
            nc.vector.engine_nop().then_inc(dense_free[b], 1)
        play("dve", dve)

    @block.tensor
    def _(pe):
        play("pe", pe)


_OUT = (1, T, D)


def kernel(**inputs):
    import concourse.bacc as _bacc
    from concourse.bass_utils import run_bass_kernel_spmd as _run

    nc = _bacc.Bacc("TRN2", target_bir_lowering=False, num_devices=1)
    arrays = {k: np.ascontiguousarray(v) for k, v in inputs.items()}
    arrays["consts"] = np.ascontiguousarray(constants()[0])
    arrays["bias_consts"] = bias_parts()
    A = {k: nc.dram_tensor(f"in_{k}", v.shape, mybir.dt.from_np(v.dtype), kind="ExternalInput").ap()
         for k, v in arrays.items()}
    out = nc.dram_tensor("out", _OUT, F32, kind="ExternalOutput").ap()
    hybrid_program(nc, A, out)
    r = _run(nc, [{f"in_{k}": v for k, v in arrays.items()}], core_ids=[0])
    return r.results[0]["out"]
```
